# Optimizing a Trainium2 kernel written in Bass

```python
import jax, jax.numpy as jnp
from jax import lax
import numpy as np

D_MODEL = 1024
BATCH = 1
SEQ = 256
DEPTH = 2

NORM_EPS = 1e-6
CONV_WIDTH = 4
DN_HEADS = 4
DN_HEAD_DIM = 128
DN_WIDTH = DN_HEADS * DN_HEAD_DIM
DN_CHUNK = 64
MB_HEADS = 4
MB_HEAD_DIM = 128
MB_WIDTH = MB_HEADS * MB_HEAD_DIM
MB_BLOCK = 256
MB_TOP_K = 3
MB_QUERY_BLOCK = 16
MB_SCALE = MB_HEAD_DIM ** -0.5
ROPE_THETA = 500000.0
ROPE_DIMS = MB_HEAD_DIM // 4
LRU_WIDTH = 512
LRU_GROUPS = 8
LRU_GROUP_DIM = LRU_WIDTH // LRU_GROUPS
LRU_C = 8.0
N_BRANCH = 3
FFN_HIDDEN = -(-8 * D_MODEL // (3 * 256)) * 256
IN_SPLIT_WIDTHS = (DN_WIDTH, DN_WIDTH, DN_WIDTH, DN_WIDTH, DN_HEADS, DN_HEADS,
                   MB_WIDTH, MB_WIDTH, MB_WIDTH, LRU_WIDTH, LRU_WIDTH, N_BRANCH * D_MODEL)
IN_COLS = sum(IN_SPLIT_WIDTHS)

kernel_name = 'hybrid_deltanet_moba_rglru_block'

def rms_norm(x, w):
    xf = x.astype(jnp.float32)
    y = xf * lax.rsqrt(jnp.mean(xf * xf, axis=-1, keepdims=True) + NORM_EPS)
    return (y * w.astype(jnp.float32)).astype(x.dtype)

def l2_normalize(x):
    return x * lax.rsqrt(jnp.sum(x * x, axis=-1, keepdims=True) + NORM_EPS)

def split_columns(p):
    out = []
    start = 0
    for w in IN_SPLIT_WIDTHS:
        out.append(p[..., start:start + w])
        start += w
    return out

def causal_depthwise_conv(x, w):
    width, ch = w.shape
    return lax.conv_general_dilated(
        x, w[:, None, :].astype(x.dtype), window_strides=(1,), padding=[(width - 1, 0)],
        dimension_numbers=('NWC', 'WIO', 'NWC'), feature_group_count=ch)

def partial_rope(x):
    t = x.shape[1]
    half = ROPE_DIMS // 2
    inv_freq = ROPE_THETA ** (-jnp.arange(half, dtype=jnp.float32) / half)
    ang = jnp.arange(t, dtype=jnp.float32)[:, None] * inv_freq[None, :]
    cos = jnp.cos(ang)[None, :, None, :]
    sin = jnp.sin(ang)[None, :, None, :]
    xr = x[..., :ROPE_DIMS].astype(jnp.float32)
    x1, x2 = xr[..., :half], xr[..., half:]
    rot = jnp.concatenate([x1 * cos - x2 * sin, x2 * cos + x1 * sin], axis=-1).astype(x.dtype)
    return jnp.concatenate([rot, x[..., ROPE_DIMS:]], axis=-1)

def chunk_gated_delta_rule(q, k, v, g, beta):
    b, h, t, dk = q.shape
    dv = v.shape[-1]
    c = DN_CHUNK
    n = t // c
    q = q.reshape(b, h, n, c, dk)
    k = k.reshape(b, h, n, c, dk)
    v = v.reshape(b, h, n, c, dv)
    g = jnp.cumsum(g.reshape(b, h, n, c), axis=-1)
    beta = beta.reshape(b, h, n, c)
    k_beta = k * beta[..., None]
    v_beta = v * beta[..., None]
    incl = jnp.tril(jnp.ones((c, c), dtype=bool))
    strict = jnp.tril(jnp.ones((c, c), dtype=bool), k=-1)
    decay = jnp.exp(jnp.where(incl, g[..., :, None] - g[..., None, :], -jnp.inf))
    lower = jnp.where(strict, jnp.einsum('bhnid,bhnjd->bhnij', k_beta, k) * decay, 0.0)
    eye = jnp.eye(c, dtype=jnp.float32)
    t_inv = lax.linalg.triangular_solve(lower + eye, jnp.broadcast_to(eye, lower.shape),
                                        left_side=True, lower=True, unit_diagonal=True)
    u = jnp.einsum('bhnij,bhnjd->bhnid', t_inv, v_beta)
    w = jnp.einsum('bhnij,bhnjd->bhnid', t_inv, k_beta * jnp.exp(g)[..., None])
    attn = jnp.einsum('bhnid,bhnjd->bhnij', q, k) * decay
    g_last = g[..., -1]
    k_to_end = k * jnp.exp(g_last[..., None] - g)[..., None]
    q_dec = q * jnp.exp(g)[..., None]

    def step(state, xs):
        q_c, k_c, u_c, w_c, a_c, gl = xs
        v_new = u_c - jnp.einsum('bhcd,bhde->bhce', w_c, state)
        o = jnp.einsum('bhcd,bhde->bhce', q_c, state) + jnp.einsum('bhij,bhje->bhie', a_c, v_new)
        state = state * jnp.exp(gl)[..., None, None] + jnp.einsum('bhcd,bhce->bhde', k_c, v_new)
        return state, o

    xs = tuple(jnp.moveaxis(z, 2, 0) for z in (q_dec, k_to_end, u, w, attn, g_last))
    s0 = jnp.zeros((b, h, dk, dv), jnp.float32)
    _, o = lax.scan(step, s0, xs)
    return jnp.moveaxis(o, 0, 2).reshape(b, h, t, dv)

def gated_deltanet(q, k, v, z, a, bb, conv_w, a_log, dt_bias, norm_w):
    b, t, _ = q.shape
    qkv = jax.nn.silu(causal_depthwise_conv(jnp.concatenate([q, k, v], axis=-1), conv_w))
    q, k, v = jnp.split(qkv, 3, axis=-1)

    def heads(y):
        return y.reshape(b, t, DN_HEADS, DN_HEAD_DIM).transpose(0, 2, 1, 3).astype(jnp.float32)

    qh = l2_normalize(heads(q)) * (DN_HEAD_DIM ** -0.5)
    kh = l2_normalize(heads(k))
    vh = heads(v)
    g = -jnp.exp(a_log.astype(jnp.float32)) * jax.nn.softplus(a.astype(jnp.float32) + dt_bias.astype(jnp.float32))
    beta = jax.nn.sigmoid(bb.astype(jnp.float32))
    o = chunk_gated_delta_rule(qh, kh, vh, g.transpose(0, 2, 1), beta.transpose(0, 2, 1))
    o = o.transpose(0, 2, 1, 3)
    zf = z.reshape(b, t, DN_HEADS, DN_HEAD_DIM).astype(jnp.float32)
    o = rms_norm(o, norm_w) * jax.nn.silu(zf)
    return o.reshape(b, t, DN_WIDTH).astype(q.dtype)

def moba_attention(q, k, v):
    b, t, _ = q.shape
    h, dh = MB_HEADS, MB_HEAD_DIM
    q = partial_rope(q.reshape(b, t, h, dh))
    k = partial_rope(k.reshape(b, t, h, dh))
    v = v.reshape(b, t, h, dh)
    nb = -(-t // MB_BLOCK)
    tp = nb * MB_BLOCK
    n_sel = min(MB_TOP_K, nb)
    pad = ((0, 0), (0, tp - t), (0, 0), (0, 0))
    kb = jnp.pad(k, pad).reshape(b, nb, MB_BLOCK, h, dh).transpose(0, 3, 1, 2, 4)
    vb = jnp.pad(v, pad).reshape(b, nb, MB_BLOCK, h, dh).transpose(0, 3, 1, 2, 4)
    qh = q.transpose(0, 2, 1, 3)
    k_mean = jnp.mean(kb.astype(jnp.float32), axis=3)
    q_block = jnp.arange(t) // MB_BLOCK
    fully_past = jnp.arange(nb)[None, :] < q_block[:, None]
    gate = jnp.where(fully_past, jnp.einsum('bhtd,bhnd->bhtn', qh.astype(jnp.float32), k_mean), -jnp.inf)
    _, sel = lax.top_k(gate, n_sel)
    sel_valid = sel < q_block[:, None]
    bi = jnp.arange(b)[:, None, None, None]
    hi = jnp.arange(h)[None, :, None, None]

    def attend_query_block(ci):
        t0 = ci * MB_QUERY_BLOCK
        qc = lax.dynamic_slice_in_dim(qh, t0, MB_QUERY_BLOCK, axis=2)
        selc = lax.dynamic_slice_in_dim(sel, t0, MB_QUERY_BLOCK, axis=2)
        validc = lax.dynamic_slice_in_dim(sel_valid, t0, MB_QUERY_BLOCK, axis=2)
        own = t0 // MB_BLOCK
        k_own = lax.dynamic_index_in_dim(kb, own, axis=2, keepdims=False)
        v_own = lax.dynamic_index_in_dim(vb, own, axis=2, keepdims=False)
        k_sel = kb[bi, hi, selc]
        v_sel = vb[bi, hi, selc]
        q_pos = t0 + jnp.arange(MB_QUERY_BLOCK)
        k_pos = own * MB_BLOCK + jnp.arange(MB_BLOCK)
        s_own = jnp.einsum('bhqd,bhkd->bhqk', qc, k_own, preferred_element_type=jnp.float32) * MB_SCALE
        s_own = jnp.where(k_pos[None, :] <= q_pos[:, None], s_own, -jnp.inf)
        s_sel = jnp.einsum('bhqd,bhqnkd->bhqnk', qc, k_sel, preferred_element_type=jnp.float32) * MB_SCALE
        s_sel = jnp.where(validc[..., None], s_sel, -jnp.inf).reshape(b, h, MB_QUERY_BLOCK, n_sel * MB_BLOCK)
        p = jax.nn.softmax(jnp.concatenate([s_own, s_sel], axis=-1), axis=-1)
        p_own = p[..., :MB_BLOCK].astype(v.dtype)
        p_sel = p[..., MB_BLOCK:].reshape(b, h, MB_QUERY_BLOCK, n_sel, MB_BLOCK).astype(v.dtype)
        return (jnp.einsum('bhqk,bhkd->bhqd', p_own, v_own)
                + jnp.einsum('bhqnk,bhqnkd->bhqd', p_sel, v_sel))

    o = lax.map(attend_query_block, jnp.arange(t // MB_QUERY_BLOCK))
    return o.transpose(1, 0, 3, 2, 4).reshape(b, t, h * dh)

def rg_lru_branch(xb, yb, conv_w, conv_b, w_r, b_r, w_i, b_i, lam):
    b, t, _ = xb.shape
    xc = causal_depthwise_conv(xb, conv_w) + conv_b.astype(xb.dtype)
    xg = xc.reshape(b, t, LRU_GROUPS, LRU_GROUP_DIM)
    r = jax.nn.sigmoid((jnp.einsum('btgi,gij->btgj', xg, w_r).reshape(b, t, LRU_WIDTH) + b_r).astype(jnp.float32))
    i = jax.nn.sigmoid((jnp.einsum('btgi,gij->btgj', xg, w_i).reshape(b, t, LRU_WIDTH) + b_i).astype(jnp.float32))
    log_a = -LRU_C * r * jax.nn.softplus(-lam.astype(jnp.float32))
    a = jnp.exp(log_a)
    u = jnp.sqrt(-jnp.expm1(2.0 * log_a)) * (i * xc.astype(jnp.float32))

    def combine(c1, c2):
        a1, b1 = c1
        a2, b2 = c2
        return a1 * a2, a2 * b1 + b2

    _, hs = lax.associative_scan(combine, (a, u), axis=1)
    return (hs * jax.nn.gelu(yb.astype(jnp.float32))).astype(xb.dtype)

def setup_inputs(seed: int = 0) -> dict:
    key = jax.random.key(seed)
    ks = iter(jax.random.split(key, 40))
    f32 = jnp.float32
    L = DEPTH

    def nrm(shape, fan_in):
        return jax.random.normal(next(ks), shape, f32) * (fan_in ** -0.5)

    def small(shape):
        return 0.02 * jax.random.normal(next(ks), shape, f32)

    x = jax.random.normal(next(ks), (BATCH, SEQ, D_MODEL), f32)
    norm_mix = 1.0 + small((L, D_MODEL))
    w_in = nrm((L, D_MODEL, IN_COLS), D_MODEL)
    b_gate = small((L, N_BRANCH * D_MODEL))
    dn_conv = nrm((L, CONV_WIDTH, 3 * DN_WIDTH), CONV_WIDTH)
    dn_a_log = jnp.log(jax.random.uniform(next(ks), (L, DN_HEADS), f32, 1.0, 16.0))
    dt = jnp.exp(jax.random.uniform(next(ks), (L, DN_HEADS), f32, np.log(1e-3), np.log(1e-1)))
    dn_dt_bias = dt + jnp.log(-jnp.expm1(-dt))
    dn_norm = 1.0 + small((L, DN_HEAD_DIM))
    dn_out = nrm((L, DN_WIDTH, D_MODEL), DN_WIDTH)
    mb_out = nrm((L, MB_WIDTH, D_MODEL), MB_WIDTH)
    lru_conv_w = nrm((L, CONV_WIDTH, LRU_WIDTH), CONV_WIDTH)
    lru_conv_b = small((L, LRU_WIDTH))
    lru_w_r = nrm((L, LRU_GROUPS, LRU_GROUP_DIM, LRU_GROUP_DIM), LRU_GROUP_DIM)
    lru_b_r = small((L, LRU_WIDTH))
    lru_w_i = nrm((L, LRU_GROUPS, LRU_GROUP_DIM, LRU_GROUP_DIM), LRU_GROUP_DIM)
    lru_b_i = small((L, LRU_WIDTH))
    a0 = jax.random.uniform(next(ks), (L, LRU_WIDTH), f32, 0.9, 0.999)
    p = a0 ** (1.0 / LRU_C)
    lru_lambda = jnp.log(p) - jnp.log1p(-p)
    lru_out = nrm((L, LRU_WIDTH, D_MODEL), LRU_WIDTH)
    w_o = nrm((L, D_MODEL, D_MODEL), D_MODEL)
    norm_ffn = 1.0 + small((L, D_MODEL))
    ffn_in = nrm((L, D_MODEL, 2 * FFN_HIDDEN), D_MODEL)
    ffn_down = nrm((L, FFN_HIDDEN, D_MODEL), FFN_HIDDEN)
    norm_final = 1.0 + small((D_MODEL,))
    return {'x': x, 'norm_mix': norm_mix, 'w_in': w_in, 'b_gate': b_gate,
            'dn_conv': dn_conv, 'dn_a_log': dn_a_log, 'dn_dt_bias': dn_dt_bias, 'dn_norm': dn_norm,
            'dn_out': dn_out, 'mb_out': mb_out,
            'lru_conv_w': lru_conv_w, 'lru_conv_b': lru_conv_b, 'lru_w_r': lru_w_r, 'lru_b_r': lru_b_r,
            'lru_w_i': lru_w_i, 'lru_b_i': lru_b_i, 'lru_lambda': lru_lambda, 'lru_out': lru_out,
            'w_o': w_o, 'norm_ffn': norm_ffn, 'ffn_in': ffn_in, 'ffn_down': ffn_down,
            'norm_final': norm_final}

def reference(x, norm_mix, w_in, b_gate, dn_conv, dn_a_log, dn_dt_bias, dn_norm, dn_out, mb_out,
              lru_conv_w, lru_conv_b, lru_w_r, lru_b_r, lru_w_i, lru_b_i, lru_lambda, lru_out,
              w_o, norm_ffn, ffn_in, ffn_down, norm_final):
    b, t, d = x.shape
    for l in range(DEPTH):
        h = rms_norm(x, norm_mix[l])
        proj = h @ w_in[l]
        (dq, dk, dv, dz, da, db, mq, mk, mv, lx, ly, gates) = split_columns(proj)
        y_dn = gated_deltanet(dq, dk, dv, dz, da, db, dn_conv[l], dn_a_log[l], dn_dt_bias[l], dn_norm[l]) @ dn_out[l]
        y_mb = moba_attention(mq, mk, mv) @ mb_out[l]
        y_lru = rg_lru_branch(lx, ly, lru_conv_w[l], lru_conv_b[l], lru_w_r[l], lru_b_r[l],
                              lru_w_i[l], lru_b_i[l], lru_lambda[l]) @ lru_out[l]
        g = jax.nn.sigmoid((gates + b_gate[l]).astype(jnp.float32)).reshape(b, t, N_BRANCH, d)
        mixed = (g[:, :, 0] * y_dn + g[:, :, 1] * y_mb + g[:, :, 2] * y_lru).astype(x.dtype)
        x = x + mixed @ w_o[l]
        h = rms_norm(x, norm_ffn[l])
        gate, up = jnp.split(h @ ffn_in[l], 2, axis=-1)
        x = x + (jax.nn.silu(gate) * up) @ ffn_down[l]
    return rms_norm(x, norm_final)


_drawn_inputs = setup_inputs


def setup_inputs(seed=0):
    import zlib

    import numpy as np

    out = dict(_drawn_inputs(seed))
    spreads = {}
    factors = {'norm_mix': 2.849,
     'b_gate': 8.0,
     'dn_norm': 5.931,
     'lru_b_r': 26.443,
     'lru_b_i': 8.0,
     'norm_ffn': 2.839,
     'norm_final': 7.941}
    for name, (base, spread) in spreads.items():
        noise = np.random.default_rng([zlib.crc32(name.encode()), seed]).standard_normal(out[name].shape)
        drawn = base * np.exp(spread * noise) if base else spread * noise
        out[name] = __import__('jax').numpy.asarray(drawn.astype(out[name].dtype))
    for name, factor in factors.items():
        out[name] = (out[name] * factor).astype(out[name].dtype)
    return out
```

```python
from contextlib import ExitStack

import numpy as np
import concourse.bass as bass
from concourse import mybir

F32 = mybir.dt.float32
F32R = mybir.dt.float32r
I32 = mybir.dt.int32
ALU = mybir.AluOpType
ACT = mybir.ActivationFunctionType
AX = mybir.AxisListType.X

P = 128
D = 1024
T = 256
L = 2
HEADS = 4
HD = 128
CHUNK = 64
NCH = T // CHUNK
TAPS = 4
EPS = 1e-6
FFN = 2816
KT = D // P
HALF = 1024

C_IN = 30
C_Y = 6
C_WO = 4
PAIRS = FFN // 256
C_FFN = 3 * PAIRS
CH = C_IN + C_Y + C_WO + C_FFN
NH = 2 * CH
FFN0 = C_IN + C_Y + C_WO
RING = 5
AHEAD = RING - 1

TQ, TK, TV, TMQ, TMK, TMV, TLX, TLY, TZ, TG = 0, 4, 8, 12, 16, 20, 24, 28, 32, 36
NT = 60

OFF = {}


def _place(names):
    at = 0
    for name, n in names:
        OFF[name] = at
        at += n
    return at


NPAR = _place([("wab", KT * 8), ("conv", 16 * TAPS), ("convb", 4), ("br", 4), ("bi", 4), ("lam", 4),
               ("dnorm", 1), ("bg", 24), ("alog", 1), ("dtb", 1), ("wr", 512), ("wi", 512)])
CON = {}
_at = 0
for _n, _k in [("ident", 128), ("causal", 128), ("ones", 128), ("ecol", 64), ("cos", 256), ("sin", 256),
               ("reset", 256), ("qscale", 1), ("eye", 64), ("upin", 64), ("low", 64), ("low1", 64),
               ("up1", 64), ("up2", 64), ("up4", 64), ("up8", 64), ("up16", 64), ("up32", 64)]:
    CON[_n] = _at
    _at += _k
NCON = _at


class Signal:

    def __init__(self, sem, name, known):
        self.sem, self.name = sem, name
        self.base, self.per, self.marks = known.get(name, (0, 0, {}))
        self.n, self.new, self.start = 0, {}, 0
        self.layer = None

    def up(self, step=None):
        self.n += 1
        if step is not None:
            self.new[step] = self.n
        return self.sem, 1

    def open_layer(self):
        self.start, self.n = self.n, 0
        self.pre, self.new = self.new, {}

    def at(self, l, step, prev=False):
        n = self.base + self.marks.get(step, 1)
        if prev:
            return self.sem, l * self.per + (n - self.per)
        return self.sem, l * self.per + n

    def last(self, l):
        return self.sem, (l * self.per + self.base if l is not None else 0) + self.n

    def learnt(self):
        return (self.start, self.n, self.new)


def build(nc, wstream, params, consts, norms, x_in, out, known):
    ctx = ExitStack()
    with ctx:
        def sb(name, shape, dt=F32):
            return ctx.enter_context(nc.sbuf_tensor(name, shape, dt))

        def sem(name):
            return ctx.enter_context(nc.semaphore(name))

        raw = sb("raw", [P, RING, HALF])
        whi = sb("whi", [P, RING, HALF], F32R)
        wlo = sb("wlo", [P, RING, HALF], F32R)
        x = sb("x", [P, KT, T])
        ahi = sb("ahi", [P, KT, T], F32R)
        alo = sb("alo", [P, KT, T], F32R)
        proj = sb("proj", [P, NT, T])
        bhi = sb("bhi", [P, 12, T], F32R)
        blo = sb("blo", [P, 12, T], F32R)
        con = sb("con", [P, NCON])
        par = sb("par", [P, NPAR])
        nrm = sb("nrm", [P, (2 * L + 1) * KT])
        rstd = sb("rstd", [P, T])
        tmp = sb("tmp", [P, 2, 2 * T])
        tmq = sb("tmq", [P, 2 * T])
        Tm = sb("Tm", [P, 8, CHUNK])
        Rm = sb("Rm", [P, 8, CHUNK])
        attnT = sb("attnT", [P, 8, CHUNK])
        Vb = sb("Vb", [P, 8, HD])
        Kend = sb("Kend", [P, 8, HD])
        rows = sb("rows", [8, 4, T])
        small = sb("small", [P, 160])
        wabh = sb("wabh", [P, KT * 8], F32R)
        wabl = sb("wabl", [P, KT * 8], F32R)
        bank = [ctx.enter_context(nc.psum_tensor(f"bank{i}", [P, 512], F32)) for i in range(8)]

        loaded_raw = [sem(f"loaded_raw{i}") for i in range(RING)]
        loaded_con, loaded_nrm, loaded_x, loaded_par = (sem(n) for n in ("loaded_con", "loaded_nrm", "loaded_x", "loaded_par"))
        stored = sem("stored")
        PE = Signal(sem("tensor_done"), "pe", known)
        DV = Signal(sem("vector_done"), "dv", known)
        AC = Signal(sem("scalar_done"), "ac", known)
        signals = (PE, DV, AC)

        block = ctx.enter_context(nc.Block())

        def c_(name, n=None, p=slice(0, P)):
            return con[p, CON[name]:CON[name] + n]

        def p_(name, i=0, n=1, p=slice(0, P)):
            return par[p, OFF[name] + i:OFF[name] + i + n]

        sm = {}
        at = 0
        for name, n in [("gcol", 8), ("bcol", 8), ("sneg", 8), ("kes", 8), ("egl", 16), ("mx", 8), ("rs", 8),
                        ("brh", 4), ("bih", 4), ("bgh", 24), ("sp2", 4), ("sp4n", 4), ("nwh", 1), ("anex", 1),
                        ("l0", 4), ("l1", 4), ("l2", 4), ("l3", 4)]:
            sm[name] = small[:, at:at + n]
            at += n
        assert at <= 160

        def tiles(t, n, p=slice(0, P)):
            return proj[p, t:t + n, :]

        def flat(ap):
            return ap.rearrange("p a b -> p (a b)")

        def mat(t):
            return flat(tiles(t, 2)).rearrange("p (g c) -> p g c", g=8)

        def over(ap, n):
            return ap.unsqueeze(1).broadcast_to([ap.shape[0], n, ap.shape[1]])

        def each(ap, n):
            return ap.unsqueeze(2).broadcast_to([ap.shape[0], ap.shape[1], n])

        SQ, EG, E1, E2, LM, LT = 48, 44, 36, 38, 40, 42
        CM, XM = 8, 10
        PR, PT, VTOK = 48, 54, 44
        S0, WB, VN = 8, 16, 18
        XC, TR, TI, A0, UU, HS = 12, 52, 48, 24, 20, 52
        MIX = 0
        lower, upper = slice(0, 64), slice(64, 128)
        halves = ((0, lower), (1, upper))

        def Sst(i):
            return flat(tiles(S0 + 2 * i, 2)).rearrange("p (h e) -> p h e", h=HEADS)

        Wb = flat(tiles(WB, 2)).rearrange("p (h e) -> p h e", h=HEADS)
        vnb = flat(tiles(VN, 2)).rearrange("p (h e) -> p h e", h=HEADS)

        def b3(i, g):
            return bank[i][:, :].rearrange("p (g c) -> p g c", g=g)

        def ffn_of(c):
            i = c - FFN0
            if i < 2:
                return ("gate", "up")[i], 0
            if i == C_FFN - 1:
                return "down", PAIRS - 1
            j, r = divmod(i - 2, 3)
            return (("gate", j + 1), ("up", j + 1), ("down", j))[r]

        uses = [len(range(s, NH, RING)) for s in range(RING)]

        def landed(l, m, nxt=False):
            s = m % RING
            return loaded_raw[s], 16 * (l * uses[s] + m // RING + 1 + (uses[s] if nxt else 0))

        def last_user(m):
            return max(range(m % RING, NH, RING))

        @block.sync
        def _(sp):
            def load(g, m):
                sp.dma_start(raw[:, m % RING, :], wstream[g, :, (m % 2) * HALF:(m % 2 + 1) * HALF]).then_inc(loaded_raw[m % RING], 16)

            sp.dma_start(x[:, :, :], x_in).then_inc(loaded_x, 16)
            sp.dma_start(nrm[:, :], norms).then_inc(loaded_nrm, 16)
            for m in range(2):
                load(m // 2, m)
            sp.dma_start(con[:, :], consts).then_inc(loaded_con, 16)
            for m in range(2, RING):
                load(m // 2, m)
            with sp.Fori(0, L) as l:
                used = [AC.at(l, ("gates", 29), prev=True), DV.at(l, ("mixed", 3), prev=True)]
                used = [(s, sp.snap(v)) for s, v in used]
                for s, v in used:
                    sp.wait_ge(s, v)
                sp.dma_start(par[:, :], params[l]).then_inc(loaded_par, 16)
                for k in range(NH):
                    m = k + RING
                    chunk = sp.snap(l * CH + m // 2) if m < NH else None
                    if k < AHEAD:
                        sp.wait_ge(*DV.at(l, ("lo_next", k), prev=True))
                    elif m < NH or k == NH - 1:
                        sp.wait_ge(*DV.at(l, ("lo", k)))
                    if m < NH:
                        load(chunk, m)
                    elif k == NH - 1:
                        for n in range(RING):
                            load(l * CH + CH + n // 2, n)
            sp.wait_ge(*DV.at(L - 1, "out"))
            sp.dma_start(out, x[:, :, :]).then_inc(stored, 16)
            sp.wait_ge(stored, 16)
            for m in range(RING):
                sp.wait_ge(*landed(L, m))

        @block.tensor
        def _(pe):
            def products(dst, wcol, slot, hi, lo, first, last):
                pe.matmul(dst, whi[:, slot, wcol], hi, start=first, stop=False, skip_group_check=True)
                pe.matmul(dst, whi[:, slot, wcol], lo, start=False, stop=False, skip_group_check=True)
                return pe.matmul(dst, wlo[:, slot, wcol], hi, start=False, stop=last, skip_group_check=True)

            def wait_split(l, k):
                if k < AHEAD:
                    pe.wait_ge(*DV.at(l, ("lo_next", k), prev=True))
                else:
                    pe.wait_ge(*DV.at(l, ("lo", k)))

            def cols(j):
                return slice(j * P, (j + 1) * P)

            def by_output(l, k, dst, start_kt, act_wait=None):
                for i in range(4):
                    kt = start_kt + i
                    if act_wait is not None:
                        act_wait(kt)
                    if i == 3:
                        early_waits(l, k)
                    for n in range(2):
                        ins = products(dst[:, n * T:(n + 1) * T], cols(2 * i + n), k % RING,
                                       ahi[:, kt, :], alo[:, kt, :], kt == 0 and n == 0, kt == KT - 1)
                ins.then_inc(*PE.up(("bulk", k)))

            def y_half(k, base):
                c = k // 2 - C_IN
                br = c % 3
                for i in range(2):
                    kt = (k % 2) * 2 + i
                    for n in range(4):
                        ins = products(bank[base + n // 2][:, (n % 2) * T:(n % 2 + 1) * T], cols(4 * i + n), k % RING,
                                       bhi[:, 4 * br + kt, :], blo[:, 4 * br + kt, :],
                                       kt == 0 and n % 2 == 0, kt == 3)
                ins.then_inc(*PE.up(("bulk", k)))

            def by_contraction(k, hi, lo, first, last):
                for n in range(8):
                    ins = products(bank[4 + n // 2][:, (n % 2) * T:(n % 2 + 1) * T], cols(n), k % RING, hi, lo,
                                   first and n % 2 == 0, last)
                    if last and n % 2:
                        ins.then_inc(*PE.up(("acc", k, n // 2)))
                if not last:
                    ins.then_inc(*PE.up(("bulk", k)))
                else:
                    PE.new[("bulk", k)] = PE.n

            def early_waits(l, k):
                if k == 18:
                    pe.wait_ge(*DV.at(l, "knorm"))
                if k == 20:
                    pe.wait_ge(*DV.at(l, "lmat"))
                if 24 <= k <= 33:
                    i, part = divmod(k - 24, 2)
                    pe.wait_ge(*DV.at(l, ("xcopy", i) if part else ("level", i)))
                if 34 < k <= 45 and (k - 34) % 3 == 1:
                    pe.wait_ge(*DV.at(l, ("w", (k - 34) // 3)))

            def exact(dst, lhsT, rhs, start=True, stop=True):
                return pe.matmul(dst, lhsT, rhs, start=start, stop=stop, skip_group_check=True)

            def norm_sum(l, step):
                pe.wait_ge(*DV.at(l, (step, "acc"), prev=(step == "mix")))
                for i in range(2):
                    ins = exact(bank[2][:, 0:T], c_("ones", 128), tmq[:, i * T:(i + 1) * T], i == 0, i == 1)
                ins.then_inc(*PE.up((step, "sum")))

            def side(l, k):
                if k == 0:
                    norm_sum(l, "mix")
                if k == 1:
                    pe.wait_ge(*DV.at(l, "wab"))
                    for j in range(2):
                        for kt in range(KT):
                            w = slice(kt * 8 + 4 * j, kt * 8 + 4 * j + 4)
                            dst = bank[3][0:4, j * T:(j + 1) * T]
                            f = kt == 0 and j == 0
                            pe.matmul(dst, wabh[:, w], ahi[:, kt, :], start=f, stop=False, skip_group_check=True)
                            pe.matmul(dst, wabh[:, w], alo[:, kt, :], start=False, stop=False, skip_group_check=True)
                            ins = pe.matmul(dst, wabl[:, w], ahi[:, kt, :], start=False, stop=kt == KT - 1, skip_group_check=True)
                    ins.then_inc(*PE.up("ab"))
                if k == 9:
                    pe.wait_ge(*DV.at(l, "grow"))
                    for m in range(2):
                        exact(bank[3][:, m:8:2], rows[0:4, 0, m * P:(m + 1) * P], c_("ident", 4, slice(0, 4)))
                        exact(bank[3][:, 8 + m:16:2], rows[0:4, 1, m * P:(m + 1) * P], c_("ident", 4, slice(0, 4)))
                    for h in range(HEADS):
                        sel = con[0:4, CON["ident"] + h:CON["ident"] + h + 1].broadcast_to([4, P])
                        ins = exact(bank[4 + h // 2][:, (h % 2) * T:(h % 2 + 1) * T], sel, rows[0:4, 0, :])
                    ins.then_inc(*PE.up("gbc"))
                if k == 12:
                    pe.wait_ge(*AC.at(l, ("sq", 3)))
                    for t in range(8):
                        ins = exact(bank[2][0:8, 0:T], c_("ecol", 64)[:, 8 * t:8 * t + 8], proj[:, SQ + t, :], t == 0, t == 7)
                    ins.then_inc(*PE.up("sumqk"))
                if k in (15, 16):
                    pe.wait_ge(*DV.at(l, "rqk"))
                    if k == 16:
                        pe.wait_ge(*AC.at(l, "eg"))
                    for h in range(HEADS):
                        t = 4 * (k - 15) + h
                        sel = con[0:8, CON["ident"] + t:CON["ident"] + t + 1].broadcast_to([8, P])
                        ins = exact(bank[(6, 4)[k - 15] + h // 2][:, (h % 2) * T:(h % 2 + 1) * T], sel, rows[0:8, 2, :])
                    ins.then_inc(*PE.up(("rbc", k - 15)))
                if k == 18:
                    for b, q0 in ((6, TK), (7, TQ)):
                        for h in range(HEADS):
                            for n in range(NCH):
                                m, a = divmod(n, 2)
                                cs = slice(n * CHUNK, (n + 1) * CHUNK)
                                ins = exact(b3(b, 8)[64 * a:64 * a + 64, 2 * h + m, :], proj[:, TK + h, cs], proj[:, q0 + h, cs])
                    ins.then_inc(*PE.up("kk"))
                if k == 20:
                    for g in range(8):
                        for a, pa in halves:
                            ins = exact(b3(2, 8)[pa, g, :], mat(LM)[pa, g, :], c_("eye", 64, pa))
                    ins.then_inc(*PE.up("lt"))
                if k == 21:
                    pe.wait_ge(*DV.at(l, ("silu", 5)))
                    for g in range(8):
                        h, m = divmod(g, 2)
                        ins = pe.transpose(b3(4 + g // 4, 4)[:, g % 4, :], proj[:, TV + h, m * P:(m + 1) * P], c_("ident", 128))
                    ins.then_inc(*PE.up("vT"))
                if k == 22:
                    for g in range(8):
                        h, m = divmod(g, 2)
                        ins = pe.transpose(b3(6 + g // 4, 4)[:, g % 4, :], proj[:, TK + h, m * P:(m + 1) * P], c_("ident", 128))
                    ins.then_inc(*PE.up("kT"))
                if 24 <= k <= 33:
                    i, part = divmod(k - 24, 2)
                    if part == 0:
                        for g in range(8):
                            for a, pa in halves:
                                ins = exact(b3(2, 8)[pa, g, :], mat(CM)[pa, g, :], Tm[pa, g, :])
                        ins.then_inc(*PE.up(("X", i)))
                    else:
                        for b, lt, rt in ((6, Rm, mat(XM)), (7, mat(XM), Rm)):
                            if i == 4 and b == 6:
                                continue
                            for g in range(8):
                                for a, pa in halves:
                                    ins = exact(b3(b, 8)[pa, g, :], lt[pa, g, :], rt[pa, g, :])
                        ins.then_inc(*PE.up(("TX", i)))
                if k == 26:
                    pe.wait_ge(*DV.at(l, "rope"))
                    pe.wait_ge(*DV.at(l, "vb"))
                    for h in range(HEADS):
                        exact(b3(5, 4)[:, h, :], proj[:, TMQ + h, 0:P], proj[:, TMK + h, 0:P])
                        ins = exact(bank[3 + h // 2][:, (h % 2) * T:(h % 2 + 1) * T], proj[:, TMQ + h, P:T], proj[:, TMK + h, :])
                    ins.then_inc(*PE.up("scores"))
                if k == 28:
                    pe.wait_ge(*DV.at(l, "masked"))
                    for g in range(8):
                        h, m = divmod(g, 2)
                        ins = pe.transpose(b3(3 + g // 4, 4)[:, g % 4, :], proj[:, TMV + h, m * P:(m + 1) * P], c_("ident", 128))
                    ins.then_inc(*PE.up("mvT"))
                if k == 30:
                    pe.wait_ge(*DV.at(l, "probs"))
                    pe.wait_ge(*AC.at(l, "vtok"))
                    pr = flat(tiles(PR, 6))
                    for g in range(12):
                        ins = pe.transpose(b3(3 + g // 4, 4)[:, g % 4, :], pr[:, g * P:(g + 1) * P], c_("ident", 128))
                    ins.then_inc(*PE.up("pT"))
                if k == 32:
                    pe.wait_ge(*DV.at(l, "pcopy"))
                    vt = flat(tiles(VTOK, 4)).rearrange("p (g d) -> p g d", g=8)
                    pt = flat(tiles(PT, 6)).rearrange("p (g q) -> p g q", g=12)
                    for h in range(HEADS):
                        d0 = bank[3 + h // 2][:, (h % 2) * T:(h % 2) * T + P]
                        d1 = bank[3 + h // 2][:, (h % 2) * T + P:(h % 2 + 1) * T]
                        exact(d0, vt[:, 2 * h, :], pt[:, h, :])
                        exact(d1, vt[:, 2 * h, :], pt[:, 4 + 2 * h, :], True, False)
                        ins = exact(d1, vt[:, 2 * h + 1, :], pt[:, 5 + 2 * h, :], False, True)
                    ins.then_inc(*PE.up("pv"))
                if k in (33, 34):
                    pe.wait_ge(*DV.at(l, "xc"))
                    if k == 34:
                        pe.wait_ge(*DV.at(l, "mb_out"))
                    else:
                        pe.wait_ge(*DV.at(l, ("xcopy", 4)))
                    w, bs = (("wi", (5, 2)), ("wr", (3, 4)))[k - 33]
                    for t in range(4):
                        ins = exact(bank[bs[t // 2]][:, (t % 2) * T:(t % 2 + 1) * T], p_(w, t * P, P), proj[:, XC + t, :])
                    ins.then_inc(*PE.up(w))
                if 34 < k <= 45:
                    n, part = divmod(k - 34, 3)
                    m, a = divmod(n, 2)
                    pa = (lower, upper)[a]
                    cs = slice(n * CHUNK, (n + 1) * CHUNK)
                    if part == 0:
                        pe.wait_ge(*DV.at(l, ("state", n)))
                        for h in range(HEADS):
                            ins = exact(b3(6, 4)[pa, h, :], proj[:, TK + h, cs], Sst(n % 2)[:, h, :])
                        ins.then_inc(*PE.up(("KS", n)))
                    if part == 1:
                        for h in range(HEADS):
                            ins = exact(b3(7, 4)[pa, h, :], Rm[pa, 2 * h + m, :], (Vb[pa, m:8:2, :] if n == 0 else Wb[pa, :, :])[:, h, :])
                        ins.then_inc(*PE.up(("VN", n)))
                    if part == 2:
                        pe.wait_ge(*AC.at(l, ("vn", n)))
                        if n == 0:
                            pe.wait_ge(*AC.at(l, "tanh_r"))
                        for h in range(HEADS):
                            o = bank[3 + h // 2][:, (h % 2) * T + n * CHUNK:(h % 2) * T + (n + 1) * CHUNK]
                            if n:
                                exact(o, Sst(n % 2)[:, h, :], proj[:, TQ + h, cs], True, False)
                            ins = exact(o, vnb[pa, h, :], attnT[pa, 2 * h + m, :], n == 0, True)
                            if n < NCH - 1:
                                ins = exact(b3(2, 4)[:, h, :], Kend[pa, 2 * h + m, :], vnb[pa, h, :])
                        ins.then_inc(*PE.up(("SU", n)))
                if k == 47:
                    pe.wait_ge(*AC.at(l, "osq"))
                    for t in range(4):
                        ins = exact(bank[2][0:8, 0:T], c_("ecol", 64)[:, 8 * t:8 * t + 8], proj[:, WB + t, :], t == 0, t == 3)
                    ins.then_inc(*PE.up("sumo"))
                if k == 50:
                    pe.wait_ge(*DV.at(l, "ro"))
                    for h in range(HEADS):
                        sel = con[0:8, CON["ident"] + h:CON["ident"] + h + 1].broadcast_to([8, P])
                        ins = exact(bank[6 + h // 2][:, (h % 2) * T:(h % 2 + 1) * T], sel, rows[0:8, 2, :])
                    ins.then_inc(*PE.up("robc"))

            pe.wait_ge(loaded_con, 16)
            pe.nop().then_inc(PE.sem, max(PE.per, 1))
            PE.n = max(PE.per, 1)
            PE.open_layer()
            with pe.Fori(0, L) as l:
                for k in range(NH):
                    c, half = divmod(k, 2)
                    wait_split(l, k)
                    if c < C_IN:
                        if c >= 2 and half == 0:
                            pe.wait_ge(*DV.at(l, ("evac", c - 2)))
                        aw = None
                        if c == 0:
                            aw = lambda kt: pe.wait_ge(*DV.at(l, ("mix", "lo", kt // 2), prev=True)) if kt % 2 == 0 else None
                        by_output(l, k, bank[c % 2], 4 * half, aw)
                        side(l, k)
                    elif c < C_IN + C_Y:
                        i = c - C_IN
                        if half == 0:
                            if i == 0:
                                pe.wait_ge(*DV.at(l, ("evac", 29)))
                                pe.wait_ge(*DV.at(l, "dn_out"))
                            if i == 2:
                                pe.wait_ge(*DV.at(l, "lru_out"))
                            if i >= 2:
                                pe.wait_ge(*DV.at(l, ("y", i - 2)))
                        y_half(k, 2 * (i % 2))
                    elif c < FFN0:
                        i = k - 2 * (C_IN + C_Y)
                        if i == 0:
                            pe.wait_ge(*DV.at(l, ("mixed", 1)))
                        if i == 4:
                            pe.wait_ge(*DV.at(l, ("mixed", 3)))
                        by_contraction(k, ahi[:, i, :], alo[:, i, :], i == 0, i == KT - 1)
                    else:
                        kind, j = ffn_of(c)
                        if kind == "down":
                            if half == 0:
                                pe.wait_ge(*DV.at(l, ("hidden", j)))
                            t = 2 * (j % 2) + half
                            by_contraction(k, bhi[:, t, :], blo[:, t, :], j == 0 and half == 0, j == PAIRS - 1 and half == 1)
                        else:
                            if half == 0 and j > 0:
                                pe.wait_ge(*DV.at(l, (kind, j - 1)))
                            aw = None
                            if kind == "gate" and j == 0:
                                aw = lambda kt: pe.wait_ge(*DV.at(l, ("ffn", "lo", kt // 2))) if kt % 2 == 0 else None
                            by_output(l, k, bank[kind == "up"], 4 * half, aw)
                            if kind == "gate" and j == 0 and half == 0:
                                norm_sum(l, "ffn")
            PE.layer = L
            norm_last = DV.at(L, ("mix", "acc"), prev=True)
            pe.wait_ge(*norm_last)
            for i in range(2):
                ins = exact(bank[2][:, 0:T], c_("ones", 128), tmq[:, i * T:(i + 1) * T], i == 0, i == 1)
            ins.then_inc(PE.sem, 1)
        PE_FINAL = PE.base + L * PE.per + 1

        @block.scalar
        def _(act):
            def hi(l, m, nxt=False):
                act.wait_ge(*landed(l, m, nxt))
                if l is not None and m >= RING:
                    act.wait_ge(*PE.at(l, ("bulk", m - RING)))
                elif l is not None and nxt:
                    act.wait_ge(*PE.at(l, ("bulk", last_user(m))))
                elif l is not None:
                    act.wait_ge(*PE.at(l, ("bulk", last_user(m)), prev=True))
                act.copy(whi[:, m % RING, :], raw[:, m % RING, :]).then_inc(*AC.up(("hi_next" if nxt or l is None else "hi", m)))

            def x_norm(l, step, nidx, bulk):
                for p in range(4):
                    if l is None:
                        if p == 0:
                            act.wait_ge(loaded_x, 16)
                            act.wait_ge(loaded_nrm, 16)
                    else:
                        act.wait_ge(*DV.at(l, (step, "x", p)))
                    for i in range(2):
                        act.activation(ahi[:, 2 * p + i, :], x[:, 2 * p + i, :], ACT.Copy,
                                       scale=nrm[:, bass.ds(nidx * KT + 2 * p + i, 1)]).then_inc(*AC.up())
                    AC.new[(step, "hi", p)] = AC.n
                    if p >= 2:
                        if l is None:
                            act.wait_ge(DV.sem, 3 * (p - 1))
                        else:
                            act.wait_ge(*DV.at(l, (step, "accp", p - 2)))
                    act.activation(tmp[:, p % 2, :], flat(x[:, 2 * p:2 * p + 2, :]), ACT.Square).then_inc(*AC.up((step, "sq", p)))

            def side(l, k):
                if k == 0:
                    act.wait_ge(loaded_par, l * 16 + 16)
                    act.copy(wabh[:, :], p_("wab", 0, 64)).then_inc(*AC.up("wabh"))
                    act.activation(sm["anex"][0:4], p_("alog", 0, 1, slice(0, 4)), ACT.Exp).then_inc(*AC.up())
                    act.wait_ge(*DV.at(l, "lamabs"))
                    act.activation(sm["l2"], sm["l1"], ACT.Exp, scale=-1.0).then_inc(*AC.up("lamexp"))
                if k == 5:
                    act.wait_ge(*DV.at(l, "aabs"))
                    act.activation(rows[0:4, 2, :], rows[0:4, 3, :], ACT.Exp, scale=-1.0).then_inc(*AC.up())
                    act.activation(rows[0:4, 1, :], rows[0:4, 1, :], ACT.Tanh, scale=0.5).then_inc(*AC.up("aexp"))
                if 3 <= k <= 14:
                    c, odd = divmod(k - 3, 2)
                    if not odd:
                        act.wait_ge(*DV.at(l, ("conv", c)))
                        act.activation(tmq[:, :], tmp[:, c % 2, :], ACT.Tanh, scale=0.5).then_inc(*AC.up(("tanh", c)))
                    elif c < 4:
                        act.wait_ge(*DV.at(l, ("silu", c)))
                        act.activation(tiles(SQ + 2 * c, 2), tiles(2 * c, 2), ACT.Square).then_inc(*AC.up(("sq", c)))
                if k == 10:
                    act.wait_ge(*DV.at(l, "dif"))
                    act.activation(sm["egl"], proj_last(), ACT.Exp).then_inc(*AC.up())
                    for h in range(2):
                        act.activation(flat(tiles(EG + 2 * h, 2)), bank[4 + h][:, :], ACT.Exp).then_inc(*AC.up())
                    AC.new["eg"] = AC.n
                    act.activation(mat(E1), mat(E1), ACT.Exp).then_inc(*AC.up())
                    act.activation(mat(E2), mat(E2), ACT.Exp, scale=-1.0).then_inc(*AC.up())
                    act.activation(sm["kes"], sm["kes"], ACT.Exp).then_inc(*AC.up())
                    act.activation(sm["sneg"], sm["gcol"], ACT.Exp).then_inc(*AC.up("decays"))
                if k == 28:
                    act.wait_ge(*DV.at(l, "rowmax"))
                    pr = flat(tiles(PR, 6))
                    for g in range(8):
                        a, b = (g * P, g * P + P) if g < 4 else (512 + (g - 4) * T, 512 + (g - 3) * T)
                        act.activation(pr[:, a:b], pr[:, a:b], ACT.Exp, bias=sm["mx"][:, g:g + 1], scale=HD ** -0.5,
                                       accum_out=sm["rs"][:, g:g + 1]).then_inc(*AC.up())
                    AC.new["exp"] = AC.n
                if k == 29:
                    act.wait_ge(*PE.at(l, "mvT"))
                    for i in range(2):
                        act.copy(flat(tiles(VTOK + 2 * i, 2)), bank[3 + i][:, :]).then_inc(*AC.up())
                    AC.new["vtok"] = AC.n
                if k == 33:
                    act.wait_ge(*PE.at(l, "pv"))
                    for i in range(2):
                        act.copy(flat(bhi[:, 4 + 2 * i:6 + 2 * i, :]), bank[3 + i][:, :]).then_inc(*AC.up())
                    AC.new["mbhi"] = AC.n
                if k in (34, 35):
                    w, bs, dst, bias = (("wi", (5, 2), TI, "bih"), ("wr", (3, 4), TR, "brh"))[k - 34]
                    act.wait_ge(*PE.at(l, w))
                    for t in range(4):
                        act.activation(proj[:, dst + t, :], bank[bs[t // 2]][:, (t % 2) * T:(t % 2 + 1) * T], ACT.Tanh,
                                       bias=sm[bias][:, t:t + 1], scale=0.5).then_inc(*AC.up())
                    AC.new[("tanh_i", "tanh_r")[k - 34]] = AC.n
                if k == 36:
                    act.wait_ge(*AC.last(l))
                    for t in range(4):
                        act.activation(proj[:, A0 + t, :], proj[:, TR + t, :], ACT.Exp,
                                       bias=sm["sp4n"][:, t:t + 1], scale=sm["sp4n"][:, t:t + 1]).then_inc(*AC.up())
                    act.wait_ge(*AC.last(l))
                    for t in range(4):
                        act.activation(proj[:, TR + t, :], proj[:, TR + t, :], ACT.Tanh,
                                       bias=sm["sp2"][:, t:t + 1], scale=sm["sp2"][:, t:t + 1]).then_inc(*AC.up())
                    AC.new["a0"] = AC.n
                if 36 <= k <= 45 and (k - 36) % 3 == 0:
                    n = (k - 36) // 3
                    pa = (lower, upper)[n % 2]
                    act.wait_ge(*PE.at(l, ("VN", n)))
                    act.copy(vnb[pa, :, :], b3(7, 4)[pa, :, :]).then_inc(*AC.up(("vn", n)))
                if k == 37:
                    act.wait_ge(*DV.at(l, ("evac", 17)))
                    act.activation(flat(tiles(TMV, 4)), flat(tiles(TZ, 4)), ACT.Tanh, scale=0.5).then_inc(*AC.up("tz"))
                if k == 40:
                    act.wait_ge(*DV.at(l, "lru_m"))
                    act.activation(tiles(TR, 4), tiles(TR, 4), ACT.Sqrt).then_inc(*AC.up("sqT"))
                if k == 43:
                    act.wait_ge(*DV.at(l, "lru_uv"))
                    act.activation(tiles(TI, 4), tiles(TLY, 4), ACT.Square).then_inc(*AC.up("y2"))
                if k == 45:
                    act.wait_ge(*DV.at(l, "gelu_in"))
                    act.activation(tiles(TI, 4), tiles(TI, 4), ACT.Tanh, scale=float(np.sqrt(2 / np.pi))).then_inc(*AC.up("gelu_t"))
                if k == 46:
                    act.wait_ge(*PE.at(l, ("SU", 3)))
                    for i in range(2):
                        act.activation(flat(tiles(WB + 2 * i, 2)), bank[3 + i][:, :], ACT.Square).then_inc(*AC.up())
                    AC.new["osq"] = AC.n
                if k == 48:
                    act.wait_ge(*DV.at(l, "lru_f"))
                    act.activation(bhi[:, 8:12, :], tiles(TI, 4), ACT.Copy, scale=0.25).then_inc(*AC.up("lruhi"))
                if k == 52:
                    act.wait_ge(*DV.at(l, "dn_f"))
                    act.activation(bhi[:, 0:4, :], tiles(TMQ, 4), ACT.Copy).then_inc(*AC.up("dnhi"))
                c = (k - 2) // 2
                if k % 2 == 0 and 18 <= c <= 29:
                    act.wait_ge(*DV.at(l, ("evac", c)))
                    for i in range(2):
                        t = 2 * c + i
                        act.activation(proj[:, t, :], proj[:, t, :], ACT.Tanh, bias=sm["bgh"][:, t - TG:t - TG + 1],
                                       scale=0.5).then_inc(*AC.up())
                    AC.new[("gates", c)] = AC.n
                if 66 <= k <= 72 and (k - 66) % 6 == 0:
                    for f in range(2):
                        i = 2 * ((k - 66) // 6) + f
                        act.wait_ge(*DV.at(l, ("mixf", i)))
                        act.activation(ahi[:, 2 * i:2 * i + 2, :], tiles(MIX + 2 * i, 2), ACT.Copy, scale=0.5).then_inc(*AC.up(("mixhi", i)))
                if k == 2 * FFN0:
                    x_norm(l, "ffn", l * 2 + 1, None)
                if k > 2 * FFN0 and k % 2 == 0:
                    kind, j = ffn_of(k // 2 - 1)
                    s = 8 * (j % 2)
                    if kind == "gate":
                        act.wait_ge(*DV.at(l, ("gate", j)))
                        act.activation(tiles(s + 2, 2), tiles(s, 2), ACT.Tanh, scale=0.5).then_inc(*AC.up(("ftanh", j)))
                    if kind == "up":
                        act.wait_ge(*DV.at(l, ("hidf", j)))
                        act.activation(bhi[:, 2 * (j % 2):2 * (j % 2) + 2, :], tiles(s + 6, 2), ACT.Copy, scale=0.5).then_inc(*AC.up(("hidhi", j)))

            def proj_last():
                return sm["egl"]

            x_norm(None, "mix", 0, None)
            for m in range(AHEAD):
                act.wait_ge(loaded_raw[m], 16)
                act.copy(whi[:, m, :], raw[:, m, :]).then_inc(*AC.up(("hi_next", m)))
            AC.first = dict(AC.new)
            act.wait_ge(AC.sem, AC.n)
            act.nop().then_inc(AC.sem, max(AC.per, 1))
            AC.n += max(AC.per, 1)
            AC.open_layer()
            with act.Fori(0, L) as l:
                for k in range(NH):
                    if k + AHEAD < NH:
                        hi(l, k + AHEAD)
                    side(l, k)
                    if k + AHEAD >= NH and k + AHEAD + 1 - NH < AHEAD:
                        hi(l, k + AHEAD + 1 - NH, True)
                x_norm(l, "mix", l * 2 + 2, None)
                hi(l, 0, True)
        @block.vector
        def _(dv):
            def step(ins, name=None):
                ins.then_inc(*DV.up(name))
                return DV.n

            def settle(l):
                dv.wait_ge(*DV.last(l))

            def lo(l, m, nxt=False):
                if l is None:
                    dv.wait_ge(AC.sem, AC.first[("hi_next", m)])
                else:
                    dv.wait_ge(*AC.at(l, ("hi_next" if nxt else "hi", m)))
                dv.tensor_tensor(wlo[:, m % RING, :], raw[:, m % RING, :], whi[:, m % RING, :], ALU.subtract)\
                  .then_inc(*DV.up(("lo_next" if nxt or l is None else "lo", m)))

            def rsqrt(l, src, y, t, scale, eps, p, done):
                w, u = t
                step(dv.tensor_scalar(w, src, scale, eps, ALU.mult, ALU.add))
                settle(l)
                step(dv.tensor_scalar(y.bitcast(I32), w.bitcast(I32), -0.5, float(0x5F3759DF), ALU.mult, ALU.add))
                for i in range(3):
                    settle(l)
                    step(dv.scalar_tensor_tensor(out=u, in0=y, scalar=-0.5, in1=y, op0=ALU.mult, op1=ALU.mult))
                    settle(l)
                    step(dv.tensor_tensor(u, u, w, ALU.mult))
                    settle(l)
                    step(dv.scalar_tensor_tensor(out=y, in0=u, scalar=1.5, in1=y, op0=ALU.add, op1=ALU.mult), done if i == 2 else None)

            def log1p(l, e, s, s2, acc):
                step(dv.tensor_scalar(s2, e, 2.0, None, ALU.add))
                settle(l)
                step(dv.reciprocal(acc, s2))
                settle(l)
                step(dv.tensor_tensor(s, e, acc, ALU.mult))
                settle(l)
                step(dv.tensor_tensor(s2, s, s, ALU.mult))
                settle(l)
                step(dv.tensor_scalar(acc, s2, 1.0 / 15, 1.0 / 13, ALU.mult, ALU.add))
                settle(l)
                step(dv.tensor_tensor(acc, acc, s2, ALU.mult))
                for c in (11, 9, 7, 5, 3):
                    settle(l)
                    step(dv.scalar_tensor_tensor(out=acc, in0=acc, scalar=1.0 / c, in1=s2, op0=ALU.add, op1=ALU.mult))
                settle(l)
                step(dv.scalar_tensor_tensor(out=acc, in0=acc, scalar=1.0, in1=s, op0=ALU.add, op1=ALU.mult))
                settle(l)
                step(dv.tensor_scalar(acc, acc, 2.0, None, ALU.mult))

            def conv(l, src, dst, w):
                step(dv.tensor_scalar(dst, src, par[:, w + 3:w + 4], None, ALU.mult))
                for s in (1, 2, 3):
                    settle(l)
                    step(dv.scalar_tensor_tensor(out=dst[:, s:T], in0=src[:, 0:T - s], scalar=par[:, w + 3 - s:w + 4 - s],
                                                 in1=dst[:, s:T], op0=ALU.mult, op1=ALU.add))

            def x_add(l, step_name, k):
                for p in range(4):
                    dv.wait_ge(*PE.at(l, ("acc", k, p)))
                    step(dv.tensor_tensor(flat(x[:, 2 * p:2 * p + 2, :]), bank[4 + p][:, :], flat(x[:, 2 * p:2 * p + 2, :]), ALU.add),
                         (step_name, "x", p))

            def x_norm(l, name, nidx, p):
                if l is None:
                    dv.wait_ge(AC.sem, AC.first[(name, "sq", p)])
                else:
                    dv.wait_ge(*AC.at(l, (name, "sq", p)))
                for i in range(2):
                    step(dv.scalar_tensor_tensor(out=alo[:, 2 * p + i, :], in0=x[:, 2 * p + i, :],
                                                 scalar=nrm[:, bass.ds(nidx * KT + 2 * p + i, 1)],
                                                 in1=ahi[:, 2 * p + i, :].bitcast(F32), op0=ALU.mult, op1=ALU.subtract))
                DV.new[(name, "lo", p)] = DV.n
                if p == 0:
                    step(dv.tensor_copy(tmq[:, :], tmp[:, 0, :]), (name, "accp", 0))
                else:
                    settle(l)
                    step(dv.tensor_tensor(tmq[:, :], tmq[:, :], tmp[:, p % 2, :], ALU.add), (name, "accp", p))
                if p == 3:
                    DV.new[(name, "acc")] = DV.n

            def rnorm(l, name):
                dv.wait_ge(*PE.at(l, (name, "sum")))
                rsqrt(l, bank[2][:, 0:T], rstd[:, :], (tmp[:, 0, 0:T], tmp[:, 0, T:2 * T]), 1.0 / D, EPS, P, (name, "rstd"))

            def side(l, k):
                if k == 0:
                    dv.wait_ge(loaded_par, l * 16 + 16)
                    dv.wait_ge(*AC.at(l, "wabh"))
                    step(dv.tensor_tensor(wabl[:, :], p_("wab", 0, 64), wabh[:, :], ALU.subtract), "wab")
                    step(dv.tensor_scalar(sm["l0"], p_("lam", 0, 4), -1.0, None, ALU.mult))
                    settle(l)
                    step(dv.tensor_tensor(sm["l1"], p_("lam", 0, 4), sm["l0"], ALU.max), "lamabs")
                    step(dv.tensor_scalar(sm["brh"], p_("br", 0, 4), 0.5, None, ALU.mult))
                    step(dv.tensor_scalar(sm["bih"], p_("bi", 0, 4), 0.5, None, ALU.mult))
                    step(dv.tensor_scalar(sm["bgh"], p_("bg", 0, 24), 0.5, None, ALU.mult))
                    step(dv.tensor_scalar(sm["nwh"], p_("dnorm"), 0.5, None, ALU.mult))
                    dv.wait_ge(*AC.at(l, "lamexp"))
                    step(dv.tensor_scalar(sm["anex"][0:4], sm["anex"][0:4], -1.0, None, ALU.mult))
                if k == 1:
                    rnorm(l, "mix")
                if k == 4:
                    log1p(l, sm["l2"], sm["l1"], sm["sp4n"], sm["l3"])
                    settle(l)
                    step(dv.scalar_tensor_tensor(out=sm["l3"], in0=sm["l0"], scalar=0.0, in1=sm["l3"], op0=ALU.max, op1=ALU.add))
                    settle(l)
                    step(dv.tensor_scalar(sm["sp2"], sm["l3"], 2.0, None, ALU.mult))
                    step(dv.tensor_scalar(sm["sp4n"], sm["l3"], -4.0, None, ALU.mult))
                    dv.wait_ge(*PE.at(l, "ab"))
                    step(dv.tensor_tensor(rows[0:4, 0, :], bank[3][0:4, 0:T], rstd[0:4, :], ALU.mult))
                    step(dv.tensor_tensor(rows[0:4, 1, :], bank[3][0:4, T:2 * T], rstd[0:4, :], ALU.mult))
                    settle(l)
                    step(dv.tensor_scalar(rows[0:4, 0, :], rows[0:4, 0, :], p_("dtb", 0, 1, slice(0, 4)), None, ALU.add))
                    settle(l)
                    step(dv.tensor_scalar(rows[0:4, 2, :], rows[0:4, 0, :], -1.0, None, ALU.mult))
                    settle(l)
                    step(dv.tensor_tensor(rows[0:4, 3, :], rows[0:4, 0, :], rows[0:4, 2, :], ALU.max), "aabs")
                if k == 6:
                    dv.wait_ge(*AC.at(l, "aexp"))
                    log1p(l, rows[0:4, 2, :], rows[0:4, 3, :], tmq4(0), tmq4(1))
                    step(dv.tensor_scalar(rows[0:4, 1, :], rows[0:4, 1, :], 0.5, 0.5, ALU.mult, ALU.add))
                    settle(l)
                    step(dv.scalar_tensor_tensor(out=rows[0:4, 2, :], in0=rows[0:4, 0, :], scalar=0.0, in1=tmq4(1), op0=ALU.max, op1=ALU.add))
                    settle(l)
                    step(dv.tensor_scalar(rows[0:4, 2, :], rows[0:4, 2, :], sm["anex"][0:4], None, ALU.mult))
                    settle(l)
                    step(dv.tensor_tensor_scan(rows[0:4, 0, :], c_("reset", 256, slice(0, 4)), rows[0:4, 2, :], 0.0, ALU.mult, ALU.add), "grow")
                if 3 <= k <= 14:
                    c, odd = divmod(k - 3, 2)
                    if not odd:
                        settle(l)
                        for i in range(2):
                            conv(l, proj[:, 2 * c + i, :], tmp[:, c % 2, i * T:(i + 1) * T], OFF["conv"] + TAPS * (2 * c + i))
                        DV.new[("conv", c)] = DV.n
                    else:
                        dv.wait_ge(*AC.at(l, ("tanh", c)))
                        step(dv.scalar_tensor_tensor(out=flat(tiles(2 * c, 2)), in0=tmq[:, :], scalar=1.0, in1=tmp[:, c % 2, :],
                                                     op0=ALU.add, op1=ALU.mult), ("silu", c))
                if k == 10:
                    dv.wait_ge(*PE.at(l, "gbc"))
                    step(dv.tensor_copy(sm["gcol"], bank[3][:, 0:8]))
                    step(dv.tensor_copy(sm["bcol"], bank[3][:, 8:16]))
                    settle(l)
                    for a, pa in halves:
                        for b in range(2):
                            gb = b3(4 + b, 4)[pa, :, 64 * a:64 * a + 64]
                            gs = slice(4 * b, 4 * b + 4)
                            step(dv.tensor_tensor(mat(LM)[pa, gs, :], gb, each(sm["gcol"][pa, gs], CHUNK), ALU.subtract))
                            step(dv.tensor_tensor(sm["kes"][pa, gs], gb[:, :, 63], sm["gcol"][pa, gs], ALU.subtract))
                    for b in range(2):
                        step(dv.tensor_copy(sm["egl"][:, 8 * b:8 * b + 8], bank[4 + b][:, 63:512:64]))
                    settle(l)
                    step(dv.tensor_scalar(mat(E1), mat(LM), 0.0, None, ALU.min))
                    step(dv.tensor_scalar(mat(E2), mat(LM), 0.0, None, ALU.max), "dif")
                if k == 12:
                    dv.wait_ge(*AC.at(l, "decays"))
                    step(dv.tensor_tensor(mat(E1), mat(E1), over(c_("upin", 64), 8), ALU.mult))
                    step(dv.tensor_tensor(mat(E2), mat(E2), over(c_("low", 64), 8), ALU.mult))
                    step(dv.scalar_tensor_tensor(out=sm["sneg"], in0=sm["sneg"], scalar=-1.0, in1=sm["bcol"], op0=ALU.mult, op1=ALU.mult))
                    settle(l)
                    step(dv.tensor_tensor(mat(E2), mat(E2), each(sm["bcol"], CHUNK), ALU.mult))
                    step(dv.tensor_scalar(sm["mx"], sm["bcol"], 0.5, None, ALU.mult))
                if k == 13:
                    dv.wait_ge(*PE.at(l, "sumqk"))
                    rsqrt(l, bank[2][0:8, 0:T], rows[0:8, 2, :], (rows[0:8, 3, :], rows[0:8, 1, :]), 1.0, 4 * EPS, 8, None)
                    settle(l)
                    step(dv.tensor_scalar(rows[0:8, 2, :], rows[0:8, 2, :], c_("qscale", 1, slice(0, 8)), None, ALU.mult), "rqk")
                if k in (16, 17):
                    dv.wait_ge(*PE.at(l, ("rbc", k - 16)))
                    for i in range(2):
                        t = flat(tiles(4 * (k - 16) + 2 * i, 2))
                        step(dv.tensor_tensor(t, t, bank[(6, 4)[k - 16] + i][:, :], ALU.mult), "knorm")
                if k == 19:
                    dv.wait_ge(*PE.at(l, "kk"))
                    step(dv.tensor_tensor(mat(LM), b3(6, 8), mat(E2), ALU.mult), "lmat")
                    step(dv.tensor_tensor(attnT[:, :, :], b3(7, 8), mat(E1), ALU.mult))
                    step(dv.tensor_tensor(tiles(TQ, 4), tiles(TQ, 4), tiles(EG, 4), ALU.mult))
                if k == 21:
                    dv.wait_ge(*PE.at(l, "lt"))
                    step(dv.tensor_copy(mat(LT), b3(2, 8)))
                    step(dv.tensor_tensor(Tm[:, :, :], mat(LM), over(c_("low1", 64), 8), ALU.mult))
                    settle(l)
                    step(dv.tensor_tensor(Rm[:, :, :], mat(LT), over(c_("up1", 64), 8), ALU.mult))
                    step(dv.tensor_tensor(Tm[:, :, :], over(c_("eye", 64), 8), Tm[:, :, :], ALU.subtract))
                    settle(l)
                    step(dv.tensor_tensor(Rm[:, :, :], over(c_("eye", 64), 8), Rm[:, :, :], ALU.subtract))
                if k == 22:
                    dv.wait_ge(*PE.at(l, "vT"))
                    for i in range(2):
                        step(dv.tensor_tensor(Vb[:, 4 * i:4 * i + 4, :], b3(4 + i, 4), each(sm["mx"][:, 4 * i:4 * i + 4], HD), ALU.mult), "vb")
                    step(dv.tensor_tensor(mat(CM), mat(LT), over(c_("up2", 64), 8), ALU.mult), ("level", 0))
                if k == 23:
                    dv.wait_ge(*PE.at(l, "kT"))
                    for i in range(2):
                        step(dv.tensor_tensor(Kend[:, 4 * i:4 * i + 4, :], b3(6 + i, 4), each(sm["kes"][:, 4 * i:4 * i + 4], HD), ALU.mult), "kend")
                if 25 <= k <= 34:
                    i, part = divmod(k - 25, 2)
                    if part == 0:
                        dv.wait_ge(*PE.at(l, ("X", i)))
                        step(dv.tensor_copy(mat(XM), b3(2, 8)), ("xcopy", i))
                        if i < 4:
                            step(dv.tensor_tensor(mat(CM), mat(LT), over(c_(("up4", "up8", "up16", "up32")[i], 64), 8), ALU.mult))
                    else:
                        dv.wait_ge(*PE.at(l, ("TX", i)))
                        if i < 4:
                            step(dv.tensor_tensor(Tm[:, :, :], Tm[:, :, :], b3(6, 8), ALU.subtract))
                        step(dv.tensor_tensor(Rm[:, :, :], Rm[:, :, :], b3(7, 8), ALU.subtract), ("level", i + 1))
                        if i == 4:
                            DV.new[("w", 0)] = DV.n
                if k == 22:
                    r = tiles(TMQ, 8, slice(0, 32))
                    s = tiles(SQ, 8, slice(0, 32))
                    step(dv.stream_shuffle(s, r, [(i + 16) % 32 for i in range(32)]))
                    settle(l)
                    step(dv.tensor_tensor(r, r, over(c_("cos", 256, slice(0, 32)), 8), ALU.mult))
                if k == 23:
                    r = tiles(TMQ, 8, slice(0, 32))
                    s = tiles(SQ, 8, slice(0, 32))
                    step(dv.tensor_tensor(s, s, over(c_("sin", 256, slice(0, 32)), 8), ALU.mult))
                    settle(l)
                    step(dv.tensor_tensor(r, r, s, ALU.add), "rope")
                if k == 27:
                    dv.wait_ge(*PE.at(l, "scores"))
                    pr = flat(tiles(PR, 6))
                    p0 = pr[:, 0:512].rearrange("p (h k) -> p h k", h=4)
                    step(dv.tensor_tensor(p0, b3(5, 4), over(c_("causal", 128), 4), ALU.add))
                    for b in range(2):
                        p1 = pr[:, 512 + 512 * b:1024 + 512 * b].rearrange("p (h k) -> p h k", h=2)
                        s1 = bank[3 + b][:, :].rearrange("p (h k) -> p h k", h=2)
                        step(dv.tensor_copy(p1[:, :, 0:P], s1[:, :, 0:P]))
                        step(dv.tensor_tensor(p1[:, :, P:T], s1[:, :, P:T], over(c_("causal", 128), 2), ALU.add), "masked")
                    settle(l)
                    step(dv.tensor_reduce(sm["mx"][:, 0:4], p0, AX, ALU.max))
                    step(dv.tensor_reduce(sm["mx"][:, 4:8], pr[:, 512:1536].rearrange("p (h k) -> p h k", h=4), AX, ALU.max))
                    settle(l)
                    step(dv.tensor_scalar(sm["mx"], sm["mx"], -(HD ** -0.5), None, ALU.mult), "rowmax")
                if k == 29:
                    dv.wait_ge(*AC.at(l, "exp"))
                    step(dv.reciprocal(sm["rs"], sm["rs"]))
                    settle(l)
                    pr = flat(tiles(PR, 6))
                    p0 = pr[:, 0:512].rearrange("p (h k) -> p h k", h=4)
                    p1 = pr[:, 512:1536].rearrange("p (h k) -> p h k", h=4)
                    step(dv.tensor_tensor(p0, p0, each(sm["rs"][:, 0:4], P), ALU.mult))
                    step(dv.tensor_tensor(p1, p1, each(sm["rs"][:, 4:8], T), ALU.mult), "probs")
                if k == 31:
                    dv.wait_ge(*PE.at(l, "pT"))
                    for i in range(3):
                        step(dv.tensor_copy(flat(tiles(PT + 2 * i, 2)), bank[3 + i][:, :]), "pcopy")
                if k == 34:
                    dv.wait_ge(*AC.at(l, "mbhi"))
                    for i in range(2):
                        step(dv.tensor_tensor(flat(blo[:, 4 + 2 * i:6 + 2 * i, :]), bank[3 + i][:, :],
                                              flat(bhi[:, 4 + 2 * i:6 + 2 * i, :]), ALU.subtract), "mb_out")
                if k in (29, 30):
                    for t in (0, 1) if k == 29 else (2, 3):
                        conv(l, proj[:, TLX + t, :], proj[:, XC + t, :], OFF["conv"] + TAPS * (12 + t))
                        settle(l)
                        step(dv.tensor_scalar(proj[:, XC + t, :], proj[:, XC + t, :], p_("convb", t), None, ALU.add), "xc")
                if k == 38:
                    dv.wait_ge(*AC.at(l, "a0"))
                    settle(l)
                    step(dv.scalar_tensor_tensor(out=tiles(HSM, 4), in0=tiles(A0, 4), scalar=1.0,
                                                 in1=tiles(TR, 4), op0=ALU.add, op1=ALU.mult), "lru_m")
                    settle(l)
                    step(dv.tensor_scalar(tiles(A0, 4), tiles(HSM, 4), -1.0, 1.0, ALU.mult, ALU.add))
                    step(dv.scalar_tensor_tensor(out=tiles(TI, 4), in0=tiles(TI, 4), scalar=1.0, in1=tiles(XC, 4),
                                                 op0=ALU.add, op1=ALU.mult))
                if k == 41:
                    dv.wait_ge(*AC.at(l, "sqT"))
                    settle(l)
                    step(dv.scalar_tensor_tensor(out=tiles(HSM, 4), in0=tiles(A0, 4), scalar=1.0, in1=tiles(TR, 4),
                                                 op0=ALU.add, op1=ALU.mult))
                    settle(l)
                    step(dv.tensor_tensor(tiles(HSM, 4), tiles(HSM, 4), tiles(TI, 4), ALU.mult), "lru_uv")
                    settle(l)
                    for t in range(4):
                        step(dv.tensor_tensor_scan(proj[:, HS + t, :], proj[:, A0 + t, :], proj[:, HSM + t, :], 0.0, ALU.mult, ALU.add))
                if k == 44:
                    dv.wait_ge(*AC.at(l, "y2"))
                    step(dv.tensor_scalar(tiles(TI, 4), tiles(TI, 4), 0.044715, 1.0, ALU.mult, ALU.add))
                    settle(l)
                    step(dv.tensor_tensor(tiles(TI, 4), tiles(TI, 4), tiles(TLY, 4), ALU.mult), "gelu_in")
                if k == 46:
                    dv.wait_ge(*AC.at(l, "gelu_t"))
                    step(dv.scalar_tensor_tensor(out=tiles(TI, 4), in0=tiles(TI, 4), scalar=1.0, in1=tiles(TLY, 4),
                                                 op0=ALU.add, op1=ALU.mult))
                    settle(l)
                    step(dv.tensor_tensor(tiles(TI, 4), tiles(TI, 4), tiles(HS, 4), ALU.mult), "lru_f")
                if k == 48:
                    dv.wait_ge(*AC.at(l, "lruhi"))
                    step(dv.scalar_tensor_tensor(out=blo[:, 8:12, :], in0=tiles(TI, 4), scalar=0.25, in1=bhi[:, 8:12, :].bitcast(F32),
                                                 op0=ALU.mult, op1=ALU.subtract), "lru_out")
                if 37 <= k <= 45:
                    n, part = divmod(k - 34, 3)
                    if part == 1 and n:
                        m = n // 2
                        pa = (lower, upper)[n % 2]
                        dv.wait_ge(*PE.at(l, ("KS", n)))
                        for h in range(HEADS):
                            g = 2 * h + m
                            step(dv.scalar_tensor_tensor(out=Wb[pa, h, :], in0=b3(6, 4)[pa, h, :], scalar=sm["sneg"][pa, g:g + 1],
                                                         in1=Vb[pa, g, :], op0=ALU.mult, op1=ALU.add), ("w", n))
                    if part == 0:
                        dv.wait_ge(*PE.at(l, ("SU", n - 1)))
                        if n == 1:
                            step(dv.tensor_copy(Sst(1), b3(2, 4)), ("state", 1))
                        else:
                            for h in range(HEADS):
                                step(dv.scalar_tensor_tensor(out=Sst(n % 2)[:, h, :], in0=Sst((n - 1) % 2)[:, h, :],
                                                             scalar=sm["egl"][:, NCH * h + n - 1:NCH * h + n],
                                                             in1=b3(2, 4)[:, h, :], op0=ALU.mult, op1=ALU.add), ("state", n))
                if k == 37:
                    dv.wait_ge(*AC.at(l, "tz"))
                    step(dv.scalar_tensor_tensor(out=tiles(TZ, 4), in0=tiles(TMV, 4), scalar=1.0, in1=tiles(TZ, 4),
                                                 op0=ALU.add, op1=ALU.mult), "zsilu")
                if k == 48:
                    dv.wait_ge(*PE.at(l, "sumo"))
                    rsqrt(l, bank[2][0:8, 0:T], rows[0:8, 2, :], (rows[0:8, 3, :], rows[0:8, 1, :]), 1.0 / HD, EPS, 8, "ro")
                if k == 51:
                    dv.wait_ge(*PE.at(l, "robc"))
                    for i in range(2):
                        step(dv.tensor_tensor(flat(tiles(TZ + 2 * i, 2)), flat(tiles(TZ + 2 * i, 2)), bank[6 + i][:, :], ALU.mult))
                    settle(l)
                    for i in range(2):
                        step(dv.scalar_tensor_tensor(out=flat(tiles(TMQ + 2 * i, 2)), in0=flat(tiles(TZ + 2 * i, 2)), scalar=sm["nwh"],
                                                     in1=bank[3 + i][:, :], op0=ALU.mult, op1=ALU.mult), "dn_f")
                if k == 52:
                    dv.wait_ge(*AC.at(l, "dnhi"))
                    step(dv.tensor_tensor(blo[:, 0:4, :], tiles(TMQ, 4), bhi[:, 0:4, :], ALU.subtract), "dn_out")
                c = k // 2 - 1
                if k % 2 == 0 and 0 <= c < C_IN:
                    dv.wait_ge(*PE.at(l, ("bulk", k - 1)))
                    if c == 0:
                        settle(l)
                    step(dv.tensor_tensor(tiles(2 * c, 2), bank[c % 2][:, :].rearrange("p (a b) -> p a b", a=2),
                                          over(rstd[:, :], 2), ALU.mult), ("evac", c))
                c = k // 2 - 1 - C_IN
                if k % 2 == 0 and 0 <= c < C_Y:
                    hf, br = divmod(c, 3)
                    dv.wait_ge(*PE.at(l, ("bulk", k - 1)))
                    if c == 0:
                        dv.wait_ge(*AC.at(l, ("gates", 29)))
                    for i in range(2):
                        f = 4 * hf + 2 * i
                        g, mx = flat(tiles(TG + 8 * br + f, 2)), flat(tiles(MIX + f, 2))
                        dst = mx if br == 0 else g
                        step(dv.scalar_tensor_tensor(out=dst, in0=g, scalar=1.0, in1=bank[2 * (c % 2) + i][:, :],
                                                     op0=ALU.add, op1=ALU.mult), ("y", c))
                    if br:
                        settle(l)
                        for i in range(2):
                            f = 4 * hf + 2 * i
                            g, mx = flat(tiles(TG + 8 * br + f, 2)), flat(tiles(MIX + f, 2))
                            step(dv.tensor_tensor(mx, mx, g, ALU.add), ("mixf", 2 * hf + i))
                    if br == 2:
                        for i in range(2):
                            q = 2 * hf + i
                            dv.wait_ge(*AC.at(l, ("mixhi", q)))
                            step(dv.scalar_tensor_tensor(out=alo[:, 2 * q:2 * q + 2, :], in0=tiles(MIX + 2 * q, 2), scalar=0.5,
                                                         in1=ahi[:, 2 * q:2 * q + 2, :].bitcast(F32), op0=ALU.mult, op1=ALU.subtract),
                                 ("mixed", q))
                if k == 2 * FFN0:
                    x_add(l, "ffn", 2 * FFN0 - 1)
                    for p in range(4):
                        x_norm(l, "ffn", l * 2 + 1, p)
                if k == 2 * FFN0 + 1:
                    rnorm(l, "ffn")
                if k > 2 * FFN0 and k % 2 == 0:
                    kind, j = ffn_of(k // 2 - 1)
                    s = 8 * (j % 2)
                    if kind != "down":
                        dv.wait_ge(*PE.at(l, ("bulk", k - 1)))
                    if kind == "gate":
                        if j == 0:
                            settle(l)
                        step(dv.tensor_tensor(tiles(s, 2), bank[0][:, :].rearrange("p (a b) -> p a b", a=2),
                                              over(rstd[:, :], 2), ALU.mult), ("gate", j))
                    if kind == "up":
                        step(dv.tensor_tensor(tiles(s + 4, 2), bank[1][:, :].rearrange("p (a b) -> p a b", a=2),
                                              over(rstd[:, :], 2), ALU.mult), ("up", j))
                        dv.wait_ge(*AC.at(l, ("ftanh", j)))
                        step(dv.scalar_tensor_tensor(out=tiles(s + 2, 2), in0=tiles(s + 2, 2), scalar=1.0, in1=tiles(s, 2),
                                                     op0=ALU.add, op1=ALU.mult))
                        settle(l)
                        step(dv.tensor_tensor(tiles(s + 6, 2), tiles(s + 2, 2), tiles(s + 4, 2), ALU.mult), ("hidf", j))
                        dv.wait_ge(*AC.at(l, ("hidhi", j)))
                        step(dv.scalar_tensor_tensor(out=blo[:, 2 * (j % 2):2 * (j % 2) + 2, :], in0=tiles(s + 6, 2), scalar=0.5,
                                                     in1=bhi[:, 2 * (j % 2):2 * (j % 2) + 2, :].bitcast(F32),
                                                     op0=ALU.mult, op1=ALU.subtract), ("hidden", j))

            HSM = UU

            def tmq4(i):
                return proj[0:4, EG + 2 + i, :]

            for p in range(4):
                x_norm(None, "mix", 0, p)
            for m in range(AHEAD):
                lo(None, m)
            DV.first = dict(DV.new)
            dv.wait_ge(DV.sem, DV.n)
            dv.nop().then_inc(DV.sem, max(DV.per, 1))
            DV.n += max(DV.per, 1)
            DV.open_layer()
            with dv.Fori(0, L) as l:
                for k in range(NH):
                    if k + AHEAD < NH:
                        lo(l, k + AHEAD)
                    side(l, k)
                    if k + AHEAD >= NH and k + AHEAD + 1 - NH < AHEAD:
                        lo(l, k + AHEAD + 1 - NH, True)
                x_add(l, "mix", NH - 1)
                for p in range(4):
                    x_norm(l, "mix", l * 2 + 2, p)
                lo(l, 0, True)
            dv.wait_ge(PE.sem, PE_FINAL)
            DV.n_end = DV.n
            rsqrt(L - 1, bank[2][:, 0:T], rstd[:, :], (tmp[:, 0, 0:T], tmp[:, 0, T:2 * T]), 1.0 / D, EPS, P, None)
            settle(L - 1)
            for kt in range(KT):
                step(dv.scalar_tensor_tensor(out=x[:, kt, :], in0=x[:, kt, :], scalar=nrm[:, 2 * L * KT + kt:2 * L * KT + kt + 1],
                                             in1=rstd[:, :], op0=ALU.mult, op1=ALU.mult), "out")
            DV.marks_out = DV.n
            DV.n = DV.n_end
        return {s.name: s.learnt() for s in signals}


def _columns(w):
    return np.concatenate([w[:, :, 0:1536], w[:, :, 2056:4616], w[:, :, 1536:2048], w[:, :, 4616:]], axis=2)


def _constants():
    con = np.zeros((P, NCON), np.float32)

    def put(name, a):
        con[:a.shape[0], CON[name]:CON[name] + a.shape[1]] = a

    put("ident", np.eye(P, dtype=np.float32))
    q = np.arange(P)
    put("causal", np.where(q[None, :] <= q[:, None], 0.0, -1e30).astype(np.float32))
    put("ones", np.ones((P, P), np.float32))
    e = np.zeros((P, 8, 8), np.float32)
    for i in range(8):
        e[:, i, i] = 1.0
    put("ecol", e.reshape(P, 64))
    half = HD // 8
    inv = (np.float32(500000.0) ** (-np.arange(half, dtype=np.float32) / np.float32(half))).astype(np.float32)
    ang = (np.arange(T, dtype=np.float32)[None, :] * inv[:, None]).astype(np.float32)
    cos, sin = np.cos(ang).astype(np.float32), np.sin(ang).astype(np.float32)
    put("cos", np.concatenate([cos, cos], 0))
    put("sin", np.concatenate([-sin, sin], 0))
    put("reset", np.broadcast_to((np.arange(T) % CHUNK != 0).astype(np.float32), (P, T)))
    put("qscale", np.array([[HD ** -0.5]] * 4 + [[1.0]] * 4, np.float32))
    i = np.arange(P)[:, None] % CHUNK
    j = np.arange(CHUNK)[None, :]
    put("eye", (i == j).astype(np.float32))
    put("upin", (j >= i).astype(np.float32))
    put("low", (j < i).astype(np.float32))

    def level(r, c, s):
        return ((r // (2 * s) == c // (2 * s)) & (r % (2 * s) >= s) & (c % (2 * s) < s)).astype(np.float32)

    put("low1", level(i, j, 1))
    for s in (1, 2, 4, 8, 16, 32):
        put(f"up{s}", level(j, i, s))
    return con


def kernel(x, norm_mix, w_in, b_gate, dn_conv, dn_a_log, dn_dt_bias, dn_norm, dn_out, mb_out,
           lru_conv_w, lru_conv_b, lru_w_r, lru_b_r, lru_w_i, lru_b_i, lru_lambda, lru_out,
           w_o, norm_ffn, ffn_in, ffn_down, norm_final):
    import concourse.bacc as bacc
    from concourse.bass_utils import run_bass_kernel_spmd

    A = np.asarray
    win = A(w_in)
    stream = np.zeros((L * CH + 3, P, 2 * HALF), np.float32)
    wi = _columns(win).reshape(L, KT, P, C_IN, 256).transpose(0, 3, 2, 1, 4).reshape(L, C_IN, P, 2 * HALF)
    ys = np.stack([A(dn_out), A(mb_out), A(lru_out)], 1).reshape(L, 3, 4, P, 2, 512)
    ys = ys.transpose(0, 4, 1, 3, 2, 5).reshape(L, C_Y, P, 2 * HALF)
    wo = A(w_o).reshape(L, C_WO, 2, P, D).transpose(0, 1, 3, 2, 4).reshape(L, C_WO, P, 2 * HALF)
    fi = A(ffn_in).reshape(L, KT, P, 2, PAIRS, 256).transpose(0, 3, 4, 2, 1, 5).reshape(L, 2, PAIRS, P, 2 * HALF)
    fd = A(ffn_down).reshape(L, PAIRS, 2, P, D).transpose(0, 1, 3, 2, 4).reshape(L, PAIRS, P, 2 * HALF)
    for l in range(L):
        s = stream[l * CH:(l + 1) * CH]
        s[0:C_IN] = wi[l]
        s[C_IN:C_IN + C_Y] = ys[l]
        s[C_IN + C_Y:FFN0] = wo[l]
        s[FFN0], s[FFN0 + 1] = fi[l, 0, 0], fi[l, 1, 0]
        for j in range(1, PAIRS):
            s[FFN0 + 3 * j - 1], s[FFN0 + 3 * j], s[FFN0 + 3 * j + 1] = fi[l, 0, j], fi[l, 1, j], fd[l, j - 1]
        s[CH - 1] = fd[l, PAIRS - 1]

    par = np.zeros((L, P, NPAR), np.float32)

    def put(name, a):
        par[:, :a.shape[1], OFF[name]:OFF[name] + a.shape[2]] = a

    def tiled(a, n):
        return A(a).reshape(L, n, P).transpose(0, 2, 1)

    put("wab", win[:, :, 2048:2056].reshape(L, KT, P, 8).transpose(0, 2, 1, 3).reshape(L, P, 64))
    cw = np.concatenate([A(dn_conv), A(lru_conv_w)], 2).reshape(L, TAPS, 16, P)
    put("conv", cw.transpose(0, 3, 2, 1).reshape(L, P, 64))
    put("convb", tiled(lru_conv_b, 4))
    put("br", tiled(lru_b_r, 4))
    put("bi", tiled(lru_b_i, 4))
    put("lam", tiled(lru_lambda, 4))
    put("dnorm", A(dn_norm).reshape(L, P, 1))
    put("bg", tiled(b_gate, 24))
    put("alog", A(dn_a_log).reshape(L, 4, 1))
    put("dtb", A(dn_dt_bias).reshape(L, 4, 1))
    for name, w in (("wr", A(lru_w_r)), ("wi", A(lru_w_i))):
        w = w.reshape(L, 4, 2, 64, 64)
        for t in range(4):
            for g in range(2):
                par[:, 64 * g:64 * g + 64, OFF[name] + P * t + 64 * g:OFF[name] + P * t + 64 * g + 64] = w[:, t, g]
    nm, nf = tiled(norm_mix, KT), tiled(norm_ffn, KT)
    nl = A(norm_final).reshape(KT, P).T
    norms = np.concatenate([w[l] for l in range(L) for w in (nm, nf)] + [nl], 1)
    xT = A(x).reshape(T, KT, P).transpose(2, 1, 0)

    arrays = {"stream_dram": stream, "params_dram": par, "consts_dram": _constants(),
              "norms_dram": np.ascontiguousarray(norms), "x_dram": np.ascontiguousarray(xT)}
    known = {}
    for _ in range(3):
        nc = bacc.Bacc("TRN2", target_bir_lowering=False, num_devices=1)
        args = [nc.dram_tensor(n, a.shape, mybir.dt.from_np(a.dtype), kind="ExternalInput").ap() for n, a in arrays.items()]
        o = nc.dram_tensor("out_dram", (P, KT, T), F32, kind="ExternalOutput").ap()
        known = build(nc, *args, o, known)
    r = run_bass_kernel_spmd(nc, [arrays], core_ids=[0])
    y = np.asarray(r.results[0]["out_dram"])
    return np.ascontiguousarray(y.transpose(2, 1, 0)).reshape(1, T, D)
```

```python
from contextlib import ExitStack

import numpy as np
import concourse.bass as bass
from concourse import mybir

F32 = mybir.dt.float32
F32R = mybir.dt.float32r
I32 = mybir.dt.int32
ALU = mybir.AluOpType
ACT = mybir.ActivationFunctionType
AX = mybir.AxisListType.X

P = 128
D = 1024
T = 256
L = 2
HEADS = 4
HD = 128
CHUNK = 64
NCH = T // CHUNK
TAPS = 4
EPS = 1e-6
FFN = 2816
KT = D // P
HALF = 1024

C_IN = 30
C_Y = 6
C_WO = 4
PAIRS = FFN // 256
C_FFN = 3 * PAIRS
CH = C_IN + C_Y + C_WO + C_FFN
NH = 2 * CH
FFN0 = C_IN + C_Y + C_WO
RING = 5
AHEAD = RING - 1

TQ, TK, TV, TMQ, TMK, TMV, TLX, TLY, TZ, TG = 0, 4, 8, 12, 16, 20, 24, 28, 32, 36
NT = 60

OFF = {}


def _place(names):
    at = 0
    for name, n in names:
        OFF[name] = at
        at += n
    return at


NPAR = _place([("wab", KT * 8), ("conv", 16 * TAPS), ("convb", 4), ("br", 4), ("bi", 4), ("lam", 4),
               ("dnorm", 1), ("bg", 24), ("alog", 4), ("dtb", 4), ("wr", 512), ("wi", 512)])
CON = {}
_at = 0
for _n, _k in [("ident", 128), ("causal", 128), ("ones", 128), ("cos", 256), ("sin", 256),
               ("tri", 128), ("eye", 64), ("upin", 64), ("low", 64), ("low1", 64),
               ("up1", 64), ("up2", 64), ("up4", 64), ("up8", 64), ("up16", 64), ("up32", 64)]:
    CON[_n] = _at
    _at += _k
NCON = _at


class Signal:

    def __init__(self, sem, name, known):
        self.sem, self.name = sem, name
        self.base, self.per, self.marks = known.get(name, (0, 0, {}))
        self.n, self.new, self.start = 0, {}, 0
        self.layer = None

    def up(self, step=None):
        self.n += 1
        if step is not None:
            self.new[step] = self.n
        return self.sem, 1

    def open_layer(self):
        self.start, self.n = self.n, 0
        self.pre, self.new = self.new, {}

    def at(self, l, step, prev=False):
        n = self.base + self.marks.get(step, 1)
        if prev:
            return self.sem, l * self.per + (n - self.per)
        return self.sem, l * self.per + n

    def last(self, l):
        return self.sem, (l * self.per + self.base if l is not None else 0) + self.n

    def learnt(self):
        return (self.start, self.n, self.new)


def build(nc, wstream, params, consts, norms, x_in, out, known):
    ctx = ExitStack()
    with ctx:
        def sb(name, shape, dt=F32):
            return ctx.enter_context(nc.sbuf_tensor(name, shape, dt))

        def sem(name):
            return ctx.enter_context(nc.semaphore(name))

        raw = sb("raw", [P, RING, HALF])
        whi = sb("whi", [P, RING, HALF], F32R)
        wlo = sb("wlo", [P, RING, HALF], F32R)
        x = sb("x", [P, KT, T])
        ahi = sb("ahi", [P, KT, T], F32R)
        alo = sb("alo", [P, KT, T], F32R)
        proj = sb("proj", [P, NT, T])
        bhi = sb("bhi", [P, 12, T], F32R)
        blo = sb("blo", [P, 12, T], F32R)
        con = sb("con", [P, NCON])
        par = sb("par", [P, NPAR])
        nrm = sb("nrm", [P, (2 * L + 1) * KT])
        rstd = sb("rstd", [P, T])
        tmp = sb("tmp", [P, 2, 2 * T])
        tmq = sb("tmq", [P, 2 * T])
        Tm = sb("Tm", [P, 8, CHUNK])
        Rm = sb("Rm", [P, 8, CHUNK])
        attnT = sb("attnT", [P, 8, CHUNK])
        Vb = sb("Vb", [P, 8, HD])
        Kend = sb("Kend", [P, 8, HD])
        small = sb("small", [P, 300])
        wabh = sb("wabh", [P, KT * 8], F32R)
        wabl = sb("wabl", [P, KT * 8], F32R)
        bank = [ctx.enter_context(nc.psum_tensor(f"bank{i}", [P, 512], F32)) for i in range(8)]

        loaded_raw = [sem(f"loaded_raw{i}") for i in range(RING)]
        loaded_con, loaded_nrm, loaded_x, loaded_par = (sem(n) for n in ("loaded_con", "loaded_nrm", "loaded_x", "loaded_par"))
        loaded_last = sem("loaded_last")
        stored = sem("stored")
        PE = Signal(sem("tensor_done"), "pe", known)
        DV = Signal(sem("vector_done"), "dv", known)
        AC = Signal(sem("scalar_done"), "ac", known)
        signals = (PE, DV, AC)

        block = ctx.enter_context(nc.Block())

        def c_(name, n=None, p=slice(0, P)):
            return con[p, CON[name]:CON[name] + n]

        def p_(name, i=0, n=1, p=slice(0, P)):
            return par[p, OFF[name] + i:OFF[name] + i + n]

        sm = {}
        at = 0
        for name, n in [("gcol", 8), ("bcol", 8), ("sneg", 8), ("kes", 8), ("egl", 16), ("mx", 8), ("rs", 8),
                        ("brh", 4), ("bih", 4), ("bgh", 24), ("sp2", 4), ("sp4n", 4), ("nwh", 1), ("anex", 4),
                        ("v", 12), ("vabs", 12), ("e", 12), ("s", 12), ("s2", 12), ("acc", 12),
                        ("g", 8), ("nr", 2), ("rqk", 16), ("ro", 8), ("n0", 16), ("n1", 16)]:
            sm[name] = small[:, at:at + n]
            at += n
        assert at <= 300

        def tiles(t, n, p=slice(0, P)):
            return proj[p, t:t + n, :]

        def flat(ap):
            return ap.rearrange("p a b -> p (a b)")

        def mat(t):
            return flat(tiles(t, 2)).rearrange("p (g c) -> p g c", g=8)

        def over(ap, n):
            return ap.unsqueeze(1).broadcast_to([ap.shape[0], n, ap.shape[1]])

        def each(ap, n):
            return ap.unsqueeze(2).broadcast_to([ap.shape[0], ap.shape[1], n])

        SQ, EG, E1, E2, LM, LT = 48, 44, 36, 38, 40, 42
        CM, XM = 8, 10
        PR, PT, VTOK = 48, 54, 44
        S0, WB, VN = 8, 16, 18
        XC, TR, TI, A0, UU, HS = 12, 52, 48, 24, 20, 52
        MIX = 0
        lower, upper = slice(0, 64), slice(64, 128)
        halves = ((0, lower), (1, upper))

        def Sst(i):
            return flat(tiles(S0 + 2 * i, 2)).rearrange("p (h e) -> p h e", h=HEADS)

        Wb = flat(tiles(WB, 2)).rearrange("p (h e) -> p h e", h=HEADS)
        vnb = flat(tiles(VN, 2)).rearrange("p (h e) -> p h e", h=HEADS)

        def b3(i, g):
            return bank[i][:, :].rearrange("p (g c) -> p g c", g=g)

        def ffn_of(c):
            i = c - FFN0
            if i < 2:
                return ("gate", "up")[i], 0
            if i == C_FFN - 1:
                return "down", PAIRS - 1
            j, r = divmod(i - 2, 3)
            return (("gate", j + 1), ("up", j + 1), ("down", j))[r]

        uses = (NH - 1) // RING
        assert NH - 1 == uses * RING
        LAST = NH - 1
        XRAW, XSPLIT = 56, 4

        def raw_of(m):
            return flat(tiles(XRAW, 4)) if m == LAST else raw[:, m % RING, :]

        def whi_of(m):
            return flat(bhi[:, XSPLIT:XSPLIT + 4, :]) if m == LAST else whi[:, m % RING, :]

        def wlo_of(m):
            return flat(blo[:, XSPLIT:XSPLIT + 4, :]) if m == LAST else wlo[:, m % RING, :]

        def landed(l, m, nxt=False):
            if m == LAST:
                return loaded_last, 16 * (l + 1)
            return loaded_raw[m % RING], 16 * (l * uses + m // RING + 1 + (uses if nxt else 0))

        def last_user(m):
            return LAST - RING + m

        @block.sync
        def _(sp):
            def load(g, m):
                sp.dma_start(raw_of(m), wstream[g, :, (m % 2) * HALF:(m % 2 + 1) * HALF]).then_inc(
                    loaded_last if m == LAST else loaded_raw[m % RING], 16)

            sp.dma_start(x[:, :, :], x_in).then_inc(loaded_x, 16)
            sp.dma_start(nrm[:, :], norms).then_inc(loaded_nrm, 16)
            for m in range(2):
                load(m // 2, m)
            sp.dma_start(con[:, :], consts).then_inc(loaded_con, 16)
            for m in range(2, RING):
                load(m // 2, m)
            with sp.Fori(0, L) as l:
                used = [AC.at(l, ("gates", 29), prev=True), DV.at(l, ("mixed", 3), prev=True)]
                used = [(s, sp.snap(v)) for s, v in used]
                for s, v in used:
                    sp.wait_ge(s, v)
                sp.dma_start(par[:, :], params[l]).then_inc(loaded_par, 16)
                for k in range(NH):
                    m = k + RING
                    chunk = sp.snap(l * CH + (m // 2 if m < NH else CH + (m - NH) // 2))
                    if k < AHEAD:
                        sp.wait_ge(*DV.at(l, ("lo_next", k), prev=True))
                    else:
                        sp.wait_ge(*DV.at(l, ("lo", k if m < NH else k - 1)))
                    load(chunk, m if m < NH else m - NH)
            for i in range(2):
                sp.wait_ge(*DV.at(L - 1, ("out", i)))
                sp.dma_start(out[:, 4 * i:4 * i + 4, :], x[:, 4 * i:4 * i + 4, :]).then_inc(stored, 16)
            sp.wait_ge(stored, 32)
            for m in range(RING):
                sp.wait_ge(*landed(L, m))

        @block.tensor
        def _(pe):
            def products(dst, wcol, m, hi, lo, first, last):
                pe.matmul(dst, whi_of(m)[:, wcol], hi, start=first, stop=False, skip_group_check=True)
                pe.matmul(dst, whi_of(m)[:, wcol], lo, start=False, stop=False, skip_group_check=True)
                return pe.matmul(dst, wlo_of(m)[:, wcol], hi, start=False, stop=last, skip_group_check=True)

            def wait_split(l, k):
                if k < AHEAD:
                    pe.wait_ge(*DV.at(l, ("lo_next", k), prev=True))
                else:
                    pe.wait_ge(*DV.at(l, ("lo", k)))

            def cols(j):
                return slice(j * P, (j + 1) * P)

            def by_output(l, k, dst, start_kt, act_wait=None):
                for i in range(4):
                    kt = start_kt + i
                    if act_wait is not None:
                        act_wait(kt)
                    if i == 3:
                        early_waits(l, k)
                    for n in range(2):
                        ins = products(dst[:, n * T:(n + 1) * T], cols(2 * i + n), k,
                                       ahi[:, kt, :], alo[:, kt, :], kt == 0 and n == 0, kt == KT - 1)
                ins.then_inc(*PE.up(("bulk", k)))

            def y_half(k, base):
                c = k // 2 - C_IN
                br = c % 3
                for i in range(2):
                    kt = (k % 2) * 2 + i
                    for n in range(4):
                        ins = products(bank[base + n // 2][:, (n % 2) * T:(n % 2 + 1) * T], cols(4 * i + n), k,
                                       bhi[:, 4 * br + kt, :], blo[:, 4 * br + kt, :],
                                       kt == 0 and n % 2 == 0, kt == 3)
                ins.then_inc(*PE.up(("bulk", k)))

            def by_contraction(k, hi, lo, first, last):
                for n in range(8):
                    ins = products(bank[4 + n // 2][:, (n % 2) * T:(n % 2 + 1) * T], cols(n), k, hi, lo,
                                   first and n % 2 == 0, last)
                    if last and n % 2:
                        ins.then_inc(*PE.up(("acc", k, n // 2)))
                if not last:
                    ins.then_inc(*PE.up(("bulk", k)))
                else:
                    PE.new[("bulk", k)] = PE.n

            def early_waits(l, k):
                if k == 18:
                    pe.wait_ge(*DV.at(l, "knorm"))
                if k == 20:
                    pe.wait_ge(*DV.at(l, "lmat"))
                if 24 <= k <= 33:
                    i, part = divmod(k - 24, 2)
                    pe.wait_ge(*DV.at(l, ("xcopy", i) if part else ("level", i)))
                if 34 < k <= 45 and (k - 34) % 3 == 1:
                    pe.wait_ge(*DV.at(l, ("w", (k - 34) // 3)))

            def exact(dst, lhsT, rhs, start=True, stop=True):
                return pe.matmul(dst, lhsT, rhs, start=start, stop=stop, skip_group_check=True)

            def norm_sum(l, step):
                pe.wait_ge(*AC.at(l, (step, "sq", 3), prev=(step == "mix")))
                for m in range(2):
                    for kt in range(KT):
                        ins = exact(bank[2][:, m:m + 1], proj[:, SQ + kt, m * P:(m + 1) * P], c_("ones", 1), kt == 0, kt == KT - 1)
                ins.then_inc(*PE.up((step, "sum")))

            def spread(dst, col, m):
                return exact(dst[:, m * P:(m + 1) * P], col.broadcast_to([P, P]), c_("ident", P))

            def norm_spread(l, step):
                pe.wait_ge(*DV.at(l, (step, "nr")))
                for m in range(2):
                    ins = spread(bank[2], sm["nr"][:, m:m + 1], m)
                ins.then_inc(*PE.up((step, "spread")))

            def side(l, k):
                if k == 0:
                    norm_sum(l, "mix")
                if k == 1:
                    pe.wait_ge(*DV.at(l, "wab"))
                    for m in range(2):
                        for kt in range(KT):
                            w = slice(kt * 8, kt * 8 + 8)
                            ts = slice(m * P, (m + 1) * P)
                            dst = bank[3][:, 8 * m:8 * m + 8]
                            pe.matmul(dst, ahi[:, kt, ts], wabh[:, w], start=kt == 0, stop=False, skip_group_check=True)
                            pe.matmul(dst, alo[:, kt, ts], wabh[:, w], start=False, stop=False, skip_group_check=True)
                            ins = pe.matmul(dst, ahi[:, kt, ts], wabl[:, w], start=False, stop=kt == KT - 1, skip_group_check=True)
                    ins.then_inc(*PE.up("ab"))
                    norm_spread(l, "mix")
                if k == 9:
                    pe.wait_ge(*DV.at(l, "grow"))
                    exact(bank[3][:, 0:8], c_("tri", P), sm["g"])
                    for h in range(HEADS):
                        for m in range(2):
                            ins = exact(bank[4 + h // 2][:, (h % 2) * T + m * P:(h % 2) * T + (m + 1) * P],
                                        sm["g"][:, 2 * h + m:2 * h + m + 1].broadcast_to([P, P]), c_("tri", P))
                    ins.then_inc(*PE.up("gbc"))
                if k == 12:
                    pe.wait_ge(*AC.at(l, ("sq", 3)))
                    for t in range(8):
                        for m in range(2):
                            ins = exact(bank[2][:, 2 * t + m:2 * t + m + 1], proj[:, SQ + t, m * P:(m + 1) * P], c_("ones", 1))
                    ins.then_inc(*PE.up("sumqk"))
                if k in (15, 16):
                    pe.wait_ge(*DV.at(l, "rqk"))
                    if k == 16:
                        pe.wait_ge(*AC.at(l, "eg"))
                    for h in range(HEADS):
                        t = 4 * (k - 15) + h
                        for m in range(2):
                            ins = spread(bank[(6, 4)[k - 15] + h // 2][:, (h % 2) * T:(h % 2 + 1) * T], sm["rqk"][:, 2 * t + m:2 * t + m + 1], m)
                    ins.then_inc(*PE.up(("rbc", k - 15)))
                if k == 18:
                    for b, q0 in ((6, TK), (7, TQ)):
                        for h in range(HEADS):
                            for n in range(NCH):
                                m, a = divmod(n, 2)
                                cs = slice(n * CHUNK, (n + 1) * CHUNK)
                                ins = exact(b3(b, 8)[64 * a:64 * a + 64, 2 * h + m, :], proj[:, TK + h, cs], proj[:, q0 + h, cs])
                    ins.then_inc(*PE.up("kk"))
                if k == 20:
                    for g in range(8):
                        for a, pa in halves:
                            ins = exact(b3(2, 8)[pa, g, :], mat(LM)[pa, g, :], c_("eye", 64, pa))
                    ins.then_inc(*PE.up("lt"))
                if k == 21:
                    pe.wait_ge(*DV.at(l, ("silu", 5)))
                    for g in range(8):
                        h, m = divmod(g, 2)
                        ins = pe.transpose(b3(4 + g // 4, 4)[:, g % 4, :], proj[:, TV + h, m * P:(m + 1) * P], c_("ident", 128))
                    ins.then_inc(*PE.up("vT"))
                if k == 22:
                    for g in range(8):
                        h, m = divmod(g, 2)
                        ins = pe.transpose(b3(6 + g // 4, 4)[:, g % 4, :], proj[:, TK + h, m * P:(m + 1) * P], c_("ident", 128))
                    ins.then_inc(*PE.up("kT"))
                if 24 <= k <= 33:
                    i, part = divmod(k - 24, 2)
                    if part == 0:
                        for g in range(8):
                            for a, pa in halves:
                                ins = exact(b3(2, 8)[pa, g, :], mat(CM)[pa, g, :], Tm[pa, g, :])
                        ins.then_inc(*PE.up(("X", i)))
                    else:
                        for b, lt, rt in ((6, Rm, mat(XM)), (7, mat(XM), Rm)):
                            if i == 4 and b == 6:
                                continue
                            for g in range(8):
                                for a, pa in halves:
                                    ins = exact(b3(b, 8)[pa, g, :], lt[pa, g, :], rt[pa, g, :])
                        ins.then_inc(*PE.up(("TX", i)))
                if k == 26:
                    pe.wait_ge(*DV.at(l, "rope"))
                    pe.wait_ge(*DV.at(l, "vb"))
                    for h in range(HEADS):
                        exact(b3(5, 4)[:, h, :], proj[:, TMQ + h, 0:P], proj[:, TMK + h, 0:P])
                        ins = exact(bank[3 + h // 2][:, (h % 2) * T:(h % 2 + 1) * T], proj[:, TMQ + h, P:T], proj[:, TMK + h, :])
                    ins.then_inc(*PE.up("scores"))
                if k == 28:
                    pe.wait_ge(*DV.at(l, "masked"))
                    for g in range(8):
                        h, m = divmod(g, 2)
                        ins = pe.transpose(b3(3 + g // 4, 4)[:, g % 4, :], proj[:, TMV + h, m * P:(m + 1) * P], c_("ident", 128))
                    ins.then_inc(*PE.up("mvT"))
                if k == 30:
                    pe.wait_ge(*DV.at(l, "probs"))
                    pe.wait_ge(*AC.at(l, "vtok"))
                    pr = flat(tiles(PR, 6))
                    for g in range(12):
                        ins = pe.transpose(b3(3 + g // 4, 4)[:, g % 4, :], pr[:, g * P:(g + 1) * P], c_("ident", 128))
                    ins.then_inc(*PE.up("pT"))
                if k == 32:
                    pe.wait_ge(*DV.at(l, "pcopy"))
                    vt = flat(tiles(VTOK, 4)).rearrange("p (g d) -> p g d", g=8)
                    pt = flat(tiles(PT, 6)).rearrange("p (g q) -> p g q", g=12)
                    for h in range(HEADS):
                        d0 = bank[3 + h // 2][:, (h % 2) * T:(h % 2) * T + P]
                        d1 = bank[3 + h // 2][:, (h % 2) * T + P:(h % 2 + 1) * T]
                        exact(d0, vt[:, 2 * h, :], pt[:, h, :])
                        exact(d1, vt[:, 2 * h, :], pt[:, 4 + 2 * h, :], True, False)
                        ins = exact(d1, vt[:, 2 * h + 1, :], pt[:, 5 + 2 * h, :], False, True)
                    ins.then_inc(*PE.up("pv"))
                if k in (33, 34):
                    pe.wait_ge(*DV.at(l, "xc"))
                    if k == 34:
                        pe.wait_ge(*DV.at(l, "mb_out"))
                    else:
                        pe.wait_ge(*DV.at(l, ("xcopy", 4)))
                    w, bs = (("wi", (5, 2)), ("wr", (3, 4)))[k - 33]
                    for t in range(4):
                        ins = exact(bank[bs[t // 2]][:, (t % 2) * T:(t % 2 + 1) * T], p_(w, t * P, P), proj[:, XC + t, :])
                    ins.then_inc(*PE.up(w))
                if 34 < k <= 45:
                    n, part = divmod(k - 34, 3)
                    m, a = divmod(n, 2)
                    pa = (lower, upper)[a]
                    cs = slice(n * CHUNK, (n + 1) * CHUNK)
                    if part == 0:
                        pe.wait_ge(*DV.at(l, ("state", n)))
                        for h in range(HEADS):
                            ins = exact(b3(6, 4)[pa, h, :], proj[:, TK + h, cs], Sst(n % 2)[:, h, :])
                        ins.then_inc(*PE.up(("KS", n)))
                    if part == 1:
                        for h in range(HEADS):
                            ins = exact(b3(7, 4)[pa, h, :], Rm[pa, 2 * h + m, :], (Vb[pa, m:8:2, :] if n == 0 else Wb[pa, :, :])[:, h, :])
                        ins.then_inc(*PE.up(("VN", n)))
                    if part == 2:
                        pe.wait_ge(*AC.at(l, ("vn", n)))
                        if n == 0:
                            pe.wait_ge(*AC.at(l, "tanh_r"))
                        for h in range(HEADS):
                            o = bank[3 + h // 2][:, (h % 2) * T + n * CHUNK:(h % 2) * T + (n + 1) * CHUNK]
                            if n:
                                exact(o, Sst(n % 2)[:, h, :], proj[:, TQ + h, cs], True, False)
                            ins = exact(o, vnb[pa, h, :], attnT[pa, 2 * h + m, :], n == 0, True)
                            if n < NCH - 1:
                                ins = exact(b3(2, 4)[:, h, :], Kend[pa, 2 * h + m, :], vnb[pa, h, :])
                        ins.then_inc(*PE.up(("SU", n)))
                if k == 47:
                    pe.wait_ge(*AC.at(l, "osq"))
                    for t in range(4):
                        for m in range(2):
                            ins = exact(bank[2][:, 2 * t + m:2 * t + m + 1], proj[:, WB + t, m * P:(m + 1) * P], c_("ones", 1))
                    ins.then_inc(*PE.up("sumo"))
                if k == 50:
                    pe.wait_ge(*DV.at(l, "ro"))
                    for h in range(HEADS):
                        for m in range(2):
                            ins = spread(bank[6 + h // 2][:, (h % 2) * T:(h % 2 + 1) * T], sm["ro"][:, 2 * h + m:2 * h + m + 1], m)
                    ins.then_inc(*PE.up("robc"))

            pe.wait_ge(loaded_con, 16)
            pe.nop().then_inc(PE.sem, max(PE.per, 1))
            PE.n = max(PE.per, 1)
            PE.open_layer()
            with pe.Fori(0, L) as l:
                for k in range(NH):
                    c, half = divmod(k, 2)
                    wait_split(l, k)
                    if c < C_IN:
                        if c >= 2 and half == 0:
                            pe.wait_ge(*DV.at(l, ("evac", c - 2)))
                        aw = None
                        if c == 0:
                            aw = lambda kt: pe.wait_ge(*DV.at(l, ("mix", "lo", kt // 2), prev=True)) if kt % 2 == 0 else None
                        by_output(l, k, bank[c % 2], 4 * half, aw)
                        side(l, k)
                    elif c < C_IN + C_Y:
                        i = c - C_IN
                        if half == 0:
                            if i == 0:
                                pe.wait_ge(*DV.at(l, ("evac", 29)))
                                pe.wait_ge(*DV.at(l, "dn_out"))
                            if i == 2:
                                pe.wait_ge(*DV.at(l, "lru_out"))
                            if i >= 2:
                                pe.wait_ge(*DV.at(l, ("y", i - 2)))
                        y_half(k, 2 * (i % 2))
                    elif c < FFN0:
                        i = k - 2 * (C_IN + C_Y)
                        if i == 0:
                            pe.wait_ge(*DV.at(l, ("mixed", 1)))
                        if i == 4:
                            pe.wait_ge(*DV.at(l, ("mixed", 3)))
                        by_contraction(k, ahi[:, i, :], alo[:, i, :], i == 0, i == KT - 1)
                    else:
                        kind, j = ffn_of(c)
                        if kind == "down":
                            if half == 0:
                                pe.wait_ge(*DV.at(l, ("hidden", j)))
                            t = 2 * (j % 2) + half
                            by_contraction(k, bhi[:, t, :], blo[:, t, :], j == 0 and half == 0, j == PAIRS - 1 and half == 1)
                        else:
                            if half == 0 and j > 0:
                                pe.wait_ge(*DV.at(l, (kind, j - 1)))
                            aw = None
                            if kind == "gate" and j == 0:
                                aw = lambda kt: pe.wait_ge(*DV.at(l, ("ffn", "lo", kt // 2))) if kt % 2 == 0 else None
                            by_output(l, k, bank[kind == "up"], 4 * half, aw)
                            if kind == "gate" and j == 0 and half == 0:
                                norm_sum(l, "ffn")
                            if kind == "gate" and j == 0 and half == 1:
                                norm_spread(l, "ffn")
            PE.layer = L
            pe.wait_ge(*AC.at(L, ("mix", "sq", 3), prev=True))
            for m in range(2):
                for kt in range(KT):
                    ins = exact(bank[2][:, m:m + 1], proj[:, SQ + kt, m * P:(m + 1) * P], c_("ones", 1), kt == 0, kt == KT - 1)
            ins.then_inc(PE.sem, 1)
            pe.wait_ge(*DV.at(L - 1, "last_nr"))
            for m in range(2):
                ins = spread(bank[2], sm["nr"][:, m:m + 1], m)
            ins.then_inc(PE.sem, 1)
        PE_FINAL = PE.base + L * PE.per + 1

        @block.scalar
        def _(act):
            def hi(l, m, nxt=False):
                act.wait_ge(*landed(l, m, nxt))
                if l is not None and m >= RING:
                    act.wait_ge(*PE.at(l, ("bulk", m - RING)))
                elif l is not None and nxt:
                    act.wait_ge(*PE.at(l, ("bulk", last_user(m))))
                elif l is not None:
                    act.wait_ge(*PE.at(l, ("bulk", last_user(m)), prev=True))
                act.copy(whi_of(m), raw_of(m)).then_inc(*AC.up(("hi_next" if nxt or l is None else "hi", m)))

            def x_norm(l, step, nidx, bulk):
                for p in range(4):
                    if l is None:
                        if p == 0:
                            act.wait_ge(loaded_x, 16)
                            act.wait_ge(loaded_nrm, 16)
                    else:
                        act.wait_ge(*DV.at(l, (step, "x", p)))
                    for i in range(2):
                        act.activation(ahi[:, 2 * p + i, :], x[:, 2 * p + i, :], ACT.Copy,
                                       scale=nrm[:, bass.ds(nidx * KT + 2 * p + i, 1)]).then_inc(*AC.up())
                    AC.new[(step, "hi", p)] = AC.n
                if l is not None:
                    act.wait_ge(*DV.at(l, (step, "x", 3)))
                for p in range(4):
                    act.activation(tiles(SQ + 2 * p, 2), x[:, 2 * p:2 * p + 2, :], ACT.Square).then_inc(*AC.up((step, "sq", p)))

            def side(l, k):
                if k == 0:
                    act.wait_ge(loaded_par, l * 16 + 16)
                    act.copy(wabh[:, :], p_("wab", 0, 64)).then_inc(*AC.up("wabh"))
                    act.activation(sm["anex"], p_("alog", 0, 4), ACT.Exp).then_inc(*AC.up("anex"))
                if k == 5:
                    act.wait_ge(*DV.at(l, "aabs"))
                    act.activation(sm["e"], sm["vabs"], ACT.Exp, scale=-1.0).then_inc(*AC.up())
                    act.activation(sm["bcol"], sm["bcol"], ACT.Tanh, scale=0.5).then_inc(*AC.up("aexp"))
                if 3 <= k <= 14:
                    c, odd = divmod(k - 3, 2)
                    if not odd:
                        act.wait_ge(*DV.at(l, ("conv", c)))
                        act.activation(tmq[:, :], tmp[:, c % 2, :], ACT.Tanh, scale=0.5).then_inc(*AC.up(("tanh", c)))
                    elif c < 4:
                        act.wait_ge(*DV.at(l, ("silu", c)))
                        act.activation(tiles(SQ + 2 * c, 2), tiles(2 * c, 2), ACT.Square).then_inc(*AC.up(("sq", c)))
                if k == 10:
                    act.wait_ge(*DV.at(l, "dif"))
                    act.activation(sm["egl"], proj_last(), ACT.Exp).then_inc(*AC.up())
                    for h in range(2):
                        act.activation(flat(tiles(EG + 2 * h, 2)), bank[4 + h][:, :], ACT.Exp).then_inc(*AC.up())
                    AC.new["eg"] = AC.n
                    act.activation(mat(E1), mat(E1), ACT.Exp).then_inc(*AC.up())
                    act.activation(mat(E2), mat(E2), ACT.Exp, scale=-1.0).then_inc(*AC.up())
                    act.activation(sm["kes"], sm["kes"], ACT.Exp).then_inc(*AC.up())
                    act.activation(sm["sneg"], sm["gcol"], ACT.Exp).then_inc(*AC.up("decays"))
                if k == 28:
                    act.wait_ge(*DV.at(l, "rowmax"))
                    pr = flat(tiles(PR, 6))
                    for g in range(8):
                        a, b = (g * P, g * P + P) if g < 4 else (512 + (g - 4) * T, 512 + (g - 3) * T)
                        act.activation(pr[:, a:b], pr[:, a:b], ACT.Exp, bias=sm["mx"][:, g:g + 1], scale=HD ** -0.5,
                                       accum_out=sm["rs"][:, g:g + 1]).then_inc(*AC.up())
                    AC.new["exp"] = AC.n
                if k == 29:
                    act.wait_ge(*PE.at(l, "mvT"))
                    for i in range(2):
                        act.copy(flat(tiles(VTOK + 2 * i, 2)), bank[3 + i][:, :]).then_inc(*AC.up())
                    AC.new["vtok"] = AC.n
                if k == 33:
                    act.wait_ge(*PE.at(l, "pv"))
                    for i in range(2):
                        act.copy(flat(bhi[:, 4 + 2 * i:6 + 2 * i, :]), bank[3 + i][:, :]).then_inc(*AC.up())
                    AC.new["mbhi"] = AC.n
                if k in (34, 35):
                    w, bs, dst, bias = (("wi", (5, 2), TI, "bih"), ("wr", (3, 4), TR, "brh"))[k - 34]
                    act.wait_ge(*PE.at(l, w))
                    for t in range(4):
                        act.activation(proj[:, dst + t, :], bank[bs[t // 2]][:, (t % 2) * T:(t % 2 + 1) * T], ACT.Tanh,
                                       bias=sm[bias][:, t:t + 1], scale=0.5).then_inc(*AC.up())
                    AC.new[("tanh_i", "tanh_r")[k - 34]] = AC.n
                if k == 36:
                    act.wait_ge(*AC.last(l))
                    for t in range(4):
                        act.activation(proj[:, A0 + t, :], proj[:, TR + t, :], ACT.Exp,
                                       bias=sm["sp4n"][:, t:t + 1], scale=sm["sp4n"][:, t:t + 1]).then_inc(*AC.up())
                    act.wait_ge(*AC.last(l))
                    for t in range(4):
                        act.activation(proj[:, TR + t, :], proj[:, TR + t, :], ACT.Tanh,
                                       bias=sm["sp2"][:, t:t + 1], scale=sm["sp2"][:, t:t + 1]).then_inc(*AC.up())
                    AC.new["a0"] = AC.n
                if 36 <= k <= 45 and (k - 36) % 3 == 0:
                    n = (k - 36) // 3
                    pa = (lower, upper)[n % 2]
                    act.wait_ge(*PE.at(l, ("VN", n)))
                    act.copy(vnb[pa, :, :], b3(7, 4)[pa, :, :]).then_inc(*AC.up(("vn", n)))
                if k == 37:
                    act.wait_ge(*DV.at(l, ("evac", 17)))
                    act.activation(flat(tiles(TMV, 4)), flat(tiles(TZ, 4)), ACT.Tanh, scale=0.5).then_inc(*AC.up("tz"))
                if k == 40:
                    act.wait_ge(*DV.at(l, "lru_m"))
                    act.activation(tiles(TR, 4), tiles(TR, 4), ACT.Sqrt).then_inc(*AC.up("sqT"))
                if k == 43:
                    act.wait_ge(*DV.at(l, "lru_uv"))
                    act.activation(tiles(TI, 4), tiles(TLY, 4), ACT.Square).then_inc(*AC.up("y2"))
                if k == 45:
                    act.wait_ge(*DV.at(l, "gelu_in"))
                    act.activation(tiles(TI, 4), tiles(TI, 4), ACT.Tanh, scale=float(np.sqrt(2 / np.pi))).then_inc(*AC.up("gelu_t"))
                if k == 46:
                    act.wait_ge(*PE.at(l, ("SU", 3)))
                    for i in range(2):
                        act.activation(flat(tiles(WB + 2 * i, 2)), bank[3 + i][:, :], ACT.Square).then_inc(*AC.up())
                    AC.new["osq"] = AC.n
                if k == 48:
                    act.wait_ge(*DV.at(l, "lru_f"))
                    act.activation(bhi[:, 8:12, :], tiles(TI, 4), ACT.Copy, scale=0.25).then_inc(*AC.up("lruhi"))
                if k == 52:
                    act.wait_ge(*DV.at(l, "dn_f"))
                    act.activation(bhi[:, 0:4, :], tiles(TMQ, 4), ACT.Copy).then_inc(*AC.up("dnhi"))
                c = (k - 2) // 2
                if k % 2 == 0 and 18 <= c <= 29:
                    act.wait_ge(*DV.at(l, ("evac", c)))
                    for i in range(2):
                        t = 2 * c + i
                        act.activation(proj[:, t, :], proj[:, t, :], ACT.Tanh, bias=sm["bgh"][:, t - TG:t - TG + 1],
                                       scale=0.5).then_inc(*AC.up())
                    AC.new[("gates", c)] = AC.n
                if 66 <= k <= 72 and (k - 66) % 6 == 0:
                    for f in range(2):
                        i = 2 * ((k - 66) // 6) + f
                        act.wait_ge(*DV.at(l, ("mixf", i)))
                        act.activation(ahi[:, 2 * i:2 * i + 2, :], tiles(MIX + 2 * i, 2), ACT.Copy, scale=0.5).then_inc(*AC.up(("mixhi", i)))
                if k == 2 * FFN0:
                    x_norm(l, "ffn", l * 2 + 1, None)
                if k > 2 * FFN0 and k % 2 == 0:
                    kind, j = ffn_of(k // 2 - 1)
                    s = 8 * (j % 2)
                    if kind == "gate":
                        act.wait_ge(*DV.at(l, ("gate", j)))
                        act.activation(tiles(s + 2, 2), tiles(s, 2), ACT.Tanh, scale=0.5).then_inc(*AC.up(("ftanh", j)))
                    if kind == "up":
                        act.wait_ge(*DV.at(l, ("hidf", j)))
                        act.activation(bhi[:, 2 * (j % 2):2 * (j % 2) + 2, :], tiles(s + 6, 2), ACT.Copy, scale=0.5).then_inc(*AC.up(("hidhi", j)))

            def proj_last():
                return sm["egl"]

            x_norm(None, "mix", 0, None)
            for m in range(AHEAD):
                act.wait_ge(loaded_raw[m], 16)
                act.copy(whi[:, m, :], raw[:, m, :]).then_inc(*AC.up(("hi_next", m)))
            AC.first = dict(AC.new)
            act.wait_ge(AC.sem, AC.n)
            act.nop().then_inc(AC.sem, max(AC.per, 1))
            AC.n += max(AC.per, 1)
            AC.open_layer()
            with act.Fori(0, L) as l:
                for k in range(NH):
                    if k == 2 * FFN0:
                        side(l, k)
                    if k + AHEAD < NH:
                        hi(l, k + AHEAD)
                    else:
                        hi(l, k + AHEAD - NH, True)
                    if k != 2 * FFN0:
                        side(l, k)
                x_norm(l, "mix", l * 2 + 2, None)
        @block.vector
        def _(dv):
            def step(ins, name=None):
                ins.then_inc(*DV.up(name))
                return DV.n

            def settle(l):
                dv.wait_ge(*DV.last(l))

            def lo(l, m, nxt=False):
                if l is None:
                    dv.wait_ge(AC.sem, AC.first[("hi_next", m)])
                else:
                    dv.wait_ge(*AC.at(l, ("hi_next" if nxt else "hi", m)))
                dv.tensor_tensor(wlo_of(m), raw_of(m), whi_of(m), ALU.subtract)\
                  .then_inc(*DV.up(("lo_next" if nxt or l is None else "lo", m)))

            def rsqrt(l, src, y, n, scale, eps, done):
                w, u = sm["n0"][:, 0:n], sm["n1"][:, 0:n]
                step(dv.tensor_scalar(w, src, scale, eps, ALU.mult, ALU.add))
                settle(l)
                step(dv.tensor_scalar(y.bitcast(I32), w.bitcast(I32), -0.5, float(0x5F3759DF), ALU.mult, ALU.add))
                for i in range(3):
                    settle(l)
                    step(dv.scalar_tensor_tensor(out=u, in0=y, scalar=-0.5, in1=y, op0=ALU.mult, op1=ALU.mult))
                    settle(l)
                    step(dv.tensor_tensor(u, u, w, ALU.mult))
                    settle(l)
                    step(dv.scalar_tensor_tensor(out=y, in0=u, scalar=1.5, in1=y, op0=ALU.add, op1=ALU.mult), done if i == 2 else None)

            def log1p(l, e, s, s2, acc):
                step(dv.tensor_scalar(s2, e, 2.0, None, ALU.add))
                settle(l)
                step(dv.reciprocal(acc, s2))
                settle(l)
                step(dv.tensor_tensor(s, e, acc, ALU.mult))
                settle(l)
                step(dv.tensor_tensor(s2, s, s, ALU.mult))
                settle(l)
                step(dv.tensor_scalar(acc, s2, 1.0 / 15, 1.0 / 13, ALU.mult, ALU.add))
                settle(l)
                step(dv.tensor_tensor(acc, acc, s2, ALU.mult))
                for c in (11, 9, 7, 5, 3):
                    settle(l)
                    step(dv.scalar_tensor_tensor(out=acc, in0=acc, scalar=1.0 / c, in1=s2, op0=ALU.add, op1=ALU.mult))
                settle(l)
                step(dv.scalar_tensor_tensor(out=acc, in0=acc, scalar=1.0, in1=s, op0=ALU.add, op1=ALU.mult))
                settle(l)
                step(dv.tensor_scalar(acc, acc, 2.0, None, ALU.mult))

            def conv(l, src, dst, w):
                step(dv.tensor_scalar(dst, src, par[:, w + 3:w + 4], None, ALU.mult))
                for s in (1, 2, 3):
                    settle(l)
                    step(dv.scalar_tensor_tensor(out=dst[:, s:T], in0=src[:, 0:T - s], scalar=par[:, w + 3 - s:w + 4 - s],
                                                 in1=dst[:, s:T], op0=ALU.mult, op1=ALU.add))

            def x_add(l, step_name, k, p):
                dv.wait_ge(*PE.at(l, ("acc", k, p)))
                step(dv.tensor_tensor(flat(x[:, 2 * p:2 * p + 2, :]), bank[4 + p][:, :], flat(x[:, 2 * p:2 * p + 2, :]), ALU.add),
                     (step_name, "x", p))

            def x_norm(l, name, nidx, p):
                if l is None:
                    dv.wait_ge(AC.sem, AC.first[(name, "hi", p)])
                else:
                    dv.wait_ge(*AC.at(l, (name, "hi", p)))
                for i in range(2):
                    step(dv.scalar_tensor_tensor(out=alo[:, 2 * p + i, :], in0=x[:, 2 * p + i, :],
                                                 scalar=nrm[:, bass.ds(nidx * KT + 2 * p + i, 1)],
                                                 in1=ahi[:, 2 * p + i, :].bitcast(F32), op0=ALU.mult, op1=ALU.subtract))
                DV.new[(name, "lo", p)] = DV.n

            def x_update(l, name, k, nidx):
                for p in range(6):
                    if p < 4:
                        x_add(l, name, k, p)
                    if p >= 2:
                        x_norm(l, name, nidx, p - 2)

            def rnorm(l, name):
                dv.wait_ge(*PE.at(l, (name, "sum")))
                rsqrt(l, bank[2][:, 0:2], sm["nr"], 2, 1.0 / D, EPS, (name, "nr"))

            def rstd_copy(l, name):
                dv.wait_ge(*PE.at(l, (name, "spread")))
                step(dv.tensor_copy(rstd[:, :], bank[2][:, 0:T]), (name, "rstd"))

            def evacuate(l, k):
                c = k // 2 - 1
                if k % 2 == 0 and 0 <= c < C_IN:
                    dv.wait_ge(*PE.at(l, ("bulk", k - 1)))
                    if c == 0:
                        settle(l)
                    step(dv.tensor_tensor(tiles(2 * c, 2), bank[c % 2][:, :].rearrange("p (a b) -> p a b", a=2),
                                          over(rstd[:, :], 2), ALU.mult), ("evac", c))

            def side(l, k):
                if k == 0:
                    dv.wait_ge(loaded_par, l * 16 + 16)
                    dv.wait_ge(*AC.at(l, "wabh"))
                    step(dv.tensor_tensor(wabl[:, :], p_("wab", 0, 64), wabh[:, :], ALU.subtract), "wab")
                    step(dv.tensor_scalar(sm["v"][:, 0:4], p_("lam", 0, 4), -1.0, None, ALU.mult))
                    step(dv.tensor_scalar(sm["brh"], p_("br", 0, 4), 0.5, None, ALU.mult))
                    step(dv.tensor_scalar(sm["bih"], p_("bi", 0, 4), 0.5, None, ALU.mult))
                    step(dv.tensor_scalar(sm["bgh"], p_("bg", 0, 24), 0.5, None, ALU.mult))
                    step(dv.tensor_scalar(sm["nwh"], p_("dnorm"), 0.5, None, ALU.mult))
                    dv.wait_ge(*AC.at(l, "anex"))
                    step(dv.tensor_scalar(sm["anex"], sm["anex"], -1.0, None, ALU.mult))
                if k == 1:
                    rnorm(l, "mix")
                if k == 4:
                    dv.wait_ge(*PE.at(l, "ab"))
                    ab = bank[3][:, 0:16].rearrange("p (m j h) -> p j h m", m=2, j=2)
                    az, bz = (a.rearrange("p (h m) -> p h m", m=2) for a in (sm["v"][:, 4:12], sm["bcol"]))
                    step(dv.tensor_tensor(az, ab[:, 0], over(sm["nr"], 4), ALU.mult))
                    step(dv.tensor_tensor(bz, ab[:, 1], over(sm["nr"], 4), ALU.mult))
                    settle(l)
                    step(dv.tensor_tensor(az, az, each(p_("dtb", 0, 4), 2), ALU.add))
                    settle(l)
                    step(dv.tensor_scalar(sm["s"], sm["v"], -1.0, None, ALU.mult))
                    settle(l)
                    step(dv.tensor_tensor(sm["vabs"], sm["v"], sm["s"], ALU.max), "aabs")
                if k == 6:
                    dv.wait_ge(*AC.at(l, "aexp"))
                    log1p(l, sm["e"], sm["s"], sm["s2"], sm["acc"])
                    step(dv.tensor_scalar(sm["bcol"], sm["bcol"], 0.5, 0.5, ALU.mult, ALU.add))
                    settle(l)
                    step(dv.scalar_tensor_tensor(out=sm["acc"], in0=sm["v"], scalar=0.0, in1=sm["acc"], op0=ALU.max, op1=ALU.add))
                    settle(l)
                    step(dv.tensor_tensor(sm["g"].rearrange("p (h m) -> p h m", m=2), sm["acc"][:, 4:12].rearrange("p (h m) -> p h m", m=2),
                                          each(sm["anex"], 2), ALU.mult), "grow")
                    step(dv.tensor_scalar(sm["sp2"], sm["acc"][:, 0:4], 2.0, None, ALU.mult))
                    step(dv.tensor_scalar(sm["sp4n"], sm["acc"][:, 0:4], -4.0, None, ALU.mult))
                if 3 <= k <= 14:
                    c, odd = divmod(k - 3, 2)
                    if not odd:
                        settle(l)
                        for i in range(2):
                            conv(l, proj[:, 2 * c + i, :], tmp[:, c % 2, i * T:(i + 1) * T], OFF["conv"] + TAPS * (2 * c + i))
                        DV.new[("conv", c)] = DV.n
                    else:
                        dv.wait_ge(*AC.at(l, ("tanh", c)))
                        step(dv.scalar_tensor_tensor(out=flat(tiles(2 * c, 2)), in0=tmq[:, :], scalar=1.0, in1=tmp[:, c % 2, :],
                                                     op0=ALU.add, op1=ALU.mult), ("silu", c))
                if k == 10:
                    dv.wait_ge(*PE.at(l, "gbc"))
                    step(dv.tensor_copy(sm["gcol"], bank[3][:, 0:8]))
                    settle(l)
                    for a, pa in halves:
                        for b in range(2):
                            gb = b3(4 + b, 4)[pa, :, 64 * a:64 * a + 64]
                            gs = slice(4 * b, 4 * b + 4)
                            step(dv.tensor_tensor(mat(LM)[pa, gs, :], gb, each(sm["gcol"][pa, gs], CHUNK), ALU.subtract))
                            step(dv.tensor_tensor(sm["kes"][pa, gs], gb[:, :, 63], sm["gcol"][pa, gs], ALU.subtract))
                    for b in range(2):
                        step(dv.tensor_copy(sm["egl"][:, 8 * b:8 * b + 8], bank[4 + b][:, 63:512:64]))
                    settle(l)
                    step(dv.tensor_scalar(mat(E1), mat(LM), 0.0, None, ALU.min))
                    step(dv.tensor_scalar(mat(E2), mat(LM), 0.0, None, ALU.max), "dif")
                if k == 12:
                    dv.wait_ge(*AC.at(l, "decays"))
                    step(dv.tensor_tensor(mat(E1), mat(E1), over(c_("upin", 64), 8), ALU.mult))
                    step(dv.tensor_tensor(mat(E2), mat(E2), over(c_("low", 64), 8), ALU.mult))
                    step(dv.scalar_tensor_tensor(out=sm["sneg"], in0=sm["sneg"], scalar=-1.0, in1=sm["bcol"], op0=ALU.mult, op1=ALU.mult))
                    settle(l)
                    step(dv.tensor_tensor(mat(E2), mat(E2), each(sm["bcol"], CHUNK), ALU.mult))
                    step(dv.tensor_scalar(sm["mx"], sm["bcol"], 0.5, None, ALU.mult))
                if k == 13:
                    dv.wait_ge(*PE.at(l, "sumqk"))
                    rsqrt(l, bank[2][:, 0:16], sm["rqk"], 16, 1.0, 4 * EPS, None)
                    settle(l)
                    step(dv.tensor_scalar(sm["rqk"][:, 0:8], sm["rqk"][:, 0:8], HD ** -0.5, None, ALU.mult), "rqk")
                if k in (16, 17):
                    dv.wait_ge(*PE.at(l, ("rbc", k - 16)))
                    for i in range(2):
                        t = flat(tiles(4 * (k - 16) + 2 * i, 2))
                        step(dv.tensor_tensor(t, t, bank[(6, 4)[k - 16] + i][:, :], ALU.mult), "knorm")
                if k == 19:
                    dv.wait_ge(*PE.at(l, "kk"))
                    step(dv.tensor_tensor(mat(LM), b3(6, 8), mat(E2), ALU.mult), "lmat")
                    step(dv.tensor_tensor(attnT[:, :, :], b3(7, 8), mat(E1), ALU.mult))
                    step(dv.tensor_tensor(tiles(TQ, 4), tiles(TQ, 4), tiles(EG, 4), ALU.mult))
                if k == 21:
                    dv.wait_ge(*PE.at(l, "lt"))
                    step(dv.tensor_copy(mat(LT), b3(2, 8)))
                    step(dv.tensor_tensor(Tm[:, :, :], mat(LM), over(c_("low1", 64), 8), ALU.mult))
                    settle(l)
                    step(dv.tensor_tensor(Rm[:, :, :], mat(LT), over(c_("up1", 64), 8), ALU.mult))
                    step(dv.tensor_tensor(Tm[:, :, :], over(c_("eye", 64), 8), Tm[:, :, :], ALU.subtract))
                    settle(l)
                    step(dv.tensor_tensor(Rm[:, :, :], over(c_("eye", 64), 8), Rm[:, :, :], ALU.subtract))
                if k == 22:
                    dv.wait_ge(*PE.at(l, "vT"))
                    for i in range(2):
                        step(dv.tensor_tensor(Vb[:, 4 * i:4 * i + 4, :], b3(4 + i, 4), each(sm["mx"][:, 4 * i:4 * i + 4], HD), ALU.mult), "vb")
                    step(dv.tensor_tensor(mat(CM), mat(LT), over(c_("up2", 64), 8), ALU.mult), ("level", 0))
                if k == 23:
                    dv.wait_ge(*PE.at(l, "kT"))
                    for i in range(2):
                        step(dv.tensor_tensor(Kend[:, 4 * i:4 * i + 4, :], b3(6 + i, 4), each(sm["kes"][:, 4 * i:4 * i + 4], HD), ALU.mult), "kend")
                if 25 <= k <= 34:
                    i, part = divmod(k - 25, 2)
                    if part == 0:
                        dv.wait_ge(*PE.at(l, ("X", i)))
                        step(dv.tensor_copy(mat(XM), b3(2, 8)), ("xcopy", i))
                        if i < 4:
                            step(dv.tensor_tensor(mat(CM), mat(LT), over(c_(("up4", "up8", "up16", "up32")[i], 64), 8), ALU.mult))
                    else:
                        dv.wait_ge(*PE.at(l, ("TX", i)))
                        if i < 4:
                            step(dv.tensor_tensor(Tm[:, :, :], Tm[:, :, :], b3(6, 8), ALU.subtract))
                        step(dv.tensor_tensor(Rm[:, :, :], Rm[:, :, :], b3(7, 8), ALU.subtract), ("level", i + 1))
                        if i == 4:
                            DV.new[("w", 0)] = DV.n
                if k == 22:
                    r = tiles(TMQ, 8, slice(0, 32))
                    s = tiles(SQ, 8, slice(0, 32))
                    step(dv.stream_shuffle(s, r, [(i + 16) % 32 for i in range(32)]))
                    settle(l)
                    step(dv.tensor_tensor(r, r, over(c_("cos", 256, slice(0, 32)), 8), ALU.mult))
                if k == 23:
                    r = tiles(TMQ, 8, slice(0, 32))
                    s = tiles(SQ, 8, slice(0, 32))
                    step(dv.tensor_tensor(s, s, over(c_("sin", 256, slice(0, 32)), 8), ALU.mult))
                    settle(l)
                    step(dv.tensor_tensor(r, r, s, ALU.add), "rope")
                if k == 27:
                    dv.wait_ge(*PE.at(l, "scores"))
                    pr = flat(tiles(PR, 6))
                    p0 = pr[:, 0:512].rearrange("p (h k) -> p h k", h=4)
                    step(dv.tensor_tensor(p0, b3(5, 4), over(c_("causal", 128), 4), ALU.add))
                    for b in range(2):
                        p1 = pr[:, 512 + 512 * b:1024 + 512 * b].rearrange("p (h k) -> p h k", h=2)
                        s1 = bank[3 + b][:, :].rearrange("p (h k) -> p h k", h=2)
                        step(dv.tensor_copy(p1[:, :, 0:P], s1[:, :, 0:P]))
                        step(dv.tensor_tensor(p1[:, :, P:T], s1[:, :, P:T], over(c_("causal", 128), 2), ALU.add), "masked")
                    settle(l)
                    step(dv.tensor_reduce(sm["mx"][:, 0:4], p0, AX, ALU.max))
                    step(dv.tensor_reduce(sm["mx"][:, 4:8], pr[:, 512:1536].rearrange("p (h k) -> p h k", h=4), AX, ALU.max))
                    settle(l)
                    step(dv.tensor_scalar(sm["mx"], sm["mx"], -(HD ** -0.5), None, ALU.mult), "rowmax")
                if k == 29:
                    dv.wait_ge(*AC.at(l, "exp"))
                    step(dv.reciprocal(sm["rs"], sm["rs"]))
                    settle(l)
                    pr = flat(tiles(PR, 6))
                    p0 = pr[:, 0:512].rearrange("p (h k) -> p h k", h=4)
                    p1 = pr[:, 512:1536].rearrange("p (h k) -> p h k", h=4)
                    step(dv.tensor_tensor(p0, p0, each(sm["rs"][:, 0:4], P), ALU.mult))
                    step(dv.tensor_tensor(p1, p1, each(sm["rs"][:, 4:8], T), ALU.mult), "probs")
                if k == 31:
                    dv.wait_ge(*PE.at(l, "pT"))
                    for i in range(3):
                        step(dv.tensor_copy(flat(tiles(PT + 2 * i, 2)), bank[3 + i][:, :]), "pcopy")
                if k == 34:
                    dv.wait_ge(*AC.at(l, "mbhi"))
                    for i in range(2):
                        step(dv.tensor_tensor(flat(blo[:, 4 + 2 * i:6 + 2 * i, :]), bank[3 + i][:, :],
                                              flat(bhi[:, 4 + 2 * i:6 + 2 * i, :]), ALU.subtract), "mb_out")
                if k in (29, 30):
                    for t in (0, 1) if k == 29 else (2, 3):
                        conv(l, proj[:, TLX + t, :], proj[:, XC + t, :], OFF["conv"] + TAPS * (12 + t))
                        settle(l)
                        step(dv.tensor_scalar(proj[:, XC + t, :], proj[:, XC + t, :], p_("convb", t), None, ALU.add), "xc")
                if k == 38:
                    dv.wait_ge(*AC.at(l, "a0"))
                    settle(l)
                    step(dv.scalar_tensor_tensor(out=tiles(HSM, 4), in0=tiles(A0, 4), scalar=1.0,
                                                 in1=tiles(TR, 4), op0=ALU.add, op1=ALU.mult), "lru_m")
                    settle(l)
                    step(dv.tensor_scalar(tiles(A0, 4), tiles(HSM, 4), -1.0, 1.0, ALU.mult, ALU.add))
                    step(dv.scalar_tensor_tensor(out=tiles(TI, 4), in0=tiles(TI, 4), scalar=1.0, in1=tiles(XC, 4),
                                                 op0=ALU.add, op1=ALU.mult))
                if k == 41:
                    dv.wait_ge(*AC.at(l, "sqT"))
                    settle(l)
                    step(dv.scalar_tensor_tensor(out=tiles(HSM, 4), in0=tiles(A0, 4), scalar=1.0, in1=tiles(TR, 4),
                                                 op0=ALU.add, op1=ALU.mult))
                    settle(l)
                    step(dv.tensor_tensor(tiles(HSM, 4), tiles(HSM, 4), tiles(TI, 4), ALU.mult), "lru_uv")
                    settle(l)
                    for t in range(4):
                        step(dv.tensor_tensor_scan(proj[:, HS + t, :], proj[:, A0 + t, :], proj[:, HSM + t, :], 0.0, ALU.mult, ALU.add))
                if k == 44:
                    dv.wait_ge(*AC.at(l, "y2"))
                    step(dv.tensor_scalar(tiles(TI, 4), tiles(TI, 4), 0.044715, 1.0, ALU.mult, ALU.add))
                    settle(l)
                    step(dv.tensor_tensor(tiles(TI, 4), tiles(TI, 4), tiles(TLY, 4), ALU.mult), "gelu_in")
                if k == 46:
                    dv.wait_ge(*AC.at(l, "gelu_t"))
                    step(dv.scalar_tensor_tensor(out=tiles(TI, 4), in0=tiles(TI, 4), scalar=1.0, in1=tiles(TLY, 4),
                                                 op0=ALU.add, op1=ALU.mult))
                    settle(l)
                    step(dv.tensor_tensor(tiles(TI, 4), tiles(TI, 4), tiles(HS, 4), ALU.mult), "lru_f")
                if k == 48:
                    dv.wait_ge(*AC.at(l, "lruhi"))
                    step(dv.scalar_tensor_tensor(out=blo[:, 8:12, :], in0=tiles(TI, 4), scalar=0.25, in1=bhi[:, 8:12, :].bitcast(F32),
                                                 op0=ALU.mult, op1=ALU.subtract), "lru_out")
                if 37 <= k <= 45:
                    n, part = divmod(k - 34, 3)
                    if part == 1 and n:
                        m = n // 2
                        pa = (lower, upper)[n % 2]
                        dv.wait_ge(*PE.at(l, ("KS", n)))
                        for h in range(HEADS):
                            g = 2 * h + m
                            step(dv.scalar_tensor_tensor(out=Wb[pa, h, :], in0=b3(6, 4)[pa, h, :], scalar=sm["sneg"][pa, g:g + 1],
                                                         in1=Vb[pa, g, :], op0=ALU.mult, op1=ALU.add), ("w", n))
                    if part == 0:
                        dv.wait_ge(*PE.at(l, ("SU", n - 1)))
                        if n == 1:
                            step(dv.tensor_copy(Sst(1), b3(2, 4)), ("state", 1))
                        else:
                            for h in range(HEADS):
                                step(dv.scalar_tensor_tensor(out=Sst(n % 2)[:, h, :], in0=Sst((n - 1) % 2)[:, h, :],
                                                             scalar=sm["egl"][:, NCH * h + n - 1:NCH * h + n],
                                                             in1=b3(2, 4)[:, h, :], op0=ALU.mult, op1=ALU.add), ("state", n))
                if k == 37:
                    dv.wait_ge(*AC.at(l, "tz"))
                    step(dv.scalar_tensor_tensor(out=tiles(TZ, 4), in0=tiles(TMV, 4), scalar=1.0, in1=tiles(TZ, 4),
                                                 op0=ALU.add, op1=ALU.mult), "zsilu")
                if k == 48:
                    dv.wait_ge(*PE.at(l, "sumo"))
                    rsqrt(l, bank[2][:, 0:8], sm["ro"], 8, 1.0 / HD, EPS, "ro")
                if k == 51:
                    dv.wait_ge(*PE.at(l, "robc"))
                    for i in range(2):
                        step(dv.tensor_tensor(flat(tiles(TZ + 2 * i, 2)), flat(tiles(TZ + 2 * i, 2)), bank[6 + i][:, :], ALU.mult))
                    settle(l)
                    for i in range(2):
                        step(dv.scalar_tensor_tensor(out=flat(tiles(TMQ + 2 * i, 2)), in0=flat(tiles(TZ + 2 * i, 2)), scalar=sm["nwh"],
                                                     in1=bank[3 + i][:, :], op0=ALU.mult, op1=ALU.mult), "dn_f")
                if k == 52:
                    dv.wait_ge(*AC.at(l, "dnhi"))
                    step(dv.tensor_tensor(blo[:, 0:4, :], tiles(TMQ, 4), bhi[:, 0:4, :], ALU.subtract), "dn_out")
                c = k // 2 - 1 - C_IN
                if k % 2 == 0 and 0 <= c < C_Y:
                    hf, br = divmod(c, 3)
                    dv.wait_ge(*PE.at(l, ("bulk", k - 1)))
                    if c == 0:
                        dv.wait_ge(*AC.at(l, ("gates", 29)))
                    for i in range(2):
                        f = 4 * hf + 2 * i
                        g, mx = flat(tiles(TG + 8 * br + f, 2)), flat(tiles(MIX + f, 2))
                        dst = mx if br == 0 else g
                        step(dv.scalar_tensor_tensor(out=dst, in0=g, scalar=1.0, in1=bank[2 * (c % 2) + i][:, :],
                                                     op0=ALU.add, op1=ALU.mult), ("y", c))
                    if br:
                        settle(l)
                        for i in range(2):
                            f = 4 * hf + 2 * i
                            g, mx = flat(tiles(TG + 8 * br + f, 2)), flat(tiles(MIX + f, 2))
                            step(dv.tensor_tensor(mx, mx, g, ALU.add), ("mixf", 2 * hf + i))
                    if br == 2:
                        for i in range(2):
                            q = 2 * hf + i
                            dv.wait_ge(*AC.at(l, ("mixhi", q)))
                            step(dv.scalar_tensor_tensor(out=alo[:, 2 * q:2 * q + 2, :], in0=tiles(MIX + 2 * q, 2), scalar=0.5,
                                                         in1=ahi[:, 2 * q:2 * q + 2, :].bitcast(F32), op0=ALU.mult, op1=ALU.subtract),
                                 ("mixed", q))
                if k == 2 * FFN0:
                    x_update(l, "ffn", 2 * FFN0 - 1, l * 2 + 1)
                if k == 2 * FFN0 + 1:
                    rnorm(l, "ffn")
                if k == 2 * FFN0 + 2:
                    rstd_copy(l, "ffn")
                if k > 2 * FFN0 and k % 2 == 0:
                    kind, j = ffn_of(k // 2 - 1)
                    s = 8 * (j % 2)
                    if kind != "down":
                        dv.wait_ge(*PE.at(l, ("bulk", k - 1)))
                    if kind == "gate":
                        if j == 0:
                            settle(l)
                        step(dv.tensor_tensor(tiles(s, 2), bank[0][:, :].rearrange("p (a b) -> p a b", a=2),
                                              over(rstd[:, :], 2), ALU.mult), ("gate", j))
                    if kind == "up":
                        step(dv.tensor_tensor(tiles(s + 4, 2), bank[1][:, :].rearrange("p (a b) -> p a b", a=2),
                                              over(rstd[:, :], 2), ALU.mult), ("up", j))
                        dv.wait_ge(*AC.at(l, ("ftanh", j)))
                        step(dv.scalar_tensor_tensor(out=tiles(s + 2, 2), in0=tiles(s + 2, 2), scalar=1.0, in1=tiles(s, 2),
                                                     op0=ALU.add, op1=ALU.mult))
                        settle(l)
                        step(dv.tensor_tensor(tiles(s + 6, 2), tiles(s + 2, 2), tiles(s + 4, 2), ALU.mult), ("hidf", j))
                        dv.wait_ge(*AC.at(l, ("hidhi", j)))
                        step(dv.scalar_tensor_tensor(out=blo[:, 2 * (j % 2):2 * (j % 2) + 2, :], in0=tiles(s + 6, 2), scalar=0.5,
                                                     in1=bhi[:, 2 * (j % 2):2 * (j % 2) + 2, :].bitcast(F32),
                                                     op0=ALU.mult, op1=ALU.subtract), ("hidden", j))

            HSM = UU

            for p in range(4):
                x_norm(None, "mix", 0, p)
            for m in range(AHEAD):
                lo(None, m)
            DV.first = dict(DV.new)
            dv.wait_ge(DV.sem, DV.n)
            dv.nop().then_inc(DV.sem, max(DV.per, 1))
            DV.n += max(DV.per, 1)
            DV.open_layer()
            with dv.Fori(0, L) as l:
                for k in range(NH):
                    if k == 2:
                        rstd_copy(l, "mix")
                    evacuate(l, k)
                    side(l, k)
                    if k + AHEAD < NH:
                        lo(l, k + AHEAD)
                    else:
                        lo(l, k + AHEAD - NH, True)
                x_update(l, "mix", NH - 1, l * 2 + 2)
            DV.n_end = DV.n
            dv.wait_ge(PE.sem, PE_FINAL)
            rsqrt(L - 1, bank[2][:, 0:2], sm["nr"], 2, 1.0 / D, EPS, "last_nr")
            dv.wait_ge(PE.sem, PE_FINAL + 1)
            for kt in range(KT):
                step(dv.scalar_tensor_tensor(out=x[:, kt, :], in0=x[:, kt, :], scalar=nrm[:, 2 * L * KT + kt:2 * L * KT + kt + 1],
                                             in1=bank[2][:, 0:T], op0=ALU.mult, op1=ALU.mult), ("out", kt // 4))
            DV.marks_out = DV.n
            DV.n = DV.n_end
        return {s.name: s.learnt() for s in signals}


def _columns(w):
    return np.concatenate([w[:, :, 0:1536], w[:, :, 2056:4616], w[:, :, 1536:2048], w[:, :, 4616:]], axis=2)


def _constants():
    con = np.zeros((P, NCON), np.float32)

    def put(name, a):
        con[:a.shape[0], CON[name]:CON[name] + a.shape[1]] = a

    put("ident", np.eye(P, dtype=np.float32))
    q = np.arange(P)
    put("causal", np.where(q[None, :] <= q[:, None], 0.0, -1e30).astype(np.float32))
    put("ones", np.ones((P, P), np.float32))
    half = HD // 8
    inv = (np.float32(500000.0) ** (-np.arange(half, dtype=np.float32) / np.float32(half))).astype(np.float32)
    ang = (np.arange(T, dtype=np.float32)[None, :] * inv[:, None]).astype(np.float32)
    cos, sin = np.cos(ang).astype(np.float32), np.sin(ang).astype(np.float32)
    put("cos", np.concatenate([cos, cos], 0))
    put("sin", np.concatenate([-sin, sin], 0))
    put("tri", ((q[:, None] <= q[None, :]) & (q[:, None] // CHUNK == q[None, :] // CHUNK)).astype(np.float32))
    i = np.arange(P)[:, None] % CHUNK
    j = np.arange(CHUNK)[None, :]
    put("eye", (i == j).astype(np.float32))
    put("upin", (j >= i).astype(np.float32))
    put("low", (j < i).astype(np.float32))

    def level(r, c, s):
        return ((r // (2 * s) == c // (2 * s)) & (r % (2 * s) >= s) & (c % (2 * s) < s)).astype(np.float32)

    put("low1", level(i, j, 1))
    for s in (1, 2, 4, 8, 16, 32):
        put(f"up{s}", level(j, i, s))
    return con


def kernel(x, norm_mix, w_in, b_gate, dn_conv, dn_a_log, dn_dt_bias, dn_norm, dn_out, mb_out,
           lru_conv_w, lru_conv_b, lru_w_r, lru_b_r, lru_w_i, lru_b_i, lru_lambda, lru_out,
           w_o, norm_ffn, ffn_in, ffn_down, norm_final):
    import concourse.bacc as bacc
    from concourse.bass_utils import run_bass_kernel_spmd

    A = np.asarray
    win = A(w_in)
    stream = np.zeros((L * CH + 3, P, 2 * HALF), np.float32)
    wi = _columns(win).reshape(L, KT, P, C_IN, 256).transpose(0, 3, 2, 1, 4).reshape(L, C_IN, P, 2 * HALF)
    ys = np.stack([A(dn_out), A(mb_out), A(lru_out)], 1).reshape(L, 3, 4, P, 2, 512)
    ys = ys.transpose(0, 4, 1, 3, 2, 5).reshape(L, C_Y, P, 2 * HALF)
    wo = A(w_o).reshape(L, C_WO, 2, P, D).transpose(0, 1, 3, 2, 4).reshape(L, C_WO, P, 2 * HALF)
    fi = A(ffn_in).reshape(L, KT, P, 2, PAIRS, 256).transpose(0, 3, 4, 2, 1, 5).reshape(L, 2, PAIRS, P, 2 * HALF)
    fd = A(ffn_down).reshape(L, PAIRS, 2, P, D).transpose(0, 1, 3, 2, 4).reshape(L, PAIRS, P, 2 * HALF)
    for l in range(L):
        s = stream[l * CH:(l + 1) * CH]
        s[0:C_IN] = wi[l]
        s[C_IN:C_IN + C_Y] = ys[l]
        s[C_IN + C_Y:FFN0] = wo[l]
        s[FFN0], s[FFN0 + 1] = fi[l, 0, 0], fi[l, 1, 0]
        for j in range(1, PAIRS):
            s[FFN0 + 3 * j - 1], s[FFN0 + 3 * j], s[FFN0 + 3 * j + 1] = fi[l, 0, j], fi[l, 1, j], fd[l, j - 1]
        s[CH - 1] = fd[l, PAIRS - 1]

    par = np.zeros((L, P, NPAR), np.float32)

    def put(name, a):
        par[:, :a.shape[1], OFF[name]:OFF[name] + a.shape[2]] = a

    def tiled(a, n):
        return A(a).reshape(L, n, P).transpose(0, 2, 1)

    put("wab", win[:, :, 2048:2056].reshape(L, KT, P, 8).transpose(0, 2, 1, 3).reshape(L, P, 64))
    cw = np.concatenate([A(dn_conv), A(lru_conv_w)], 2).reshape(L, TAPS, 16, P)
    put("conv", cw.transpose(0, 3, 2, 1).reshape(L, P, 64))
    put("convb", tiled(lru_conv_b, 4))
    put("br", tiled(lru_b_r, 4))
    put("bi", tiled(lru_b_i, 4))
    put("lam", tiled(lru_lambda, 4))
    put("dnorm", A(dn_norm).reshape(L, P, 1))
    put("bg", tiled(b_gate, 24))
    put("alog", np.broadcast_to(A(dn_a_log).reshape(L, 1, 4), (L, P, 4)))
    put("dtb", np.broadcast_to(A(dn_dt_bias).reshape(L, 1, 4), (L, P, 4)))
    for name, w in (("wr", A(lru_w_r)), ("wi", A(lru_w_i))):
        w = w.reshape(L, 4, 2, 64, 64)
        for t in range(4):
            for g in range(2):
                par[:, 64 * g:64 * g + 64, OFF[name] + P * t + 64 * g:OFF[name] + P * t + 64 * g + 64] = w[:, t, g]
    nm, nf = tiled(norm_mix, KT), tiled(norm_ffn, KT)
    nl = A(norm_final).reshape(KT, P).T
    norms = np.concatenate([w[l] for l in range(L) for w in (nm, nf)] + [nl], 1)
    xT = A(x).reshape(T, KT, P).transpose(2, 1, 0)

    arrays = {"stream_dram": stream, "params_dram": par, "consts_dram": _constants(),
              "norms_dram": np.ascontiguousarray(norms), "x_dram": np.ascontiguousarray(xT)}
    known = {}
    for _ in range(3):
        nc = bacc.Bacc("TRN2", target_bir_lowering=False, num_devices=1)
        args = [nc.dram_tensor(n, a.shape, mybir.dt.from_np(a.dtype), kind="ExternalInput").ap() for n, a in arrays.items()]
        o = nc.dram_tensor("out_dram", (P, KT, T), F32, kind="ExternalOutput").ap()
        known = build(nc, *args, o, known)
    r = run_bass_kernel_spmd(nc, [arrays], core_ids=[0])
    y = np.asarray(r.results[0]["out_dram"])
    return np.ascontiguousarray(y.transpose(2, 1, 0)).reshape(1, T, D)
```

```python
from contextlib import ExitStack

import numpy as np
import concourse.bass as bass
from concourse import mybir

F32 = mybir.dt.float32
F32R = mybir.dt.float32r
I32 = mybir.dt.int32
ALU = mybir.AluOpType
ACT = mybir.ActivationFunctionType
AX = mybir.AxisListType.X

P = 128
D = 1024
T = 256
L = 2
HEADS = 4
HD = 128
CHUNK = 64
NCH = T // CHUNK
TAPS = 4
EPS = 1e-6
FFN = 2816
KT = D // P
HALF = 1024

C_IN = 30
C_Y = 6
C_WO = 4
PAIRS = FFN // 256
C_FFN = 3 * PAIRS
CH = C_IN + C_Y + C_WO + C_FFN
NH = 2 * CH
FFN0 = C_IN + C_Y + C_WO
RING = 5
AHEAD = RING - 1

TQ, TK, TV, TMQ, TMK, TMV, TLX, TLY, TZ, TG = 0, 4, 8, 12, 16, 20, 24, 28, 32, 36
NT = 60

OFF = {}


def _place(names):
    at = 0
    for name, n in names:
        OFF[name] = at
        at += n
    return at


NPAR = _place([("wab", KT * 8), ("conv", 16 * TAPS), ("convb", 4), ("br", 4), ("bi", 4), ("lam", 4),
               ("dnorm", 1), ("bg", 24), ("alog", 4), ("dtb", 4), ("wr", 512), ("wi", 512)])
CON = {}
_at = 0
for _n, _k in [("ident", 128), ("causal", 128), ("ones", 128), ("ecol", 64), ("cos", 256), ("sin", 256),
               ("tri", 128), ("eye", 64), ("upin", 64), ("low", 64), ("low1", 64),
               ("up1", 64), ("up2", 64), ("up4", 64), ("up8", 64), ("up16", 64), ("up32", 64)]:
    CON[_n] = _at
    _at += _k
NCON = _at


class Signal:

    def __init__(self, sem, name, known):
        self.sem, self.name = sem, name
        self.base, self.per, self.marks = known.get(name, (0, 0, {}))
        self.n, self.new, self.start = 0, {}, 0

    def up(self, step=None):
        self.n += 1
        if step is not None:
            self.new[step] = self.n
        return self.sem, 1

    def open_layer(self):
        self.start, self.n = self.n, 0
        self.pre, self.new = self.new, {}

    def at(self, l, step, prev=False):
        n = self.base + self.marks.get(step, 1)
        if prev:
            return self.sem, l * self.per + (n - self.per)
        return self.sem, l * self.per + n

    def last(self, l, back=0):
        return self.sem, (l * self.per + self.base if l is not None else 0) + self.n - back

    def learnt(self):
        return (self.start, self.n, self.new)


def build(nc, wstream, params, consts, norms, x_in, out, known):
    ctx = ExitStack()
    with ctx:
        def sb(name, shape, dt=F32):
            return ctx.enter_context(nc.sbuf_tensor(name, shape, dt))

        def sem(name):
            return ctx.enter_context(nc.semaphore(name))

        raw = sb("raw", [P, RING, HALF])
        whi = sb("whi", [P, RING, HALF], F32R)
        wlo = sb("wlo", [P, RING, HALF], F32R)
        x = sb("x", [P, KT, T])
        ahi = sb("ahi", [P, KT, T], F32R)
        alo = sb("alo", [P, KT, T], F32R)
        proj = sb("proj", [P, NT, T])
        bhi = sb("bhi", [P, 12, T], F32R)
        blo = sb("blo", [P, 12, T], F32R)
        con = sb("con", [P, NCON])
        par = sb("par", [P, NPAR])
        nrm = sb("nrm", [P, (2 * L + 1) * KT])
        rstd = sb("rstd", [P, T])
        tmp = sb("tmp", [P, 2, 2 * T])
        tmq = sb("tmq", [P, 2 * T])
        Tm = sb("Tm", [P, 8, CHUNK])
        Rm = sb("Rm", [P, 8, CHUNK])
        attnT = sb("attnT", [P, 8, CHUNK])
        Vb = sb("Vb", [P, 8, HD])
        Kend = sb("Kend", [P, 8, HD])
        small = sb("small", [P, 300])
        wabh = sb("wabh", [P, KT * 8], F32R)
        wabl = sb("wabl", [P, KT * 8], F32R)
        bank = [ctx.enter_context(nc.psum_tensor(f"bank{i}", [P, 512], F32)) for i in range(8)]

        loaded_raw = [sem(f"loaded_raw{i}") for i in range(RING)]
        loaded_x = [sem(f"loaded_x{i}") for i in range(4)]
        loaded_con, loaded_nrm, loaded_par = (sem(n) for n in ("loaded_con", "loaded_nrm", "loaded_par"))
        loaded_last = sem("loaded_last")
        stored = sem("stored")
        PE = Signal(sem("tensor_done"), "pe", known)
        DV = Signal(sem("vector_done"), "dv", known)
        AC = Signal(sem("scalar_done"), "ac", known)
        signals = (PE, DV, AC)

        block = ctx.enter_context(nc.Block())

        def c_(name, n=None, p=slice(0, P)):
            return con[p, CON[name]:CON[name] + n]

        def p_(name, i=0, n=1, p=slice(0, P)):
            return par[p, OFF[name] + i:OFF[name] + i + n]

        sm = {}
        at = 0
        for name, n in [("gcol", 8), ("bcol", 8), ("sneg", 8), ("kes", 8), ("egl", 16), ("mx", 8), ("rs", 8),
                        ("brh", 4), ("bih", 4), ("bgh", 24), ("sp2", 4), ("sp4n", 4), ("nwh", 1), ("anex", 4),
                        ("v", 12), ("vabs", 12), ("e", 12), ("s", 12), ("s2", 12), ("acc", 12),
                        ("g", 8), ("nr", 2), ("rqk", 16), ("ro", 8), ("n0", 16), ("n1", 16)]:
            sm[name] = small[:, at:at + n]
            at += n
        assert at <= 300

        def tiles(t, n, p=slice(0, P)):
            return proj[p, t:t + n, :]

        def flat(ap):
            return ap.rearrange("p a b -> p (a b)")

        def mat(t):
            return flat(tiles(t, 2)).rearrange("p (g c) -> p g c", g=8)

        def over(ap, n):
            return ap.unsqueeze(1).broadcast_to([ap.shape[0], n, ap.shape[1]])

        def each(ap, n):
            return ap.unsqueeze(2).broadcast_to([ap.shape[0], ap.shape[1], n])

        SQ, EG, E1, E2, LM, LT = 48, 44, 36, 38, 40, 42
        CM, XM = 8, 10
        PR, PT, VTOK = 48, 54, 44
        S0, WB, VN = 8, 16, 18
        XC, TR, TI, A0, UU, HS = 12, 52, 48, 24, 20, 52
        MIX = 0
        lower, upper = slice(0, 64), slice(64, 128)
        halves = ((0, lower), (1, upper))

        def Sst(i):
            return flat(tiles(S0 + 2 * i, 2)).rearrange("p (h e) -> p h e", h=HEADS)

        Wb = flat(tiles(WB, 2)).rearrange("p (h e) -> p h e", h=HEADS)
        vnb = flat(tiles(VN, 2)).rearrange("p (h e) -> p h e", h=HEADS)

        def b3(i, g):
            return bank[i][:, :].rearrange("p (g c) -> p g c", g=g)

        def ffn_of(c):
            i = c - FFN0
            if i < 2:
                return ("gate", "up")[i], 0
            if i == C_FFN - 1:
                return "down", PAIRS - 1
            j, r = divmod(i - 2, 3)
            return (("gate", j + 1), ("up", j + 1), ("down", j))[r]

        CONV_AT = (5, 6, 7, 9, 11, 15)
        uses = (NH - 1) // RING
        assert NH - 1 == uses * RING
        LAST = NH - 1
        XRAW, XSPLIT = 56, 4

        def raw_of(m):
            return flat(tiles(XRAW, 4)) if m == LAST else raw[:, m % RING, :]

        def whi_of(m):
            return flat(bhi[:, XSPLIT:XSPLIT + 4, :]) if m == LAST else whi[:, m % RING, :]

        def wlo_of(m):
            return flat(blo[:, XSPLIT:XSPLIT + 4, :]) if m == LAST else wlo[:, m % RING, :]

        def y_bank(i):
            return 2 * ((i + 1) % 2)

        def gate_bank(j):
            return bank[3 if j == 1 else 0]

        def in_bank(c):
            return bank[4 if c == 2 else c % 2]

        def landed(l, m, nxt=False):
            if m == LAST:
                return loaded_last, 16 * (l + 1)
            return loaded_raw[m % RING], 16 * (l * uses + m // RING + 1 + (uses if nxt else 0))

        def last_user(m):
            return LAST - RING + m

        @block.sync
        def _(sp):
            def load(g, m):
                sp.dma_start(raw_of(m), wstream[g, :, (m % 2) * HALF:(m % 2 + 1) * HALF]).then_inc(
                    loaded_last if m == LAST else loaded_raw[m % RING], 16)

            sp.dma_start(nrm[:, :], norms).then_inc(loaded_nrm, 16)
            for p in range(4):
                sp.dma_start(x[:, 2 * p:2 * p + 2, :], x_in[:, 2 * p:2 * p + 2, :]).then_inc(loaded_x[p], 16)
            for m in range(RING):
                load(m // 2, m)
            sp.dma_start(con[:, :], consts).then_inc(loaded_con, 16)
            with sp.Fori(0, L) as l:
                used = [AC.at(l, ("gates", 29), prev=True), DV.at(l, ("mixed", 3), prev=True)]
                used = [(s, sp.snap(v)) for s, v in used]
                for s, v in used:
                    sp.wait_ge(s, v)
                sp.dma_start(par[:, :], params[l]).then_inc(loaded_par, 16)
                for k in range(NH):
                    m = k + RING
                    chunk = sp.snap(l * CH + (m // 2 if m < NH else CH + (m - NH) // 2))
                    if k < AHEAD:
                        sp.wait_ge(*DV.at(l, ("lo_next", k), prev=True))
                    else:
                        sp.wait_ge(*DV.at(l, ("lo", k if m < NH else k - 1)))
                    load(chunk, m if m < NH else m - NH)
            for i in range(2):
                sp.wait_ge(*DV.at(L - 1, ("out", i)))
                sp.dma_start(out[:, 4 * i:4 * i + 4, :], x[:, 4 * i:4 * i + 4, :]).then_inc(stored, 16)
            sp.wait_ge(stored, 32)
            for m in range(RING):
                sp.wait_ge(*landed(L, m))

        @block.tensor
        def _(pe):
            def products(dst, wcol, m, hi, lo, first, last):
                pe.matmul(dst, whi_of(m)[:, wcol], hi, start=first, stop=False, skip_group_check=True)
                pe.matmul(dst, whi_of(m)[:, wcol], lo, start=False, stop=False, skip_group_check=True)
                return pe.matmul(dst, wlo_of(m)[:, wcol], hi, start=False, stop=last, skip_group_check=True)

            def wait_split(l, k):
                if k < AHEAD:
                    pe.wait_ge(*DV.at(l, ("lo_next", k), prev=True))
                else:
                    pe.wait_ge(*DV.at(l, ("lo", k)))

            def cols(j):
                return slice(j * P, (j + 1) * P)

            def by_output(l, k, dst, start_kt, act_wait=None):
                for i in range(4):
                    kt = start_kt + i
                    if act_wait is not None:
                        act_wait(kt)
                    if i == 3:
                        early_waits(l, k)
                    for n in range(2):
                        ins = products(dst[:, n * T:(n + 1) * T], cols(2 * i + n), k,
                                       ahi[:, kt, :], alo[:, kt, :], kt == 0 and n == 0, kt == KT - 1)
                ins.then_inc(*PE.up(("bulk", k)))

            def y_half(k, base):
                c = k // 2 - C_IN
                br = c % 3
                for i in range(2):
                    kt = (k % 2) * 2 + i
                    for n in range(4):
                        ins = products(bank[base + n // 2][:, (n % 2) * T:(n % 2 + 1) * T], cols(4 * i + n), k,
                                       bhi[:, 4 * br + kt, :], blo[:, 4 * br + kt, :],
                                       kt == 0 and n % 2 == 0, kt == 3)
                ins.then_inc(*PE.up(("bulk", k)))

            def by_contraction(k, hi, lo, first, last):
                for n in range(8):
                    ins = products(bank[4 + n // 2][:, (n % 2) * T:(n % 2 + 1) * T], cols(n), k, hi, lo,
                                   first and n % 2 == 0, last)
                    if last and n % 2:
                        ins.then_inc(*PE.up(("acc", k, n // 2)))
                if not last:
                    ins.then_inc(*PE.up(("bulk", k)))
                else:
                    PE.new[("bulk", k)] = PE.n

            def early_waits(l, k):
                if k == 18:
                    pe.wait_ge(*DV.at(l, "knorm"))
                if k == 20:
                    pe.wait_ge(*DV.at(l, "lmat"))
                if 24 <= k <= 33:
                    i, part = divmod(k - 24, 2)
                    pe.wait_ge(*DV.at(l, ("xcopy", i) if part else ("level", i)))
                if 34 < k <= 45 and (k - 34) % 3 == 1:
                    pe.wait_ge(*DV.at(l, ("w", (k - 34) // 3)))

            def exact(dst, lhsT, rhs, start=True, stop=True):
                return pe.matmul(dst, lhsT, rhs, start=start, stop=stop, skip_group_check=True)

            def norm_sum(l, step):
                pe.wait_ge(*DV.at(l, (step, "acc")))
                for m in range(2):
                    for i in range(2):
                        ins = exact(bank[2][:, m:m + 1], tmq[:, i * T + m * P:i * T + (m + 1) * P], c_("ones", 1), i == 0, i == 1)
                ins.then_inc(*PE.up((step, "sum")))

            def spread(dst, col, m):
                return exact(dst[:, m * P:(m + 1) * P], col.broadcast_to([P, P]), c_("ident", P))

            def norm_spread(l, step):
                pe.wait_ge(*DV.at(l, (step, "nr")))
                for m in range(2):
                    ins = spread(bank[2], sm["nr"][:, m:m + 1], m)
                ins.then_inc(*PE.up((step, "spread")))

            def side(l, k):
                if k == 2:
                    pe.wait_ge(loaded_con, 16)
                    norm_sum(l, "mix")
                if k == 1:
                    pe.wait_ge(*DV.at(l, "wab"))
                    dst = bank[3][0:8, 0:T]
                    for kt in range(KT):
                        w = slice(kt * 8, kt * 8 + 8)
                        pe.matmul(dst, wabh[:, w], ahi[:, kt, :], start=kt == 0, stop=False, skip_group_check=True)
                        pe.matmul(dst, wabh[:, w], alo[:, kt, :], start=False, stop=False, skip_group_check=True)
                        ins = pe.matmul(dst, wabl[:, w], ahi[:, kt, :], start=False, stop=kt == KT - 1, skip_group_check=True)
                    ins.then_inc(*PE.up("ab"))
                if k == 3:
                    norm_spread(l, "mix")
                    pe.wait_ge(*DV.at(l, "abrows"))
                    for m in range(2):
                        ins = exact(bank[3][:, T + 8 * m:T + 8 * m + 8], proj[0:8, EG, m * P:(m + 1) * P], c_("ident", 8, slice(0, 8)))
                    ins.then_inc(*PE.up("abT"))
                if k == 11:
                    pe.wait_ge(*DV.at(l, "grow"))
                    exact(bank[3][:, 0:8], c_("tri", P), sm["g"])
                    for h in range(HEADS):
                        for m in range(2):
                            ins = exact(bank[4 + h // 2][:, (h % 2) * T + m * P:(h % 2) * T + (m + 1) * P],
                                        sm["g"][:, 2 * h + m:2 * h + m + 1].broadcast_to([P, P]), c_("tri", P))
                    ins.then_inc(*PE.up("gbc"))
                if k == 12:
                    pe.wait_ge(*AC.at(l, ("sq", 3)))
                    for t in range(8):
                        ins = exact(bank[2][0:8, 0:T], c_("ecol", 64)[:, 8 * t:8 * t + 8], proj[:, SQ + t, :], t == 0, t == 7)
                    ins.then_inc(*PE.up("sumqk"))
                if k in (13, 48):
                    pe.wait_ge(*DV.at(l, ("sumrows", k)))
                    for m in range(2):
                        ins = exact(bank[2][:, T + 8 * m:T + 8 * m + 8], proj[0:8, SQ if k == 13 else WB, m * P:(m + 1) * P],
                                    c_("ident", 8, slice(0, 8)))
                    ins.then_inc(*PE.up(("sumT", k)))
                if k in (15, 16):
                    pe.wait_ge(*DV.at(l, "rqk"))
                    if k == 16:
                        pe.wait_ge(*AC.at(l, "eg"))
                    for h in range(HEADS):
                        t = 4 * (k - 15) + h
                        for m in range(2):
                            ins = spread(bank[(6, 4)[k - 15] + h // 2][:, (h % 2) * T:(h % 2 + 1) * T], sm["rqk"][:, 2 * t + m:2 * t + m + 1], m)
                    ins.then_inc(*PE.up(("rbc", k - 15)))
                if k == 18:
                    for b, q0 in ((6, TK), (7, TQ)):
                        for h in range(HEADS):
                            for n in range(NCH):
                                m, a = divmod(n, 2)
                                cs = slice(n * CHUNK, (n + 1) * CHUNK)
                                ins = exact(b3(b, 8)[64 * a:64 * a + 64, 2 * h + m, :], proj[:, TK + h, cs], proj[:, q0 + h, cs])
                    ins.then_inc(*PE.up("kk"))
                if k == 20:
                    for g in range(8):
                        for a, pa in halves:
                            ins = exact(b3(2, 8)[pa, g, :], mat(LM)[pa, g, :], c_("eye", 64, pa))
                    ins.then_inc(*PE.up("lt"))
                if k == 21:
                    pe.wait_ge(*DV.at(l, ("silu", 5)))
                    for g in range(8):
                        h, m = divmod(g, 2)
                        ins = pe.transpose(b3(4 + g // 4, 4)[:, g % 4, :], proj[:, TV + h, m * P:(m + 1) * P], c_("ident", 128))
                    ins.then_inc(*PE.up("vT"))
                if k == 22:
                    for g in range(8):
                        h, m = divmod(g, 2)
                        ins = pe.transpose(b3(6 + g // 4, 4)[:, g % 4, :], proj[:, TK + h, m * P:(m + 1) * P], c_("ident", 128))
                    ins.then_inc(*PE.up("kT"))
                if 24 <= k <= 33:
                    i, part = divmod(k - 24, 2)
                    if part == 0:
                        for g in range(8):
                            for a, pa in halves:
                                ins = exact(b3(2, 8)[pa, g, :], mat(CM)[pa, g, :], Tm[pa, g, :])
                        ins.then_inc(*PE.up(("X", i)))
                    else:
                        for b, lt, rt in ((6, Rm, mat(XM)), (7, mat(XM), Rm)):
                            if i == 4 and b == 6:
                                continue
                            for g in range(8):
                                for a, pa in halves:
                                    ins = exact(b3(b, 8)[pa, g, :], lt[pa, g, :], rt[pa, g, :])
                        ins.then_inc(*PE.up(("TX", i)))
                if k == 26:
                    pe.wait_ge(*DV.at(l, "rope"))
                    pe.wait_ge(*AC.at(l, "vb"))
                    for h in range(HEADS):
                        exact(b3(5, 4)[:, h, :], proj[:, TMQ + h, 0:P], proj[:, TMK + h, 0:P])
                        ins = exact(bank[3 + h // 2][:, (h % 2) * T:(h % 2 + 1) * T], proj[:, TMQ + h, P:T], proj[:, TMK + h, :])
                    ins.then_inc(*PE.up("scores"))
                if k == 28:
                    pe.wait_ge(*DV.at(l, "masked"))
                    for g in range(8):
                        h, m = divmod(g, 2)
                        ins = pe.transpose(b3(3 + g // 4, 4)[:, g % 4, :], proj[:, TMV + h, m * P:(m + 1) * P], c_("ident", 128))
                    ins.then_inc(*PE.up("mvT"))
                if k == 30:
                    pe.wait_ge(*DV.at(l, "probs"))
                    pe.wait_ge(*AC.at(l, "vtok"))
                    pr = flat(tiles(PR, 6))
                    for g in range(12):
                        ins = pe.transpose(b3(3 + g // 4, 4)[:, g % 4, :], pr[:, g * P:(g + 1) * P], c_("ident", 128))
                    ins.then_inc(*PE.up("pT"))
                if k == 32:
                    pe.wait_ge(*AC.at(l, "pcopy"))
                    vt = flat(tiles(VTOK, 4)).rearrange("p (g d) -> p g d", g=8)
                    pt = flat(tiles(PT, 6)).rearrange("p (g q) -> p g q", g=12)
                    for h in range(HEADS):
                        d0 = bank[3 + h // 2][:, (h % 2) * T:(h % 2) * T + P]
                        d1 = bank[3 + h // 2][:, (h % 2) * T + P:(h % 2 + 1) * T]
                        exact(d0, vt[:, 2 * h, :], pt[:, h, :])
                        exact(d1, vt[:, 2 * h, :], pt[:, 4 + 2 * h, :], True, False)
                        ins = exact(d1, vt[:, 2 * h + 1, :], pt[:, 5 + 2 * h, :], False, True)
                    ins.then_inc(*PE.up("pv"))
                if k in (33, 34):
                    pe.wait_ge(*DV.at(l, "xc"))
                    if k == 34:
                        pe.wait_ge(*DV.at(l, "mb_out"))
                    else:
                        pe.wait_ge(*DV.at(l, ("xcopy", 4)))
                    w, bs = (("wi", (5, 2)), ("wr", (3, 4)))[k - 33]
                    for t in range(4):
                        ins = exact(bank[bs[t // 2]][:, (t % 2) * T:(t % 2 + 1) * T], p_(w, t * P, P), proj[:, XC + t, :])
                    ins.then_inc(*PE.up(w))
                if 34 < k <= 45:
                    n, part = divmod(k - 34, 3)
                    m, a = divmod(n, 2)
                    pa = (lower, upper)[a]
                    cs = slice(n * CHUNK, (n + 1) * CHUNK)
                    if part == 0:
                        pe.wait_ge(*DV.at(l, ("state", n)))
                        for h in range(HEADS):
                            ins = exact(b3(6, 4)[pa, h, :], proj[:, TK + h, cs], Sst(n % 2)[:, h, :])
                        ins.then_inc(*PE.up(("KS", n)))
                    if part == 1:
                        for h in range(HEADS):
                            ins = exact(b3(7, 4)[pa, h, :], Rm[pa, 2 * h + m, :], (Vb[pa, m:8:2, :] if n == 0 else Wb[pa, :, :])[:, h, :])
                        ins.then_inc(*PE.up(("VN", n)))
                    if part == 2:
                        pe.wait_ge(*AC.at(l, ("vn", n)))
                        if n == 0:
                            pe.wait_ge(*AC.at(l, "tanh_r"))
                        for h in range(HEADS):
                            o = bank[3 + h // 2][:, (h % 2) * T + n * CHUNK:(h % 2) * T + (n + 1) * CHUNK]
                            if n:
                                exact(o, Sst(n % 2)[:, h, :], proj[:, TQ + h, cs], True, False)
                            ins = exact(o, vnb[pa, h, :], attnT[pa, 2 * h + m, :], n == 0, True)
                            if n < NCH - 1:
                                ins = exact(b3(2, 4)[:, h, :], Kend[pa, 2 * h + m, :], vnb[pa, h, :])
                        ins.then_inc(*PE.up(("SU", n)))
                if k == 47:
                    pe.wait_ge(*AC.at(l, "osq"))
                    for t in range(4):
                        ins = exact(bank[2][0:8, 0:T], c_("ecol", 64)[:, 8 * t:8 * t + 8], proj[:, WB + t, :], t == 0, t == 3)
                    ins.then_inc(*PE.up("sumo"))
                if k == 50:
                    pe.wait_ge(*DV.at(l, "ro"))
                    for h in range(HEADS):
                        for m in range(2):
                            ins = spread(bank[6 + h // 2][:, (h % 2) * T:(h % 2 + 1) * T], sm["ro"][:, 2 * h + m:2 * h + m + 1], m)
                    ins.then_inc(*PE.up("robc"))

            pe.nop().then_inc(PE.sem, max(PE.per, 1))
            PE.n = max(PE.per, 1)
            PE.open_layer()
            with pe.Fori(0, L) as l:
                for k in range(NH):
                    c, half = divmod(k, 2)
                    if c < FFN0 + 2:
                        wait_split(l, k)
                    elif half == 0:
                        wait_split(l, k + 1)
                    if c < C_IN:
                        if c > 2 and half == 0:
                            pe.wait_ge(*DV.at(l, ("evac", c - 2)))
                        aw = None
                        if c == 0:
                            aw = lambda kt: pe.wait_ge(*DV.at(l, ("mix", "lo", kt // 2), prev=True)) if kt % 2 == 0 else None
                        by_output(l, k, in_bank(c), 4 * half, aw)
                        side(l, k)
                    elif c < C_IN + C_Y:
                        i = c - C_IN
                        if half == 0:
                            if i < 2:
                                pe.wait_ge(*DV.at(l, ("evac", 28 + i)))
                            if i == 0:
                                pe.wait_ge(*DV.at(l, "dn_out"))
                            if i == 2:
                                pe.wait_ge(*DV.at(l, "lru_out"))
                            if i >= 2:
                                pe.wait_ge(*DV.at(l, ("y", i - 2)))
                        y_half(k, y_bank(i))
                    elif c < FFN0:
                        i = k - 2 * (C_IN + C_Y)
                        if i == 0:
                            pe.wait_ge(*DV.at(l, ("mixed", 1)))
                        if i == 4:
                            pe.wait_ge(*DV.at(l, ("mixed", 3)))
                        by_contraction(k, ahi[:, i, :], alo[:, i, :], i == 0, i == KT - 1)
                    else:
                        kind, j = ffn_of(c)
                        if kind == "down":
                            if half == 0:
                                pe.wait_ge(*DV.at(l, ("hidden", j)))
                            t = 2 * (j % 2) + half
                            by_contraction(k, bhi[:, t, :], blo[:, t, :], j == 0 and half == 0, j == PAIRS - 1 and half == 1)
                        else:
                            if half == 0 and j > (kind == "gate"):
                                pe.wait_ge(*DV.at(l, (kind, j - 1)))
                            aw = None
                            if kind == "gate" and j == 0:
                                aw = lambda kt: pe.wait_ge(*DV.at(l, ("ffn", "lo", kt // 2))) if kt % 2 == 0 else None
                            by_output(l, k, bank[1] if kind == "up" else gate_bank(j), 4 * half, aw)
                            if kind == "up" and j == 0 and half == 0:
                                norm_sum(l, "ffn")
                            if kind == "up" and j == 0 and half == 1:
                                norm_spread(l, "ffn")
            pe.wait_ge(*DV.at(L - 1, "last_acc"))
            for m in range(2):
                for i in range(2):
                    ins = exact(bank[2][:, m:m + 1], tmq[:, i * T + m * P:i * T + (m + 1) * P], c_("ones", 1), i == 0, i == 1)
            ins.then_inc(PE.sem, 1)
            pe.wait_ge(*DV.at(L - 1, "last_nr"))
            for m in range(2):
                ins = spread(bank[2], sm["nr"][:, m:m + 1], m)
            ins.then_inc(PE.sem, 1)
        PE_FINAL = PE.base + L * PE.per + 1

        @block.scalar
        def _(act):
            def hi(l, m, nxt=False):
                act.wait_ge(*landed(l, m, nxt))
                if l is not None and m >= RING:
                    act.wait_ge(*PE.at(l, ("bulk", m - RING)))
                elif l is not None and nxt:
                    act.wait_ge(*PE.at(l, ("bulk", last_user(m))))
                elif l is not None:
                    act.wait_ge(*PE.at(l, ("bulk", last_user(m)), prev=True))
                act.copy(whi_of(m), raw_of(m)).then_inc(*AC.up(("hi_next" if nxt or l is None else "hi", m)))

            def x_norm(l, step, nidx):
                def squares(p):
                    act.activation(tiles(SQ + 2 * p, 2), x[:, 2 * p:2 * p + 2, :], ACT.Square).then_inc(*AC.up((step, "sq", p)))

                for p in range(4):
                    if l is None:
                        if p == 0:
                            act.wait_ge(loaded_nrm, 16)
                        act.wait_ge(loaded_x[p], 16)
                    else:
                        act.wait_ge(*DV.at(l, (step, "x", p)))
                    for i in range(2):
                        act.activation(ahi[:, 2 * p + i, :], x[:, 2 * p + i, :], ACT.Copy,
                                       scale=nrm[:, bass.ds(nidx * KT + 2 * p + i, 1)]).then_inc(*AC.up())
                    AC.new[(step, "hi", p)] = AC.n
                    if p and l is not None:
                        squares(p - 1)
                if l is not None:
                    squares(3)
                else:
                    for m in range(AHEAD):
                        act.wait_ge(loaded_raw[m], 16)
                        act.copy(whi[:, m, :], raw[:, m, :]).then_inc(*AC.up(("hi_next", m)))
                    for p in range(4):
                        squares(p)

            def side(l, k):
                if k == 0:
                    act.wait_ge(loaded_par, l * 16 + 16)
                    act.copy(wabh[:, :], p_("wab", 0, 64)).then_inc(*AC.up("wabh"))
                    act.activation(sm["anex"], p_("alog", 0, 4), ACT.Exp).then_inc(*AC.up("anex"))
                if k == 5:
                    act.wait_ge(*DV.at(l, "aabs"))
                    act.activation(sm["e"], sm["vabs"], ACT.Exp, scale=-1.0).then_inc(*AC.up())
                    act.activation(sm["bcol"], sm["bcol"], ACT.Tanh, scale=0.5).then_inc(*AC.up("aexp"))
                if k in CONV_AT:
                    c = CONV_AT.index(k)
                    act.wait_ge(*DV.at(l, ("conv", c)))
                    act.activation(tmq[:, :], tmp[:, c % 2, :], ACT.Tanh, scale=0.5).then_inc(*AC.up(("tanh", c)))
                if k - 1 in CONV_AT and k - 1 <= CONV_AT[3]:
                    c = CONV_AT.index(k - 1)
                    act.wait_ge(*DV.at(l, ("silu", c)))
                    act.activation(tiles(SQ + 2 * c, 2), tiles(2 * c, 2), ACT.Square).then_inc(*AC.up(("sq", c)))
                if k == 21:
                    act.wait_ge(*PE.at(l, "lt"))
                    act.copy(mat(LT), b3(2, 8)).then_inc(*AC.up("ltcopy"))
                if k in (22, 23):
                    name, dst, scale, b = (("vb", Vb, "mx", 4), ("kend", Kend, "kes", 6))[k - 22]
                    act.wait_ge(*PE.at(l, ("vT", "kT")[k - 22]))
                    for g in range(8):
                        act.activation(dst[:, g, :], b3(b + g // 4, 4)[:, g % 4, :], ACT.Copy, scale=sm[scale][:, g:g + 1]).then_inc(*AC.up(name))
                if k in (27, 28):
                    act.wait_ge(*DV.at(l, ("evac", k - 15)))
                    if k == 27:
                        act.wait_ge(*PE.at(l, "scores"))
                    for t in (0, 1) if k == 27 else (2, 3):
                        act.activation(proj[:, XC + t, :], proj[:, TLX + t, :], ACT.Identity, bias=p_("convb", t),
                                       scale=p_("conv", TAPS * (12 + t) + 3)).then_inc(*AC.up(("xtap", t // 2)))
                if k + 1 in CONV_AT:
                    c = CONV_AT.index(k + 1)
                    act.wait_ge(*DV.at(l, ("evac", c)))
                    if c >= 2:
                        act.wait_ge(*DV.at(l, ("silu", c - 2)))
                    for i in range(2):
                        act.activation(tmp[:, c % 2, i * T:(i + 1) * T], proj[:, 2 * c + i, :], ACT.Copy,
                                       scale=p_("conv", TAPS * (2 * c + i) + 3)).then_inc(*AC.up(("tap", c)))
                if k == 12:
                    act.wait_ge(*DV.at(l, "dif"))
                    act.activation(sm["egl"], sm["egl"], ACT.Exp).then_inc(*AC.up())
                    for h in range(2):
                        act.activation(flat(tiles(EG + 2 * h, 2)), bank[4 + h][:, :], ACT.Exp).then_inc(*AC.up())
                    AC.new["eg"] = AC.n
                    act.activation(mat(E1), mat(E1), ACT.Exp).then_inc(*AC.up())
                    act.activation(mat(E2), mat(E2), ACT.Exp, scale=-1.0).then_inc(*AC.up())
                    act.activation(sm["kes"], sm["kes"], ACT.Exp).then_inc(*AC.up())
                    act.activation(sm["sneg"], sm["gcol"], ACT.Exp).then_inc(*AC.up("decays"))
                if k == 28:
                    act.wait_ge(*DV.at(l, "rowmax"))
                    pr = flat(tiles(PR, 6))
                    for g in range(8):
                        a, b = (g * P, g * P + P) if g < 4 else (512 + (g - 4) * T, 512 + (g - 3) * T)
                        act.activation(pr[:, a:b], pr[:, a:b], ACT.Exp, bias=sm["mx"][:, g:g + 1], scale=HD ** -0.5,
                                       accum_out=sm["rs"][:, g:g + 1]).then_inc(*AC.up())
                    AC.new["exp"] = AC.n
                if k == 29:
                    act.wait_ge(*PE.at(l, "mvT"))
                    for i in range(2):
                        act.copy(flat(tiles(VTOK + 2 * i, 2)), bank[3 + i][:, :]).then_inc(*AC.up())
                    AC.new["vtok"] = AC.n
                if k == 31:
                    act.wait_ge(*PE.at(l, "pT"))
                    for i in range(3):
                        act.copy(flat(tiles(PT + 2 * i, 2)), bank[3 + i][:, :]).then_inc(*AC.up("pcopy"))
                if k == 33:
                    act.wait_ge(*PE.at(l, "pv"))
                    for i in range(2):
                        act.copy(flat(bhi[:, 4 + 2 * i:6 + 2 * i, :]), bank[3 + i][:, :]).then_inc(*AC.up())
                    AC.new["mbhi"] = AC.n
                if k in (34, 35):
                    w, bs, dst, bias = (("wi", (5, 2), TI, "bih"), ("wr", (3, 4), TR, "brh"))[k - 34]
                    act.wait_ge(*PE.at(l, w))
                    for t in range(4):
                        act.activation(proj[:, dst + t, :], bank[bs[t // 2]][:, (t % 2) * T:(t % 2 + 1) * T], ACT.Tanh,
                                       bias=sm[bias][:, t:t + 1], scale=0.5).then_inc(*AC.up())
                    AC.new[("tanh_i", "tanh_r")[k - 34]] = AC.n
                if 36 <= k <= 45 and (k - 36) % 3 == 0:
                    n = (k - 36) // 3
                    pa = (lower, upper)[n % 2]
                    act.wait_ge(*PE.at(l, ("VN", n)))
                    act.copy(vnb[pa, :, :], b3(7, 4)[pa, :, :]).then_inc(*AC.up(("vn", n)))
                if k == 36:
                    act.wait_ge(*AC.last(l))
                    for t in range(4):
                        act.activation(proj[:, A0 + t, :], proj[:, TR + t, :], ACT.Exp,
                                       bias=sm["sp4n"][:, t:t + 1], scale=sm["sp4n"][:, t:t + 1]).then_inc(*AC.up())
                if k == 37:
                    act.wait_ge(*AC.last(l))
                    for t in range(4):
                        act.activation(proj[:, TR + t, :], proj[:, TR + t, :], ACT.Tanh,
                                       bias=sm["sp2"][:, t:t + 1], scale=sm["sp2"][:, t:t + 1]).then_inc(*AC.up())
                    AC.new["a0"] = AC.n
                if k == 37:
                    act.wait_ge(*DV.at(l, ("evac", 17)))
                    act.activation(flat(tiles(TMV, 4)), flat(tiles(TZ, 4)), ACT.Tanh, scale=0.5).then_inc(*AC.up("tz"))
                if k == 40:
                    act.wait_ge(*DV.at(l, "lru_m"))
                    act.activation(tiles(TR, 4), tiles(TR, 4), ACT.Sqrt).then_inc(*AC.up("sqT"))
                if k == 43:
                    act.wait_ge(*DV.at(l, "lru_uv"))
                    act.activation(tiles(TI, 4), tiles(TLY, 4), ACT.Square).then_inc(*AC.up("y2"))
                if k == 45:
                    act.wait_ge(*DV.at(l, "gelu_in"))
                    act.activation(tiles(TI, 4), tiles(TI, 4), ACT.Tanh, scale=float(np.sqrt(2 / np.pi))).then_inc(*AC.up("gelu_t"))
                if k == 46:
                    act.wait_ge(*PE.at(l, ("SU", 3)))
                    for i in range(2):
                        act.activation(flat(tiles(WB + 2 * i, 2)), bank[3 + i][:, :], ACT.Square).then_inc(*AC.up())
                    AC.new["osq"] = AC.n
                if k == 48:
                    act.wait_ge(*DV.at(l, "lru_f"))
                    act.activation(bhi[:, 8:12, :], tiles(TI, 4), ACT.Copy, scale=0.25).then_inc(*AC.up("lruhi"))
                if k == 52:
                    act.wait_ge(*DV.at(l, "dn_f"))
                    act.activation(bhi[:, 0:4, :], tiles(TMQ, 4), ACT.Copy).then_inc(*AC.up("dnhi"))
                c = (k - 2) // 2
                if k % 2 == 0 and 18 <= c <= 29:
                    act.wait_ge(*DV.at(l, ("evac", c)))
                    for i in range(2):
                        t = 2 * c + i
                        act.activation(proj[:, t, :], proj[:, t, :], ACT.Tanh, bias=sm["bgh"][:, t - TG:t - TG + 1],
                                       scale=0.5).then_inc(*AC.up())
                    AC.new[("gates", c)] = AC.n
                if 66 <= k <= 72 and (k - 66) % 6 == 0:
                    for f in range(2):
                        i = 2 * ((k - 66) // 6) + f
                        act.wait_ge(*DV.at(l, ("mixf", i)))
                        act.activation(ahi[:, 2 * i:2 * i + 2, :], tiles(MIX + 2 * i, 2), ACT.Copy, scale=0.5).then_inc(*AC.up(("mixhi", i)))
                if k == 2 * FFN0:
                    x_norm(l, "ffn", l * 2 + 1)
                if k > 2 * FFN0 and k % 2 == 0:
                    kind, j = ffn_of(k // 2 - 1)
                    s = 8 * (j % 2)
                    for i in (0,) if (kind, j) == ("up", 0) else (j,) if kind == "gate" and j else ():
                        act.wait_ge(*DV.at(l, ("gate", i)))
                        act.activation(tiles(8 * (i % 2) + 2, 2), tiles(8 * (i % 2), 2), ACT.Tanh, scale=0.5).then_inc(*AC.up(("ftanh", i)))
                    if kind == "up":
                        act.wait_ge(*DV.at(l, ("hidf", j)))
                        act.activation(bhi[:, 2 * (j % 2):2 * (j % 2) + 2, :], tiles(s + 6, 2), ACT.Copy, scale=0.5).then_inc(*AC.up(("hidhi", j)))

            x_norm(None, "mix", 0)
            AC.first = dict(AC.new)
            act.wait_ge(AC.sem, AC.n)
            act.nop().then_inc(AC.sem, max(AC.per, 1))
            AC.n += max(AC.per, 1)
            AC.open_layer()
            with act.Fori(0, L) as l:
                for k in range(NH):
                    if k == 2 * FFN0:
                        side(l, k)
                    if k + AHEAD < NH:
                        hi(l, k + AHEAD)
                    else:
                        hi(l, k + AHEAD - NH, True)
                    if k != 2 * FFN0:
                        side(l, k)
                x_norm(l, "mix", l * 2 + 2)
        @block.vector
        def _(dv):
            def step(ins, name=None):
                ins.then_inc(*DV.up(name))
                return DV.n

            def settle(l, back=0):
                dv.wait_ge(*DV.last(l, back))

            def lo(l, m, nxt=False):
                if l is None:
                    dv.wait_ge(AC.sem, AC.first[("hi_next", m)])
                else:
                    dv.wait_ge(*AC.at(l, ("hi_next" if nxt else "hi", m)))
                dv.tensor_tensor(wlo_of(m), raw_of(m), whi_of(m), ALU.subtract)\
                  .then_inc(*DV.up(("lo_next" if nxt or l is None else "lo", m)))

            def rsqrt(l, src, y, n, scale, eps, done):
                w, u = sm["n0"][:, 0:n], sm["n1"][:, 0:n]
                step(dv.tensor_scalar(w if len(src.shape) == 2 else w.rearrange("p (t m) -> p t m", m=2), src, scale, eps, ALU.mult, ALU.add))
                settle(l)
                step(dv.tensor_scalar(y.bitcast(I32), w.bitcast(I32), -0.5, float(0x5F3759DF), ALU.mult, ALU.add))
                for i in range(3):
                    settle(l)
                    step(dv.scalar_tensor_tensor(out=u, in0=y, scalar=-0.5, in1=y, op0=ALU.mult, op1=ALU.mult))
                    settle(l)
                    step(dv.tensor_tensor(u, u, w, ALU.mult))
                    settle(l)
                    step(dv.scalar_tensor_tensor(out=y, in0=u, scalar=1.5, in1=y, op0=ALU.add, op1=ALU.mult), done if i == 2 else None)

            def log1p(l, e, s, s2, acc):
                step(dv.tensor_scalar(s2, e, 2.0, None, ALU.add))
                settle(l)
                step(dv.reciprocal(acc, s2))
                settle(l)
                step(dv.tensor_tensor(s, e, acc, ALU.mult))
                settle(l)
                step(dv.tensor_tensor(s2, s, s, ALU.mult))
                settle(l)
                step(dv.tensor_scalar(acc, s2, 1.0 / 15, 1.0 / 13, ALU.mult, ALU.add))
                settle(l)
                step(dv.tensor_tensor(acc, acc, s2, ALU.mult))
                for c in (11, 9, 7, 5, 3):
                    settle(l)
                    step(dv.scalar_tensor_tensor(out=acc, in0=acc, scalar=1.0 / c, in1=s2, op0=ALU.add, op1=ALU.mult))
                settle(l)
                step(dv.scalar_tensor_tensor(out=acc, in0=acc, scalar=1.0, in1=s, op0=ALU.add, op1=ALU.mult))
                settle(l)
                step(dv.tensor_scalar(acc, acc, 2.0, None, ALU.mult))

            def conv(l, srcs, dsts, ws, done):
                for s in (1, 2, 3):
                    for i in range(2):
                        if s > 1:
                            settle(l, 1)
                        step(dv.scalar_tensor_tensor(out=dsts[i][:, s:T], in0=srcs[i][:, 0:T - s], scalar=par[:, ws[i] + 3 - s:ws[i] + 4 - s],
                                                     in1=dsts[i][:, s:T], op0=ALU.mult, op1=ALU.add), done)

            def x_add(l, step_name, k, p):
                dv.wait_ge(*PE.at(l, ("acc", k, p)))
                step(dv.tensor_tensor(flat(x[:, 2 * p:2 * p + 2, :]), bank[4 + p][:, :], flat(x[:, 2 * p:2 * p + 2, :]), ALU.add),
                     (step_name, "x", p))

            def x_norm(l, name, nidx, p):
                if l is None:
                    dv.wait_ge(AC.sem, AC.first[(name, "hi", p)])
                else:
                    dv.wait_ge(*AC.at(l, (name, "hi", p)))
                for i in range(2):
                    step(dv.scalar_tensor_tensor(out=alo[:, 2 * p + i, :], in0=x[:, 2 * p + i, :],
                                                 scalar=nrm[:, bass.ds(nidx * KT + 2 * p + i, 1)],
                                                 in1=ahi[:, 2 * p + i, :].bitcast(F32), op0=ALU.mult, op1=ALU.subtract))
                DV.new[(name, "lo", p)] = DV.n

            def x_update(l, name, k, nidx):
                for p in range(5):
                    if p < 4:
                        x_add(l, name, k, p)
                    if p >= 1:
                        x_norm(l, name, nidx, p - 1)

            def add_squares(l, name, done, prev=False):
                dv.wait_ge(*AC.at(l, (name, "sq", 1), prev=prev))
                step(dv.tensor_tensor(tmq[:, :], flat(tiles(SQ, 2)), flat(tiles(SQ + 2, 2)), ALU.add))
                for p in (2, 3):
                    dv.wait_ge(*AC.at(l, (name, "sq", p), prev=prev))
                    settle(l)
                    step(dv.tensor_tensor(tmq[:, :], tmq[:, :], flat(tiles(SQ + 2 * p, 2)), ALU.add), done)

            def rnorm(l, name):
                dv.wait_ge(*PE.at(l, (name, "sum")))
                rsqrt(l, bank[2][:, 0:2], sm["nr"], 2, 1.0 / D, EPS, (name, "nr"))

            def rstd_copy(l, name):
                dv.wait_ge(*PE.at(l, (name, "spread")))
                step(dv.tensor_copy(rstd[:, :], bank[2][:, 0:T]), (name, "rstd"))

            def evacuate(l, k):
                for c in (0, 1) if k == 4 else (k // 2 - 1,) if k % 2 == 0 and k > 4 and k // 2 <= C_IN else ():
                    dv.wait_ge(*PE.at(l, ("bulk", 2 * c + 1)))
                    if c == 0:
                        settle(l)
                    step(dv.tensor_tensor(tiles(2 * c, 2), in_bank(c)[:, :].rearrange("p (a b) -> p a b", a=2),
                                          over(rstd[:, :], 2), ALU.mult), ("evac", c))

            def side(l, k):
                if k == 0:
                    dv.wait_ge(loaded_par, l * 16 + 16)
                    dv.wait_ge(*AC.at(l, "wabh"))
                    step(dv.tensor_tensor(wabl[:, :], p_("wab", 0, 64), wabh[:, :], ALU.subtract), "wab")
                    step(dv.tensor_scalar(sm["v"][:, 0:4], p_("lam", 0, 4), -1.0, None, ALU.mult))
                    step(dv.tensor_scalar(sm["brh"], p_("br", 0, 4), 0.5, None, ALU.mult))
                    step(dv.tensor_scalar(sm["bih"], p_("bi", 0, 4), 0.5, None, ALU.mult))
                    step(dv.tensor_scalar(sm["bgh"], p_("bg", 0, 24), 0.5, None, ALU.mult))
                    step(dv.tensor_scalar(sm["nwh"], p_("dnorm"), 0.5, None, ALU.mult))
                    dv.wait_ge(*AC.at(l, "anex"))
                    step(dv.tensor_scalar(sm["anex"], sm["anex"], -1.0, None, ALU.mult))
                    add_squares(l, "mix", ("mix", "acc"), prev=True)
                if k == 2:
                    dv.wait_ge(*PE.at(l, "ab"))
                    step(dv.tensor_copy(proj[0:8, EG, :], bank[3][0:8, 0:T]), "abrows")
                if k == 4:
                    dv.wait_ge(*PE.at(l, "abT"))
                    ab = bank[3][:, T:T + 16].rearrange("p (m j h) -> p j h m", m=2, j=2)
                    az, bz = (a.rearrange("p (h m) -> p h m", m=2) for a in (sm["v"][:, 4:12], sm["bcol"]))
                    step(dv.tensor_tensor(az, ab[:, 0], over(sm["nr"], 4), ALU.mult))
                    step(dv.tensor_tensor(bz, ab[:, 1], over(sm["nr"], 4), ALU.mult))
                    settle(l)
                    step(dv.tensor_tensor(az, az, each(p_("dtb", 0, 4), 2), ALU.add))
                    settle(l)
                    step(dv.tensor_scalar(sm["s"], sm["v"], -1.0, None, ALU.mult))
                    settle(l)
                    step(dv.tensor_tensor(sm["vabs"], sm["v"], sm["s"], ALU.max), "aabs")
                if k == 8:
                    dv.wait_ge(*AC.at(l, "aexp"))
                    log1p(l, sm["e"], sm["s"], sm["s2"], sm["acc"])
                    step(dv.tensor_scalar(sm["bcol"], sm["bcol"], 0.5, 0.5, ALU.mult, ALU.add))
                    settle(l)
                    step(dv.scalar_tensor_tensor(out=sm["acc"], in0=sm["v"], scalar=0.0, in1=sm["acc"], op0=ALU.max, op1=ALU.add))
                    settle(l)
                    step(dv.tensor_tensor(sm["g"].rearrange("p (h m) -> p h m", m=2), sm["acc"][:, 4:12].rearrange("p (h m) -> p h m", m=2),
                                          each(sm["anex"], 2), ALU.mult), "grow")
                    step(dv.tensor_scalar(sm["sp2"], sm["acc"][:, 0:4], 2.0, None, ALU.mult))
                    step(dv.tensor_scalar(sm["sp4n"], sm["acc"][:, 0:4], -4.0, None, ALU.mult))
                if k in (16, 17):
                    if k == 17:
                        dv.wait_ge(*DV.at(l, ("evac", 7)))
                    dv.wait_ge(*PE.at(l, ("rbc", k - 16)))
                    for i in range(2):
                        t = flat(tiles(4 * (k - 16) + 2 * i, 2))
                        step(dv.tensor_tensor(t, t, bank[(6, 4)[k - 16] + i][:, :], ALU.mult), "knorm")
                if k - 1 in CONV_AT:
                    c = CONV_AT.index(k - 1)
                    dv.wait_ge(*AC.at(l, ("tanh", c)))
                    step(dv.scalar_tensor_tensor(out=flat(tiles(2 * c, 2)), in0=tmq[:, :], scalar=1.0, in1=tmp[:, c % 2, :],
                                                 op0=ALU.add, op1=ALU.mult), ("silu", c))
                if k in CONV_AT:
                    c = CONV_AT.index(k)
                    dv.wait_ge(*AC.at(l, ("tap", c)))
                    conv(l, [proj[:, 2 * c + i, :] for i in range(2)], [tmp[:, c % 2, i * T:(i + 1) * T] for i in range(2)],
                         [OFF["conv"] + TAPS * (2 * c + i) for i in range(2)], ("conv", c))
                if k == 12:
                    dv.wait_ge(*PE.at(l, "gbc"))
                    step(dv.tensor_copy(sm["gcol"], bank[3][:, 0:8]))
                    settle(l)
                    for a, pa in halves:
                        for b in range(2):
                            gb = b3(4 + b, 4)[pa, :, 64 * a:64 * a + 64]
                            gs = slice(4 * b, 4 * b + 4)
                            step(dv.tensor_tensor(mat(LM)[pa, gs, :], gb, each(sm["gcol"][pa, gs], CHUNK), ALU.subtract))
                            step(dv.tensor_tensor(sm["kes"][pa, gs], gb[:, :, 63], sm["gcol"][pa, gs], ALU.subtract))
                    for b in range(2):
                        step(dv.tensor_copy(sm["egl"][:, 8 * b:8 * b + 8], bank[4 + b][:, 63:512:64]))
                    settle(l)
                    step(dv.tensor_scalar(mat(E1), mat(LM), 0.0, None, ALU.min))
                    step(dv.tensor_scalar(mat(E2), mat(LM), 0.0, None, ALU.max), "dif")
                if k == 17:
                    dv.wait_ge(*AC.at(l, "decays"))
                    step(dv.tensor_tensor(mat(E1), mat(E1), over(c_("upin", 64), 8), ALU.mult))
                    step(dv.tensor_tensor(mat(E2), mat(E2), over(c_("low", 64), 8), ALU.mult))
                    step(dv.scalar_tensor_tensor(out=sm["sneg"], in0=sm["sneg"], scalar=-1.0, in1=sm["bcol"], op0=ALU.mult, op1=ALU.mult))
                    settle(l)
                    step(dv.tensor_tensor(mat(E2), mat(E2), each(sm["bcol"], CHUNK), ALU.mult))
                    step(dv.tensor_scalar(sm["mx"], sm["bcol"], 0.5, None, ALU.mult))
                if k in (13, 48):
                    dv.wait_ge(*PE.at(l, "sumqk" if k == 13 else "sumo"))
                    step(dv.tensor_copy(proj[0:8, SQ if k == 13 else WB, :], bank[2][0:8, 0:T]), ("sumrows", k))
                if k == 14:
                    dv.wait_ge(*PE.at(l, ("sumT", 13)))
                    rsqrt(l, bank[2][:, T:T + 16].rearrange("p (m t) -> p t m", m=2), sm["rqk"], 16, 1.0, 4 * EPS, None)
                    settle(l)
                    step(dv.tensor_scalar(sm["rqk"][:, 0:8], sm["rqk"][:, 0:8], HD ** -0.5, None, ALU.mult), "rqk")
                if k == 19:
                    dv.wait_ge(*PE.at(l, "kk"))
                    settle(l)
                    step(dv.tensor_tensor(mat(LM), b3(6, 8), mat(E2), ALU.mult), "lmat")
                    step(dv.tensor_tensor(attnT[:, :, :], b3(7, 8), mat(E1), ALU.mult))
                    step(dv.tensor_tensor(tiles(TQ, 4), tiles(TQ, 4), tiles(EG, 4), ALU.mult))
                if k == 21:
                    dv.wait_ge(*DV.at(l, "lmat"))
                    step(dv.tensor_tensor(Tm[:, :, :], mat(LM), over(c_("low1", 64), 8), ALU.mult))
                    settle(l)
                    step(dv.tensor_tensor(Tm[:, :, :], over(c_("eye", 64), 8), Tm[:, :, :], ALU.subtract))
                if k == 22:
                    dv.wait_ge(*AC.at(l, "ltcopy"))
                    dv.wait_ge(*PE.at(l, "vT"))
                    step(dv.tensor_tensor(Rm[:, :, :], mat(LT), over(c_("up1", 64), 8), ALU.mult))
                    step(dv.tensor_tensor(mat(CM), mat(LT), over(c_("up2", 64), 8), ALU.mult))
                    settle(l, 1)
                    step(dv.tensor_tensor(Rm[:, :, :], over(c_("eye", 64), 8), Rm[:, :, :], ALU.subtract), ("level", 0))
                if 25 <= k <= 34:
                    i, part = divmod(k - 25, 2)
                    if part == 0:
                        dv.wait_ge(*PE.at(l, ("X", i)))
                        step(dv.tensor_copy(mat(XM), b3(2, 8)), ("xcopy", i))
                        if i < 4:
                            step(dv.tensor_tensor(mat(CM), mat(LT), over(c_(("up4", "up8", "up16", "up32")[i], 64), 8), ALU.mult))
                    else:
                        dv.wait_ge(*PE.at(l, ("TX", i)))
                        if i < 4:
                            step(dv.tensor_tensor(Tm[:, :, :], Tm[:, :, :], b3(6, 8), ALU.subtract))
                        step(dv.tensor_tensor(Rm[:, :, :], Rm[:, :, :], b3(7, 8), ALU.subtract), ("level", i + 1))
                        if i == 4:
                            DV.new[("w", 0)] = DV.n
                if k in (18, 21):
                    r, s = (tiles(t + 4 * (k == 21), 4, slice(0, 32)) for t in (TMQ, SQ))
                    step(dv.stream_shuffle(s, r, [(i + 16) % 32 for i in range(32)]), ("shuffle", k == 21))
                if k in (20, 23):
                    r = tiles(TMQ + 4 * (k == 23), 4, slice(0, 32))
                    dv.wait_ge(*DV.at(l, ("shuffle", k == 23)))
                    step(dv.tensor_tensor(r, r, over(c_("cos", 256, slice(0, 32)), 4), ALU.mult))
                if k in (20, 24):
                    s = tiles(SQ + 4 * (k == 24), 4, slice(0, 32))
                    step(dv.tensor_tensor(s, s, over(c_("sin", 256, slice(0, 32)), 4), ALU.mult), ("cossin", k == 24))
                if k in (22, 25):
                    r, s = (tiles(t + 4 * (k == 25), 4, slice(0, 32)) for t in (TMQ, SQ))
                    dv.wait_ge(*DV.at(l, ("cossin", k == 25)))
                    step(dv.tensor_tensor(r, r, s, ALU.add), "rope")
                if k == 27:
                    dv.wait_ge(*PE.at(l, "scores"))
                    pr = flat(tiles(PR, 6))
                    p0 = pr[:, 0:512].rearrange("p (h k) -> p h k", h=4)
                    step(dv.tensor_tensor(p0, b3(5, 4), over(c_("causal", 128), 4), ALU.add))
                    for b in range(2):
                        p1 = pr[:, 512 + 512 * b:1024 + 512 * b].rearrange("p (h k) -> p h k", h=2)
                        s1 = bank[3 + b][:, :].rearrange("p (h k) -> p h k", h=2)
                        step(dv.tensor_copy(p1[:, :, 0:P], s1[:, :, 0:P]))
                        step(dv.tensor_tensor(p1[:, :, P:T], s1[:, :, P:T], over(c_("causal", 128), 2), ALU.add), "masked")
                if k == 28:
                    pr = flat(tiles(PR, 6))
                    p0 = pr[:, 0:512].rearrange("p (h k) -> p h k", h=4)
                    dv.wait_ge(*DV.at(l, "masked"))
                    step(dv.tensor_reduce(sm["mx"][:, 0:4], p0, AX, ALU.max))
                    step(dv.tensor_reduce(sm["mx"][:, 4:8], pr[:, 512:1536].rearrange("p (h k) -> p h k", h=4), AX, ALU.max))
                    settle(l)
                    step(dv.tensor_scalar(sm["mx"], sm["mx"], -(HD ** -0.5), None, ALU.mult), "rowmax")
                if k == 29:
                    dv.wait_ge(*AC.at(l, "exp"))
                    step(dv.reciprocal(sm["rs"], sm["rs"]))
                    settle(l)
                    pr = flat(tiles(PR, 6))
                    p0 = pr[:, 0:512].rearrange("p (h k) -> p h k", h=4)
                    p1 = pr[:, 512:1536].rearrange("p (h k) -> p h k", h=4)
                    step(dv.tensor_tensor(p0, p0, each(sm["rs"][:, 0:4], P), ALU.mult))
                    step(dv.tensor_tensor(p1, p1, each(sm["rs"][:, 4:8], T), ALU.mult), "probs")
                if k == 34:
                    dv.wait_ge(*AC.at(l, "mbhi"))
                    for i in range(2):
                        step(dv.tensor_tensor(flat(blo[:, 4 + 2 * i:6 + 2 * i, :]), bank[3 + i][:, :],
                                              flat(bhi[:, 4 + 2 * i:6 + 2 * i, :]), ALU.subtract), "mb_out")
                if 37 <= k <= 45:
                    n, part = divmod(k - 34, 3)
                    if part == 1 and n:
                        m = n // 2
                        pa = (lower, upper)[n % 2]
                        dv.wait_ge(*PE.at(l, ("KS", n)))
                        for h in range(HEADS):
                            g = 2 * h + m
                            step(dv.scalar_tensor_tensor(out=Wb[pa, h, :], in0=b3(6, 4)[pa, h, :], scalar=sm["sneg"][pa, g:g + 1],
                                                         in1=Vb[pa, g, :], op0=ALU.mult, op1=ALU.add), ("w", n))
                    if part == 0:
                        dv.wait_ge(*PE.at(l, ("SU", n - 1)))
                        if n == 1:
                            step(dv.tensor_copy(Sst(1), b3(2, 4)), ("state", 1))
                        else:
                            for h in range(HEADS):
                                step(dv.scalar_tensor_tensor(out=Sst(n % 2)[:, h, :], in0=Sst((n - 1) % 2)[:, h, :],
                                                             scalar=sm["egl"][:, NCH * h + n - 1:NCH * h + n],
                                                             in1=b3(2, 4)[:, h, :], op0=ALU.mult, op1=ALU.add), ("state", n))
                if k in (31, 32):
                    i = k - 31
                    dv.wait_ge(*AC.at(l, ("xtap", i)))
                    conv(l, [proj[:, TLX + t, :] for t in (2 * i, 2 * i + 1)], [proj[:, XC + t, :] for t in (2 * i, 2 * i + 1)],
                         [OFF["conv"] + TAPS * (12 + t) for t in (2 * i, 2 * i + 1)], "xc")
                if k == 36:
                    dv.wait_ge(*AC.at(l, "tanh_i"))
                    step(dv.scalar_tensor_tensor(out=tiles(TI, 4), in0=tiles(TI, 4), scalar=1.0, in1=tiles(XC, 4),
                                                 op0=ALU.add, op1=ALU.mult))
                if k == 39:
                    dv.wait_ge(*AC.at(l, "a0"))
                    settle(l)
                    step(dv.scalar_tensor_tensor(out=tiles(HSM, 4), in0=tiles(A0, 4), scalar=1.0,
                                                 in1=tiles(TR, 4), op0=ALU.add, op1=ALU.mult), "lru_m")
                    settle(l)
                    step(dv.tensor_scalar(tiles(A0, 4), tiles(HSM, 4), -1.0, 1.0, ALU.mult, ALU.add))
                if k == 41:
                    dv.wait_ge(*AC.at(l, "sqT"))
                    settle(l)
                    step(dv.scalar_tensor_tensor(out=tiles(HSM, 4), in0=tiles(A0, 4), scalar=1.0, in1=tiles(TR, 4),
                                                 op0=ALU.add, op1=ALU.mult))
                    settle(l)
                    step(dv.tensor_tensor(tiles(HSM, 4), tiles(HSM, 4), tiles(TI, 4), ALU.mult), "lru_uv")
                if k == 42:
                    dv.wait_ge(*DV.at(l, "lru_uv"))
                    for t in range(4):
                        step(dv.tensor_tensor_scan(proj[:, HS + t, :], proj[:, A0 + t, :], proj[:, HSM + t, :], 0.0, ALU.mult, ALU.add))
                if k == 44:
                    dv.wait_ge(*AC.at(l, "y2"))
                    step(dv.tensor_scalar(tiles(TI, 4), tiles(TI, 4), 0.044715, 1.0, ALU.mult, ALU.add))
                    settle(l)
                    step(dv.tensor_tensor(tiles(TI, 4), tiles(TI, 4), tiles(TLY, 4), ALU.mult), "gelu_in")
                if k == 46:
                    dv.wait_ge(*AC.at(l, "gelu_t"))
                    step(dv.scalar_tensor_tensor(out=tiles(TI, 4), in0=tiles(TI, 4), scalar=1.0, in1=tiles(TLY, 4),
                                                 op0=ALU.add, op1=ALU.mult))
                    settle(l)
                    step(dv.tensor_tensor(tiles(TI, 4), tiles(TI, 4), tiles(HS, 4), ALU.mult), "lru_f")
                if k == 48:
                    dv.wait_ge(*AC.at(l, "lruhi"))
                    step(dv.scalar_tensor_tensor(out=blo[:, 8:12, :], in0=tiles(TI, 4), scalar=0.25, in1=bhi[:, 8:12, :].bitcast(F32),
                                                 op0=ALU.mult, op1=ALU.subtract), "lru_out")
                if k == 38:
                    dv.wait_ge(*AC.at(l, "tz"))
                    step(dv.scalar_tensor_tensor(out=tiles(TZ, 4), in0=tiles(TMV, 4), scalar=1.0, in1=tiles(TZ, 4),
                                                 op0=ALU.add, op1=ALU.mult), "zsilu")
                if k == 49:
                    dv.wait_ge(*PE.at(l, ("sumT", 48)))
                    rsqrt(l, bank[2][:, T:T + 16].rearrange("p (m t) -> p t m", m=2)[:, 0:4, :], sm["ro"], 8, 1.0 / HD, EPS, "ro")
                if k == 51:
                    dv.wait_ge(*PE.at(l, "robc"))
                    for i in range(2):
                        step(dv.tensor_tensor(flat(tiles(TZ + 2 * i, 2)), flat(tiles(TZ + 2 * i, 2)), bank[6 + i][:, :], ALU.mult))
                    settle(l)
                    for i in range(2):
                        step(dv.scalar_tensor_tensor(out=flat(tiles(TMQ + 2 * i, 2)), in0=flat(tiles(TZ + 2 * i, 2)), scalar=sm["nwh"],
                                                     in1=bank[3 + i][:, :], op0=ALU.mult, op1=ALU.mult), "dn_f")
                if k == 52:
                    dv.wait_ge(*AC.at(l, "dnhi"))
                    step(dv.tensor_tensor(blo[:, 0:4, :], tiles(TMQ, 4), bhi[:, 0:4, :], ALU.subtract), "dn_out")
                c = k // 2 - 1 - C_IN
                if k % 2 == 0 and 0 <= c < C_Y:
                    hf, br = divmod(c, 3)
                    dv.wait_ge(*PE.at(l, ("bulk", k - 1)))
                    if c == 0:
                        dv.wait_ge(*AC.at(l, ("gates", 29)))
                    for i in range(2):
                        f = 4 * hf + 2 * i
                        g, mx = flat(tiles(TG + 8 * br + f, 2)), flat(tiles(MIX + f, 2))
                        dst = mx if br == 0 else g
                        step(dv.scalar_tensor_tensor(out=dst, in0=g, scalar=1.0, in1=bank[y_bank(c) + i][:, :],
                                                     op0=ALU.add, op1=ALU.mult), ("y", c))
                    if br:
                        settle(l)
                        for i in range(2):
                            f = 4 * hf + 2 * i
                            g, mx = flat(tiles(TG + 8 * br + f, 2)), flat(tiles(MIX + f, 2))
                            step(dv.tensor_tensor(mx, mx, g, ALU.add), ("mixf", 2 * hf + i))
                    if br == 2:
                        for i in range(2):
                            q = 2 * hf + i
                            dv.wait_ge(*AC.at(l, ("mixhi", q)))
                            step(dv.scalar_tensor_tensor(out=alo[:, 2 * q:2 * q + 2, :], in0=tiles(MIX + 2 * q, 2), scalar=0.5,
                                                         in1=ahi[:, 2 * q:2 * q + 2, :].bitcast(F32), op0=ALU.mult, op1=ALU.subtract),
                                 ("mixed", q))
                if k == 2 * FFN0:
                    x_update(l, "ffn", 2 * FFN0 - 1, l * 2 + 1)
                    add_squares(l, "ffn", ("ffn", "acc"))
                if k > 2 * FFN0 and k % 2 == 0:
                    kind, j = ffn_of(k // 2 - 1)
                    s = 8 * (j % 2)
                    if kind != "down":
                        dv.wait_ge(*PE.at(l, ("bulk", k - 1)))
                    for i in (0,) if (kind, j) == ("up", 0) else (j,) if kind == "gate" and j else ():
                        if i == 0:
                            settle(l)
                        step(dv.tensor_tensor(tiles(8 * (i % 2), 2), gate_bank(i)[:, :].rearrange("p (a b) -> p a b", a=2),
                                              over(rstd[:, :], 2), ALU.mult), ("gate", i))
                    if kind == "up":
                        step(dv.tensor_tensor(tiles(s + 4, 2), bank[1][:, :].rearrange("p (a b) -> p a b", a=2),
                                              over(rstd[:, :], 2), ALU.mult), ("up", j))
                        dv.wait_ge(*AC.at(l, ("ftanh", j)))
                        step(dv.scalar_tensor_tensor(out=tiles(s + 2, 2), in0=tiles(s + 2, 2), scalar=1.0, in1=tiles(s, 2),
                                                     op0=ALU.add, op1=ALU.mult))
                        settle(l)
                        step(dv.tensor_tensor(tiles(s + 6, 2), tiles(s + 2, 2), tiles(s + 4, 2), ALU.mult), ("hidf", j))
                        dv.wait_ge(*AC.at(l, ("hidhi", j)))
                        step(dv.scalar_tensor_tensor(out=blo[:, 2 * (j % 2):2 * (j % 2) + 2, :], in0=tiles(s + 6, 2), scalar=0.5,
                                                     in1=bhi[:, 2 * (j % 2):2 * (j % 2) + 2, :].bitcast(F32),
                                                     op0=ALU.mult, op1=ALU.subtract), ("hidden", j))

            HSM = UU

            for p in range(4):
                x_norm(None, "mix", 0, p)
            for m in range(AHEAD):
                lo(None, m)
            DV.first = dict(DV.new)
            dv.wait_ge(DV.sem, DV.n)
            dv.nop().then_inc(DV.sem, max(DV.per, 1))
            DV.n += max(DV.per, 1)
            DV.open_layer()
            with dv.Fori(0, L) as l:
                for k in range(NH):
                    if k in (3, 2 * FFN0 + 3):
                        rnorm(l, "mix" if k == 3 else "ffn")
                    if k in (4, 2 * FFN0 + 4):
                        rstd_copy(l, "mix" if k == 4 else "ffn")
                    evacuate(l, k)
                    side(l, k)
                    if k == 2 * FFN0 - 1:
                        continue
                    if k == 2 * FFN0:
                        lo(l, k - 1 + AHEAD)
                    if k + AHEAD < NH:
                        lo(l, k + AHEAD)
                    else:
                        lo(l, k + AHEAD - NH, True)
                x_update(l, "mix", NH - 1, l * 2 + 2)
            DV.n_end = DV.n
            dv.wait_ge(*AC.at(L, ("mix", "sq", 1), prev=True))
            step(dv.tensor_tensor(tmq[:, :], flat(tiles(SQ, 2)), flat(tiles(SQ + 2, 2)), ALU.add))
            for p in (2, 3):
                dv.wait_ge(*AC.at(L, ("mix", "sq", p), prev=True))
                settle(L - 1)
                step(dv.tensor_tensor(tmq[:, :], tmq[:, :], flat(tiles(SQ + 2 * p, 2)), ALU.add), "last_acc")
            dv.wait_ge(PE.sem, PE_FINAL)
            rsqrt(L - 1, bank[2][:, 0:2], sm["nr"], 2, 1.0 / D, EPS, "last_nr")
            dv.wait_ge(PE.sem, PE_FINAL + 1)
            for kt in range(KT):
                step(dv.scalar_tensor_tensor(out=x[:, kt, :], in0=x[:, kt, :], scalar=nrm[:, 2 * L * KT + kt:2 * L * KT + kt + 1],
                                             in1=bank[2][:, 0:T], op0=ALU.mult, op1=ALU.mult), ("out", kt // 4))
            DV.n = DV.n_end
        return {s.name: s.learnt() for s in signals}


def _columns(w):
    return np.concatenate([w[:, :, 0:1536], w[:, :, 2056:4616], w[:, :, 1536:2048], w[:, :, 4616:]], axis=2)


def _constants():
    con = np.zeros((P, NCON), np.float32)

    def put(name, a):
        con[:a.shape[0], CON[name]:CON[name] + a.shape[1]] = a

    put("ident", np.eye(P, dtype=np.float32))
    q = np.arange(P)
    put("causal", np.where(q[None, :] <= q[:, None], 0.0, -1e30).astype(np.float32))
    put("ones", np.ones((P, P), np.float32))
    e = np.zeros((P, 8, 8), np.float32)
    for i in range(8):
        e[:, i, i] = 1.0
    put("ecol", e.reshape(P, 64))
    half = HD // 8
    inv = (np.float32(500000.0) ** (-np.arange(half, dtype=np.float32) / np.float32(half))).astype(np.float32)
    ang = (np.arange(T, dtype=np.float32)[None, :] * inv[:, None]).astype(np.float32)
    cos, sin = np.cos(ang).astype(np.float32), np.sin(ang).astype(np.float32)
    put("cos", np.concatenate([cos, cos], 0))
    put("sin", np.concatenate([-sin, sin], 0))
    put("tri", ((q[:, None] <= q[None, :]) & (q[:, None] // CHUNK == q[None, :] // CHUNK)).astype(np.float32))
    i = np.arange(P)[:, None] % CHUNK
    j = np.arange(CHUNK)[None, :]
    put("eye", (i == j).astype(np.float32))
    put("upin", (j >= i).astype(np.float32))
    put("low", (j < i).astype(np.float32))

    def level(r, c, s):
        return ((r // (2 * s) == c // (2 * s)) & (r % (2 * s) >= s) & (c % (2 * s) < s)).astype(np.float32)

    put("low1", level(i, j, 1))
    for s in (1, 2, 4, 8, 16, 32):
        put(f"up{s}", level(j, i, s))
    return con


def kernel(x, norm_mix, w_in, b_gate, dn_conv, dn_a_log, dn_dt_bias, dn_norm, dn_out, mb_out,
           lru_conv_w, lru_conv_b, lru_w_r, lru_b_r, lru_w_i, lru_b_i, lru_lambda, lru_out,
           w_o, norm_ffn, ffn_in, ffn_down, norm_final):
    import concourse.bacc as bacc
    from concourse.bass_utils import run_bass_kernel_spmd

    A = np.asarray
    win = A(w_in)
    stream = np.zeros((L * CH + 3, P, 2 * HALF), np.float32)
    wi = _columns(win).reshape(L, KT, P, C_IN, 256).transpose(0, 3, 2, 1, 4).reshape(L, C_IN, P, 2 * HALF)
    ys = np.stack([A(dn_out), A(mb_out), A(lru_out)], 1).reshape(L, 3, 4, P, 2, 512)
    ys = ys.transpose(0, 4, 1, 3, 2, 5).reshape(L, C_Y, P, 2 * HALF)
    wo = A(w_o).reshape(L, C_WO, 2, P, D).transpose(0, 1, 3, 2, 4).reshape(L, C_WO, P, 2 * HALF)
    fi = A(ffn_in).reshape(L, KT, P, 2, PAIRS, 256).transpose(0, 3, 4, 2, 1, 5).reshape(L, 2, PAIRS, P, 2 * HALF)
    fd = A(ffn_down).reshape(L, PAIRS, 2, P, D).transpose(0, 1, 3, 2, 4).reshape(L, PAIRS, P, 2 * HALF)
    for l in range(L):
        s = stream[l * CH:(l + 1) * CH]
        s[0:C_IN] = wi[l]
        s[C_IN:C_IN + C_Y] = ys[l]
        s[C_IN + C_Y:FFN0] = wo[l]
        s[FFN0], s[FFN0 + 1] = fi[l, 0, 0], fi[l, 1, 0]
        for j in range(1, PAIRS):
            s[FFN0 + 3 * j - 1], s[FFN0 + 3 * j], s[FFN0 + 3 * j + 1] = fi[l, 0, j], fi[l, 1, j], fd[l, j - 1]
        s[CH - 1] = fd[l, PAIRS - 1]

    par = np.zeros((L, P, NPAR), np.float32)

    def put(name, a):
        par[:, :a.shape[1], OFF[name]:OFF[name] + a.shape[2]] = a

    def tiled(a, n):
        return A(a).reshape(L, n, P).transpose(0, 2, 1)

    put("wab", win[:, :, 2048:2056].reshape(L, KT, P, 8).transpose(0, 2, 1, 3).reshape(L, P, 64))
    cw = np.concatenate([A(dn_conv), A(lru_conv_w)], 2).reshape(L, TAPS, 16, P)
    put("conv", cw.transpose(0, 3, 2, 1).reshape(L, P, 64))
    put("convb", tiled(lru_conv_b, 4))
    put("br", tiled(lru_b_r, 4))
    put("bi", tiled(lru_b_i, 4))
    put("lam", tiled(lru_lambda, 4))
    put("dnorm", A(dn_norm).reshape(L, P, 1))
    put("bg", tiled(b_gate, 24))
    put("alog", np.broadcast_to(A(dn_a_log).reshape(L, 1, 4), (L, P, 4)))
    put("dtb", np.broadcast_to(A(dn_dt_bias).reshape(L, 1, 4), (L, P, 4)))
    for name, w in (("wr", A(lru_w_r)), ("wi", A(lru_w_i))):
        w = w.reshape(L, 4, 2, 64, 64)
        for t in range(4):
            for g in range(2):
                par[:, 64 * g:64 * g + 64, OFF[name] + P * t + 64 * g:OFF[name] + P * t + 64 * g + 64] = w[:, t, g]
    nm, nf = tiled(norm_mix, KT), tiled(norm_ffn, KT)
    nl = A(norm_final).reshape(KT, P).T
    norms = np.concatenate([w[l] for l in range(L) for w in (nm, nf)] + [nl], 1)
    xT = A(x).reshape(T, KT, P).transpose(2, 1, 0)

    arrays = {"stream_dram": stream, "params_dram": par, "consts_dram": _constants(),
              "norms_dram": np.ascontiguousarray(norms), "x_dram": np.ascontiguousarray(xT)}
    known = {}
    for _ in range(3):
        nc = bacc.Bacc("TRN2", target_bir_lowering=False, num_devices=1)
        args = [nc.dram_tensor(n, a.shape, mybir.dt.from_np(a.dtype), kind="ExternalInput").ap() for n, a in arrays.items()]
        o = nc.dram_tensor("out_dram", (P, KT, T), F32, kind="ExternalOutput").ap()
        known = build(nc, *args, o, known)
    r = run_bass_kernel_spmd(nc, [arrays], core_ids=[0])
    y = np.asarray(r.results[0]["out_dram"])
    return np.ascontiguousarray(y.transpose(2, 1, 0)).reshape(1, T, D)
```
